# Optimizing a Trainium2 kernel written in Bass

```python
import math
import jax, jax.numpy as jnp
from jax import lax
import numpy as np

D_MODEL = 1024
BATCH = 1
SEQ = 256
DEPTH = 2

GRID_W = 64
CTX_LEN = 256
N_EVEN = (DEPTH + 1) // 2
N_ODD = DEPTH // 2
MIX_WIDTH = D_MODEL
DA_HEADS = 4
DA_DK = 64
DA_DV = 2 * DA_DK
MLA_HEADS = 4
MLA_NOPE = 128
MLA_ROPE = 64
MLA_V = 128
MLA_Q_LORA = 256
MLA_KV_LORA = 128
EV_IN = 3 * DA_HEADS * 2 * DA_DK + MLA_Q_LORA + MLA_KV_LORA + MLA_ROPE
NA_HEADS = 16
NA_DH = 64
NA_KH = 8
NA_KW = 16
D_FF = -(-8 * D_MODEL // (3 * 256)) * 256
ROPE_THETA = 10000.0
Q_BLOCK = 128
EPS = 1e-6
NEG_INF = -1e30


def rms_norm(x, g):
    xf = x.astype(jnp.float32)
    y = xf * lax.rsqrt(jnp.mean(xf * xf, axis=-1, keepdims=True) + EPS)
    return (y * g.astype(jnp.float32)).astype(x.dtype)

def softmax_f32(s):
    return jax.nn.softmax(s.astype(jnp.float32), axis=-1)

def adaln(cond, mod_w, mod_b):
    return jnp.split(jax.nn.silu(cond) @ mod_w + mod_b, 6, axis=-1)

def modulate(h, shift, scale):
    return h * (1 + scale) + shift

def swiglu(h, w_in, w_out):
    g, u = jnp.split(h @ w_in, 2, axis=-1)
    return (jax.nn.silu(g) * u) @ w_out

def axial_rope_tables(S, dim):
    t = jnp.arange(S)
    row = (t // GRID_W).astype(jnp.float32)
    col = (t % GRID_W).astype(jnp.float32)
    half = dim // 2
    inv = ROPE_THETA ** (-jnp.arange(0, half, 2, dtype=jnp.float32) / half)
    ar = row[:, None] * inv
    ac = col[:, None] * inv
    return (jnp.cos(ar), jnp.sin(ar), jnp.cos(ac), jnp.sin(ac))

def _rotate(x, cos, sin):
    x1, x2 = jnp.split(x, 2, axis=-1)
    return jnp.concatenate([x1 * cos - x2 * sin, x1 * sin + x2 * cos], axis=-1)

def apply_axial_rope(x, tables):
    cr, sr, cc, sc = tables
    xr, xc = jnp.split(x, 2, axis=-1)
    return jnp.concatenate([_rotate(xr, cr, sr), _rotate(xc, cc, sc)], axis=-1).astype(x.dtype)

def sweep_query_blocks(fn, *qs):
    S = qs[0].shape[-2]
    nb = S // Q_BLOCK
    blocks = tuple(jnp.moveaxis(q.reshape(q.shape[:-2] + (nb, Q_BLOCK, q.shape[-1])), -3, 0) for q in qs)
    out = lax.map(lambda a: fn(*a), blocks)
    out = jnp.moveaxis(out, 0, -3)
    return out.reshape(out.shape[:-3] + (S, out.shape[-1]))

def merge_heads(*outs):
    return jnp.concatenate([o.transpose(0, 2, 1, 3).reshape(o.shape[0], o.shape[2], -1) for o in outs], axis=-1)

def even_project(h, w_in, da_q_g, da_k_g, mla_q_a_g, mla_w_uq, mla_kv_a_g, mla_w_ukv, mla_q_g, mla_k_g, mla_kr_g):
    B, T, _ = h.shape
    n_dq = DA_HEADS * 2 * DA_DK
    idx = [n_dq, 2 * n_dq, 3 * n_dq, 3 * n_dq + MLA_Q_LORA, 3 * n_dq + MLA_Q_LORA + MLA_KV_LORA]
    dq, dk, dv, cq, ckv, kr = jnp.split(h @ w_in, idx, axis=-1)
    dq = rms_norm(dq.reshape(B, T, DA_HEADS, 2, DA_DK), da_q_g).transpose(0, 2, 3, 1, 4)
    dk = rms_norm(dk.reshape(B, T, DA_HEADS, 2, DA_DK), da_k_g).transpose(0, 2, 3, 1, 4)
    dv = dv.reshape(B, T, DA_HEADS, DA_DV).transpose(0, 2, 1, 3)
    q = (rms_norm(cq, mla_q_a_g) @ mla_w_uq).reshape(B, T, MLA_HEADS, MLA_NOPE + MLA_ROPE)
    q = rms_norm(q, mla_q_g).transpose(0, 2, 1, 3)
    qn, qr = q[..., :MLA_NOPE], q[..., MLA_NOPE:]
    kv = (rms_norm(ckv, mla_kv_a_g) @ mla_w_ukv).reshape(B, T, MLA_HEADS, MLA_NOPE + MLA_V)
    kn = rms_norm(kv[..., :MLA_NOPE], mla_k_g).transpose(0, 2, 1, 3)
    mv = kv[..., MLA_NOPE:].transpose(0, 2, 1, 3)
    kr = rms_norm(kr, mla_kr_g)
    return dq, dk, dv, qn, qr, kn, kr, mv

def diff_attend(q, k, v, lam, lam_init, out_g):
    s = jnp.einsum('bhiqd,bhikd->bhiqk', q, k) * (DA_DK ** -0.5)
    p = softmax_f32(s)
    a = p[:, :, 0] - lam * p[:, :, 1]
    o = jnp.einsum('bhqk,bhkd->bhqd', a.astype(v.dtype), v)
    return rms_norm(o, out_g) * (1.0 - lam_init)

def mla_attend(qn, qr, kn, kr, v):
    s = (jnp.einsum('bhqd,bhkd->bhqk', qn, kn) + jnp.einsum('bhqd,bkd->bhqk', qr, kr)) * ((MLA_NOPE + MLA_ROPE) ** -0.5)
    p = softmax_f32(s)
    return jnp.einsum('bhqk,bhkd->bhqd', p.astype(v.dtype), v)

def even_mixer(hx, hc, need_ctx, w_in, da_q_g, da_k_g, lam, lam_init, da_out_g,
               mla_q_a_g, mla_w_uq, mla_kv_a_g, mla_w_ukv, mla_q_g, mla_k_g, mla_kr_g):
    proj = lambda h: even_project(h, w_in, da_q_g, da_k_g, mla_q_a_g, mla_w_uq, mla_kv_a_g, mla_w_ukv,
                                  mla_q_g, mla_k_g, mla_kr_g)
    dq_x, dk_x, dv_x, qn_x, qr_x, kn_x, kr_x, mv_x = proj(hx)
    dq_c, dk_c, dv_c, qn_c, qr_c, kn_c, kr_c, mv_c = proj(hc)
    S = hx.shape[1]
    tab_da = axial_rope_tables(S, DA_DK)
    tab_mla = axial_rope_tables(S, MLA_ROPE)
    dq_x = apply_axial_rope(dq_x, tab_da)
    dk_x = apply_axial_rope(dk_x, tab_da)
    qr_x = apply_axial_rope(qr_x, tab_mla)
    kr_x = apply_axial_rope(kr_x, tab_mla)
    dk_all = jnp.concatenate([dk_c, dk_x], axis=-2)
    dv_all = jnp.concatenate([dv_c, dv_x], axis=-2)
    kn_all = jnp.concatenate([kn_c, kn_x], axis=-2)
    kr_all = jnp.concatenate([kr_c, kr_x], axis=-2)
    mv_all = jnp.concatenate([mv_c, mv_x], axis=-2)
    da_x = sweep_query_blocks(lambda q: diff_attend(q, dk_all, dv_all, lam, lam_init, da_out_g), dq_x)
    mla_x = sweep_query_blocks(lambda a, b: mla_attend(a, b, kn_all, kr_all, mv_all), qn_x, qr_x)
    y_x = merge_heads(da_x, mla_x)
    y_c = None
    if need_ctx:
        da_c = diff_attend(dq_c, dk_c, dv_c, lam, lam_init, da_out_g)
        mla_c = mla_attend(qn_c, qr_c, kn_c, kr_c, mv_c)
        y_c = merge_heads(da_c, mla_c)
    return y_x, y_c

def odd_project(h, w_in, q_g, k_g):
    B, T, _ = h.shape
    q, k, v = jnp.split((h @ w_in).reshape(B, T, 3 * NA_HEADS, NA_DH), 3, axis=2)
    q = rms_norm(q, q_g).transpose(0, 2, 1, 3)
    k = rms_norm(k, k_g).transpose(0, 2, 1, 3)
    return q, k, v.transpose(0, 2, 1, 3)

def dense_attend(q, k, v):
    p = softmax_f32(jnp.einsum('bhqd,bhkd->bhqk', q, k) * (NA_DH ** -0.5))
    return jnp.einsum('bhqk,bhkd->bhqd', p.astype(v.dtype), v)

def na_latent(q, k, v, kc, vc, rpb):
    B, H, S, d = q.shape
    rows = S // GRID_W
    kh = min(NA_KH, rows)
    kg = k.reshape(B, H, rows, GRID_W, d)
    vg = v.reshape(B, H, rows, GRID_W, d)
    qg = q.reshape(B, H, rows, GRID_W, d)
    cols = jnp.arange(GRID_W)
    col_start = jnp.clip(cols - NA_KW // 2, 0, GRID_W - NA_KW)
    col_valid = (cols[None, :] >= col_start[:, None]) & (cols[None, :] < col_start[:, None] + NA_KW)
    dc_idx = jnp.clip(cols[None, :] - cols[:, None], -(NA_KW - 1), NA_KW - 1) + NA_KW - 1
    rpb_c = rpb[:, :, dc_idx]
    scale = NA_DH ** -0.5

    def row_step(args):
        r, q_row = args
        rs = jnp.clip(r - kh // 2, 0, rows - kh)
        kb = lax.dynamic_slice_in_dim(kg, rs, kh, axis=2)
        vb = lax.dynamic_slice_in_dim(vg, rs, kh, axis=2)
        dr_idx = rs + jnp.arange(kh) - r + NA_KH - 1
        bias = jnp.take(rpb_c, dr_idx, axis=1).transpose(0, 2, 1, 3)
        s_loc = jnp.einsum('bhqd,bhiwd->bhqiw', q_row, kb).astype(jnp.float32) * scale + bias
        s_loc = jnp.where(col_valid[:, None, :], s_loc, NEG_INF).reshape(B, H, GRID_W, kh * GRID_W)
        s_ctx = jnp.einsum('bhqd,bhkd->bhqk', q_row, kc).astype(jnp.float32) * scale
        p = softmax_f32(jnp.concatenate([s_loc, s_ctx], axis=-1))
        p_loc = p[..., :kh * GRID_W].reshape(B, H, GRID_W, kh, GRID_W).astype(v.dtype)
        p_ctx = p[..., kh * GRID_W:].astype(v.dtype)
        return jnp.einsum('bhqiw,bhiwd->bhqd', p_loc, vb) + jnp.einsum('bhqk,bhkd->bhqd', p_ctx, vc)

    out = lax.map(row_step, (jnp.arange(rows), jnp.moveaxis(qg, 2, 0)))
    return jnp.moveaxis(out, 0, 2).reshape(B, H, S, d)

def odd_mixer(hx, hc, need_ctx, w_in, q_g, k_g, rpb):
    q_x, k_x, v_x = odd_project(hx, w_in, q_g, k_g)
    q_c, k_c, v_c = odd_project(hc, w_in, q_g, k_g)
    y_x = merge_heads(na_latent(q_x, k_x, v_x, k_c, v_c, rpb))
    y_c = merge_heads(dense_attend(q_c, k_c, v_c)) if need_ctx else None
    return y_x, y_c

def first_inputs(seed: int = 0) -> dict:
    key = jax.random.key(seed)
    ks = iter(jax.random.split(key, 40))
    nrm = lambda shape, s: jax.random.normal(next(ks), shape, jnp.float32) * s
    gain = lambda shape: 1.0 + 0.1 * jax.random.normal(next(ks), shape, jnp.float32)
    D = D_MODEL
    return {
        "x": nrm((BATCH, SEQ, D), 1.0),
        "c": nrm((BATCH, D), 1.0),
        "ctx": nrm((BATCH, CTX_LEN, D), 1.0),
        "c_ctx": nrm((D,), 1.0),
        "mod_w": nrm((DEPTH, D, 6 * D), 0.5 * D ** -0.5),
        "mod_b": nrm((DEPTH, 6 * D), 0.02),
        "norm_mix_g": gain((DEPTH, D)),
        "norm_ffn_g": gain((DEPTH, D)),
        "w_out": nrm((DEPTH, MIX_WIDTH, D), MIX_WIDTH ** -0.5),
        "ffn_w_in": nrm((DEPTH, D, 2 * D_FF), D ** -0.5),
        "ffn_w_out": nrm((DEPTH, D_FF, D), D_FF ** -0.5),
        "ev_w_in": nrm((N_EVEN, D, EV_IN), D ** -0.5),
        "da_q_g": gain((N_EVEN, DA_DK)),
        "da_k_g": gain((N_EVEN, DA_DK)),
        "da_lq1": nrm((N_EVEN, DA_DK), 0.1),
        "da_lk1": nrm((N_EVEN, DA_DK), 0.1),
        "da_lq2": nrm((N_EVEN, DA_DK), 0.1),
        "da_lk2": nrm((N_EVEN, DA_DK), 0.1),
        "da_out_g": gain((N_EVEN, DA_DV)),
        "mla_q_a_g": gain((N_EVEN, MLA_Q_LORA)),
        "mla_w_uq": nrm((N_EVEN, MLA_Q_LORA, MLA_HEADS * (MLA_NOPE + MLA_ROPE)), MLA_Q_LORA ** -0.5),
        "mla_kv_a_g": gain((N_EVEN, MLA_KV_LORA)),
        "mla_w_ukv": nrm((N_EVEN, MLA_KV_LORA, MLA_HEADS * (MLA_NOPE + MLA_V)), MLA_KV_LORA ** -0.5),
        "mla_q_g": gain((N_EVEN, MLA_NOPE + MLA_ROPE)),
        "mla_k_g": gain((N_EVEN, MLA_NOPE)),
        "mla_kr_g": gain((N_EVEN, MLA_ROPE)),
        "od_w_in": nrm((N_ODD, D, 3 * NA_HEADS * NA_DH), D ** -0.5),
        "na_q_g": gain((N_ODD, NA_DH)),
        "na_k_g": gain((N_ODD, NA_DH)),
        "na_rpb": nrm((N_ODD, NA_HEADS, 2 * NA_KH - 1, 2 * NA_KW - 1), 0.5),
    }

def first_block(x, c, ctx, c_ctx, mod_w, mod_b, norm_mix_g, norm_ffn_g, w_out, ffn_w_in, ffn_w_out,
              ev_w_in, da_q_g, da_k_g, da_lq1, da_lk1, da_lq2, da_lk2, da_out_g,
              mla_q_a_g, mla_w_uq, mla_kv_a_g, mla_w_ukv, mla_q_g, mla_k_g, mla_kr_g,
              od_w_in, na_q_g, na_k_g, na_rpb):
    for l in range(DEPTH):
        need_ctx = l < DEPTH - 1
        sh_a, sc_a, g_a, sh_f, sc_f, g_f = [m[:, None, :] for m in adaln(c, mod_w[l], mod_b[l])]
        csh_a, csc_a, cg_a, csh_f, csc_f, cg_f = adaln(c_ctx, mod_w[l], mod_b[l])
        hx = modulate(rms_norm(x, norm_mix_g[l]), sh_a, sc_a)
        hc = modulate(rms_norm(ctx, norm_mix_g[l]), csh_a, csc_a)
        e = l // 2
        if l % 2 == 0:
            lam_init = 0.8 - 0.6 * math.exp(-0.3 * l)
            lam = (jnp.exp(jnp.sum(da_lq1[e] * da_lk1[e]).astype(jnp.float32))
                   - jnp.exp(jnp.sum(da_lq2[e] * da_lk2[e]).astype(jnp.float32)) + lam_init)
            y_x, y_c = even_mixer(hx, hc, need_ctx, ev_w_in[e], da_q_g[e], da_k_g[e], lam, lam_init, da_out_g[e],
                                  mla_q_a_g[e], mla_w_uq[e], mla_kv_a_g[e], mla_w_ukv[e],
                                  mla_q_g[e], mla_k_g[e], mla_kr_g[e])
        else:
            y_x, y_c = odd_mixer(hx, hc, need_ctx, od_w_in[e], na_q_g[e], na_k_g[e], na_rpb[e])
        x = x + g_a * (y_x @ w_out[l])
        x = x + g_f * swiglu(modulate(rms_norm(x, norm_ffn_g[l]), sh_f, sc_f), ffn_w_in[l], ffn_w_out[l])
        if need_ctx:
            ctx = ctx + cg_a * (y_c @ w_out[l])
            ctx = ctx + cg_f * swiglu(modulate(rms_norm(ctx, norm_ffn_g[l]), csh_f, csc_f), ffn_w_in[l], ffn_w_out[l])
    return x


CHUNK = 64
PE_DIM = 256
M_HEADS = 4
M_DK = 256
M_DV = 256
M_QK = M_HEADS * M_DK
M_V = M_HEADS * M_DV
CONV_K = 4
R_HEADS = 4
R_DK = 256
R_DV = 512
R_QK = R_HEADS * R_DK
R_V = R_HEADS * R_DV
ROPE_BASE = 10000.0
D_FF_2 = 4 * D_MODEL
IN_SIZES = (M_QK, M_QK, M_V, M_V, M_HEADS, M_HEADS, R_QK, R_QK, R_V, R_V, D_MODEL, D_MODEL)
N_IN = M_QK * 2 + M_V * 2 + M_HEADS * 2 + R_QK * 2 + R_V * 2 + D_MODEL * 2
F_GATE_OFFSET = M_QK * 2 + M_V * 2 + M_HEADS


def split_cols(z):
    outs = []
    off = 0
    for s in IN_SIZES:
        outs.append(z[..., off:off + s])
        off += s
    return outs

def rmsnorm(x, g):
    xf = x.astype(jnp.float32)
    y = xf * lax.rsqrt(jnp.mean(xf * xf, axis=-1, keepdims=True) + EPS)
    return (y * g.astype(jnp.float32)).astype(x.dtype)

def head_layernorm(y, g, n_heads):
    B, S, W = y.shape
    yf = y.astype(jnp.float32).reshape(B, S, n_heads, W // n_heads)
    mu = jnp.mean(yf, axis=-1, keepdims=True)
    var = jnp.mean(jnp.square(yf - mu), axis=-1, keepdims=True)
    yn = ((yf - mu) * lax.rsqrt(var + EPS)).reshape(B, S, W)
    return yn * g.astype(jnp.float32)

def causal_conv(u, w, b):
    S = u.shape[1]
    up = jnp.pad(u, ((0, 0), (CONV_K - 1, 0), (0, 0)))
    out = b
    for j in range(CONV_K):
        out = out + up[:, j:j + S, :] * w[j]
    return out

def rope(x, cos, sin):
    half = x.shape[-1] // 2
    x1, x2 = x[..., :half], x[..., half:]
    return jnp.concatenate([x1 * cos - x2 * sin, x1 * sin + x2 * cos], axis=-1)

def to_chunks(x, n_heads):
    B, S, W = x.shape
    return x.reshape(B, S // CHUNK, CHUNK, n_heads, W // n_heads).transpose(1, 0, 3, 2, 4)

def gates_to_chunks(g):
    B, S, H = g.shape
    return g.reshape(B, S // CHUNK, CHUNK, H).transpose(1, 0, 3, 2)

def from_chunks(y):
    NC, B, H, L, d = y.shape
    return y.transpose(1, 0, 3, 2, 4).reshape(B, NC * L, H * d)

def mlstm_chunkwise(q, k, v, li, lf):
    NC, B, H, L, dk = q.shape
    dv = v.shape[-1]
    causal = jnp.tril(jnp.ones((L, L), dtype=bool))

    def step(carry, inp):
        C, n, m = carry
        qc, kc, vc, lic, lfc = inp
        b = jnp.cumsum(lfc, axis=-1)
        log_intra = b[..., :, None] - b[..., None, :] + lic[..., None, :]
        log_intra = jnp.where(causal, log_intra, -jnp.inf)
        log_inter = b + m[..., None]
        m_t = jnp.maximum(log_inter, jnp.max(log_intra, axis=-1))
        d_intra = jnp.exp(log_intra - m_t[..., None])
        d_inter = jnp.exp(log_inter - m_t)
        s = jnp.einsum('bhtd,bhsd->bhts', qc, kc) * d_intra
        num = jnp.einsum('bhts,bhsv->bhtv', s, vc) + d_inter[..., None] * jnp.einsum('bhtd,bhdv->bhtv', qc, C)
        den = jnp.sum(s, axis=-1) + d_inter * jnp.einsum('bhtd,bhd->bht', qc, n)
        h = num / jnp.maximum(jnp.abs(den), jnp.exp(-m_t))[..., None]
        b_end = b[..., -1]
        log_w = b_end[..., None] - b + lic
        m_new = jnp.maximum(b_end + m, jnp.max(log_w, axis=-1))
        w = jnp.exp(log_w - m_new[..., None])
        decay = jnp.exp(b_end + m - m_new)
        C = decay[..., None, None] * C + jnp.einsum('bhsd,bhsv->bhdv', kc * w[..., None], vc)
        n = decay[..., None] * n + jnp.einsum('bhs,bhsd->bhd', w, kc)
        return (C, n, m_new), h

    init = (jnp.zeros((B, H, dk, dv), jnp.float32), jnp.zeros((B, H, dk), jnp.float32),
            jnp.zeros((B, H), jnp.float32))
    _, hs = lax.scan(step, init, (q, k, v, li, lf))
    return hs

def retention_chunkwise(q, k, v, log_gamma):
    NC, B, H, L, dk = q.shape
    dv = v.shape[-1]
    pos = jnp.arange(L, dtype=jnp.float32)
    diff = pos[:, None] - pos[None, :]
    lg = log_gamma[:, None, None]
    intra = jnp.where(diff >= 0, jnp.exp(jnp.maximum(diff, 0.0) * lg), 0.0)
    inter = jnp.exp((pos + 1.0) * log_gamma[:, None])
    kdec = jnp.exp((L - 1.0 - pos) * log_gamma[:, None])
    cdec = jnp.exp(L * log_gamma)

    def step(R, inp):
        qc, kc, vc = inp
        s = jnp.einsum('bhtd,bhsd->bhts', qc, kc) * intra
        y = jnp.einsum('bhts,bhsv->bhtv', s, vc) + jnp.einsum('bhtd,bhdv->bhtv', qc, R) * inter[..., None]
        R = cdec[:, None, None] * R + jnp.einsum('bhsd,bhsv->bhdv', kc * kdec[..., None], vc)
        return R, y

    _, ys = lax.scan(step, jnp.zeros((B, H, dk, dv), jnp.float32), (q, k, v))
    return ys

def second_inputs(seed: int = 0) -> dict:
    key = jax.random.key(seed)
    ks = jax.random.split(key, 24)
    f32 = jnp.float32

    def nrm(k, shape, scale):
        return jax.random.normal(k, shape, f32) * scale

    def gain(k, shape):
        return 1.0 + 0.05 * jax.random.normal(k, shape, f32)

    b_in = nrm(ks[4], (DEPTH, N_IN), 0.02)
    f_bias = jnp.linspace(3.0, 6.0, M_HEADS, dtype=f32)[None, :] + nrm(ks[5], (DEPTH, M_HEADS), 0.1)
    b_in = b_in.at[:, F_GATE_OFFSET:F_GATE_OFFSET + M_HEADS].set(f_bias)
    return {
        "x": nrm(ks[0], (BATCH, SEQ, D_MODEL), 1.0),
        "p": nrm(ks[1], (DEPTH, BATCH, SEQ, PE_DIM), 1.0),
        "norm1_g": gain(ks[2], (DEPTH, D_MODEL)),
        "w_in": nrm(ks[3], (DEPTH, D_MODEL, N_IN), D_MODEL ** -0.5),
        "b_in": b_in,
        "conv_w": nrm(ks[6], (DEPTH, CONV_K, 2 * M_QK), CONV_K ** -0.5),
        "conv_b": nrm(ks[7], (DEPTH, 2 * M_QK), 0.02),
        "m_norm_g": gain(ks[8], (DEPTH, M_V)),
        "r_norm_g": gain(ks[9], (DEPTH, R_V)),
        "w_bm": nrm(ks[10], (DEPTH, M_V, D_MODEL), M_V ** -0.5),
        "w_br": nrm(ks[11], (DEPTH, R_V, D_MODEL), R_V ** -0.5),
        "w_out": nrm(ks[12], (DEPTH, D_MODEL, D_MODEL), D_MODEL ** -0.5),
        "norm2_g": gain(ks[13], (DEPTH, D_MODEL)),
        "w_ff1": nrm(ks[14], (DEPTH, D_MODEL, D_FF_2), D_MODEL ** -0.5),
        "b_ff1": nrm(ks[15], (DEPTH, D_FF_2), 0.02),
        "w_ff2": nrm(ks[16], (DEPTH, D_FF_2, D_MODEL), D_FF_2 ** -0.5),
        "b_ff2": nrm(ks[17], (DEPTH, D_MODEL), 0.02),
        "norm3_g": gain(ks[18], (DEPTH, D_MODEL)),
        "w_pe_gate": nrm(ks[19], (DEPTH, D_MODEL, D_MODEL), D_MODEL ** -0.5),
        "w_pe": nrm(ks[20], (DEPTH, PE_DIM, D_MODEL), PE_DIM ** -0.5),
        "final_g": gain(ks[21], (D_MODEL,)),
    }

def second_block(x, p, norm1_g, w_in, b_in, conv_w, conv_b, m_norm_g, r_norm_g, w_bm, w_br,
              w_out, norm2_g, w_ff1, b_ff1, w_ff2, b_ff2, norm3_g, w_pe_gate, w_pe, final_g):
    B, S, _ = x.shape
    dt = x.dtype
    f32 = jnp.float32
    pos = jnp.arange(S, dtype=f32)
    inv_freq = ROPE_BASE ** (-jnp.arange(0, R_DK, 2, dtype=f32) / R_DK)
    ang = pos[:, None] * inv_freq[None, :]
    cos = jnp.cos(ang)[:, None, :]
    sin = jnp.sin(ang)[:, None, :]
    log_gamma = jnp.log(1.0 - jnp.exp2(-5.0 - jnp.arange(R_HEADS, dtype=f32)))

    for i in range(DEPTH):
        h = rmsnorm(x, norm1_g[i])
        z = h @ w_in[i] + b_in[i]
        _, _, mv, mo, mi, mf, rq, rk, rv, rg, gm, gr = split_cols(z)
        qk = jax.nn.silu(causal_conv(z[..., :2 * M_QK], conv_w[i], conv_b[i]))
        mq = qk[..., :M_QK] * (M_DK ** -0.5)
        mk = qk[..., M_QK:]

        hm = mlstm_chunkwise(
            to_chunks(mq.astype(f32), M_HEADS), to_chunks(mk.astype(f32), M_HEADS),
            to_chunks(mv.astype(f32), M_HEADS),
            gates_to_chunks(mi.astype(f32)), gates_to_chunks(jax.nn.log_sigmoid(mf.astype(f32))))
        hm = from_chunks(hm)
        y_m = (jax.nn.sigmoid(mo.astype(f32)) * head_layernorm(hm, m_norm_g[i], M_HEADS)).astype(dt)

        rq4 = rope(rq.astype(f32).reshape(B, S, R_HEADS, R_DK), cos, sin)
        rk4 = rope(rk.astype(f32).reshape(B, S, R_HEADS, R_DK), cos, sin) * (R_DK ** -0.5)
        hr = retention_chunkwise(
            to_chunks(rq4.reshape(B, S, R_QK), R_HEADS), to_chunks(rk4.reshape(B, S, R_QK), R_HEADS),
            to_chunks(rv.astype(f32), R_HEADS), log_gamma)
        hr = from_chunks(hr)
        y_r = (jax.nn.silu(rg.astype(f32)) * head_layernorm(hr, r_norm_g[i], R_HEADS)).astype(dt)

        merged = jax.nn.sigmoid(gm) * (y_m @ w_bm[i]) + jax.nn.sigmoid(gr) * (y_r @ w_br[i])
        x = x + merged @ w_out[i]

        h2 = rmsnorm(x, norm2_g[i])
        x = x + jnp.square(jax.nn.relu(h2 @ w_ff1[i] + b_ff1[i])) @ w_ff2[i] + b_ff2[i]

        h3 = rmsnorm(x, norm3_g[i])
        x = x + jax.nn.sigmoid(h3 @ w_pe_gate[i]) * (p[i] @ w_pe[i])

    return rmsnorm(x, final_g)


def setup_inputs(seed=0):
    out = dict(first_inputs(seed))
    for name, value in second_inputs(seed + 1).items():
        if name != "x":
            out[name + "_2"] = value
    return out


def reference(
    x, c, ctx, c_ctx, mod_w, mod_b, norm_mix_g, norm_ffn_g, w_out, ffn_w_in, ffn_w_out, ev_w_in,
    da_q_g, da_k_g, da_lq1, da_lk1, da_lq2, da_lk2, da_out_g, mla_q_a_g, mla_w_uq, mla_kv_a_g,
    mla_w_ukv, mla_q_g, mla_k_g, mla_kr_g, od_w_in, na_q_g, na_k_g, na_rpb, p_2, norm1_g_2,
    w_in_2, b_in_2, conv_w_2, conv_b_2, m_norm_g_2, r_norm_g_2, w_bm_2, w_br_2, w_out_2,
    norm2_g_2, w_ff1_2, b_ff1_2, w_ff2_2, b_ff2_2, norm3_g_2, w_pe_gate_2, w_pe_2, final_g_2,
):
    x = first_block(
        x, c, ctx, c_ctx, mod_w, mod_b, norm_mix_g, norm_ffn_g, w_out, ffn_w_in, ffn_w_out,
        ev_w_in, da_q_g, da_k_g, da_lq1, da_lk1, da_lq2, da_lk2, da_out_g, mla_q_a_g, mla_w_uq,
        mla_kv_a_g, mla_w_ukv, mla_q_g, mla_k_g, mla_kr_g, od_w_in, na_q_g, na_k_g, na_rpb,
    )
    return second_block(
        x, p_2, norm1_g_2, w_in_2, b_in_2, conv_w_2, conv_b_2, m_norm_g_2, r_norm_g_2, w_bm_2,
        w_br_2, w_out_2, norm2_g_2, w_ff1_2, b_ff1_2, w_ff2_2, b_ff2_2, norm3_g_2, w_pe_gate_2,
        w_pe_2, final_g_2,
    )


_drawn_inputs = setup_inputs


def setup_inputs(seed=0):
    import zlib

    import numpy as np

    out = dict(_drawn_inputs(seed))
    spreads = {}
    factors = {'da_q_g': 5.784,
     'da_k_g': 5.042,
     'da_lq1': 200.0,
     'da_lk1': 3.212,
     'da_lq2': 3.305,
     'mla_q_a_g': 8.0,
     'mla_kv_a_g': 5.48,
     'mla_q_g': 8.0,
     'mla_k_g': 8.0,
     'mla_kr_g': 8.0,
     'na_q_g': 8.0,
     'na_k_g': 8.0,
     'na_rpb': 5.832,
     'conv_b_2': 8.0,
     'm_norm_g_2': 3.234,
     'r_norm_g_2': 3.182,
     'b_ff2_2': 3.392,
     'norm3_g_2': 21.02,
     'b_ff1_2': 3.148}
    for name, (base, spread) in spreads.items():
        noise = np.random.default_rng([zlib.crc32(name.encode()), seed]).standard_normal(out[name].shape)
        drawn = base * np.exp(spread * noise) if base else spread * noise
        out[name] = __import__('jax').numpy.asarray(drawn.astype(out[name].dtype))
    for name, factor in factors.items():
        out[name] = (out[name] * factor).astype(out[name].dtype)
    return out
```

```python
from contextlib import ExitStack

import numpy as np

import concourse.bass as bass
from concourse import mybir

ALU = mybir.AluOpType
ACT = mybir.ActivationFunctionType
F32 = mybir.dt.float32
AX_X = mybir.AxisListType.X

P = 128
D = 1024
KD = D // P
SEQ = 256
TX = SEQ // P
GRID_W = 64
DA_H, DA_DK, DA_DV = 4, 64, 128
ML_H, ML_NOPE, ML_ROPE, ML_V = 4, 128, 64, 128
ML_QL, ML_KVL = 256, 128
ML_QK = ML_NOPE + ML_ROPE
EV_IN = 3 * DA_H * 2 * DA_DK + ML_QL + ML_KVL + ML_ROPE
NA_H, NA_DH, NA_KH, NA_KW = 16, 64, 8, 16
NA_ROWS = SEQ // GRID_W
D_FF = 2816
KF = D_FF // P
EPS = 1e-6
LAM_INIT = 0.2
R_H = 4
QK_SCALE = 1.0 / 16.0
NEG = -1e30

NC_ = 512
KC = 4
CHUNK = KC * NC_
RING = 4
REL_W = 2 * GRID_W - 1

COLS = [("cond", 2 * KD), ("mix_g", 2 * KD), ("ffn_g", 2 * KD), ("n1", 2 * KD), ("n2", 2 * KD), ("n3", 2 * KD),
        ("b_mqk", 32), ("b_rqk", 32), ("conv_w", 128), ("conv_b", 32), ("b_ff1", 64)]
ROWS = [("da_q_g", 64), ("da_k_g", 64), ("lq", 128), ("lk", 128), ("da_out_g", 128), ("mla_q_a_g", 256),
        ("mla_kv_a_g", 128), ("mla_q_g", 192), ("mla_k_g", 128), ("mla_kr_g", 64), ("na_q_g", 64), ("na_k_g", 64)]
TABS = [("ident", 128), ("cos", 64), ("sin", 64), ("cosT", 256), ("sinT", 256), ("decay", 4 * 384), ("mask", 384),
        ("sel_x", 128), ("sel_c", 128), ("sel_h", 4 * 128), ("na_mask", GRID_W)]


def spans(items):
    at, out = 0, {}
    for name, n in items:
        out[name] = (at, at + n)
        at += n
    return out, at


def tables():
    s, n = spans(TABS)
    t = np.zeros((P, n), np.float32)

    def put(name, a):
        t[:a.shape[0], s[name][0]:s[name][1]] = a.reshape(a.shape[0], -1)

    put("ident", np.eye(P))
    tok = np.arange(SEQ)
    half = DA_DK // 2
    inv = (np.float32(10000.0) ** (-np.arange(0, half, 2, dtype=np.float32) / np.float32(half))).astype(np.float32)
    ang = np.stack([(tok // GRID_W).astype(np.float32)[:, None] * inv,
                    (tok % GRID_W).astype(np.float32)[:, None] * inv], 1).astype(np.float32)
    by_tile = ang.reshape(TX, P, 2, half // 2).transpose(1, 0, 2, 3)
    put("cos", np.cos(by_tile))
    put("sin", np.sin(by_tile))
    inv2 = (np.float32(10000.0) ** (-np.arange(0, 256, 2, dtype=np.float32) / np.float32(256))).astype(np.float32)
    ang2 = (inv2[:, None] * tok.astype(np.float32)[None, :]).astype(np.float32)
    put("cosT", np.cos(ang2))
    put("sinT", np.sin(ang2))
    p = np.arange(P)
    s_of = np.concatenate([np.zeros(256), np.full(128, 128)])[None, :] + p[:, None]
    t_of = np.concatenate([np.arange(256), np.arange(128, 256)])[None, :] + 0 * p[:, None]
    lg = np.log(1.0 - np.exp2(-5.0 - np.arange(R_H)))
    put("decay", np.stack([np.where(t_of >= s_of, np.exp((t_of - s_of) * g), 0.0) for g in lg], 1))
    put("mask", np.where(t_of >= s_of, 0.0, NEG))
    put("sel_x", np.stack([np.ones(P), np.zeros(P)]))
    put("sel_c", np.stack([np.zeros(P), np.ones(P)]))
    put("sel_h", np.repeat(np.eye(R_H)[:, :, None], P, 2))
    qc, kc = (p % GRID_W)[:, None], np.arange(GRID_W)[None, :]
    start = np.clip(qc - NA_KW // 2, 0, GRID_W - NA_KW)
    put("na_mask", np.where((kc >= start) & (kc < start + NA_KW), 0.0, NEG))
    return t


class Event:

    def __init__(self, sem, name, plan):
        self.sem, self.name, self.plan, self.count = sem, name, plan, 0

    def now(self, *step, by=1):
        self.count += by
        self.plan[(self.name, step)] = self.count
        return self.sem, by

    def after(self, *step):
        return self.sem, self.plan.get((self.name, step), 1)

    def alias(self, *step):
        self.plan[(self.name, step)] = self.count


def attention_units(v):
    phases = {}
    da, mla, na = [], [], []
    for h in range(DA_H):
        for t in range(4):
            k0, nk = (0, 512) if t < TX else (256, 256)
            da.append(dict(scores=[[(v["dqT"][64 * i:64 * i + 64, h, t * P:(t + 1) * P],
                                     v["dkT"][64 * i:64 * i + 64, h, k0:k0 + nk])] for i in range(2)],
                           nk=nk, scale=DA_DK ** -0.5, bias=None, dv=DA_DV,
                           value=[v["z"][:, (k0 // P) + j, 1024 + h * 128:1024 + (h + 1) * 128] for j in range(nk // P)],
                           out=v["y4"][:, t, h * 128:(h + 1) * 128]))
    for h in range(ML_H):
        for t in range(4):
            k0, nk = (0, 512) if t < TX else (256, 256)
            q = slice(t * P, (t + 1) * P)
            mla.append(dict(scores=[[(v["qnT"][:, h, q], v["knT"][:, h, k0:k0 + nk]),
                                     (v["qrT"][0:64, h, q], v["krT"][0:64, k0:k0 + nk])]],
                            nk=nk, scale=ML_QK ** -0.5, bias=None, dv=ML_V,
                            value=[v["kv"][:, (k0 // P) + j, h * 256 + 128:h * 256 + 256] for j in range(nk // P)],
                            out=v["y4"][:, t, 512 + h * 128:512 + (h + 1) * 128]))
    for h in range(NA_H):
        for t in range(TX):
            part = slice(64 * (h % 2), 64 * (h % 2) + 64)
            na.append(dict(scores=[[(v["nqT"][part, h // 2, t * P:(t + 1) * P], v["nkT"][part, h // 2, :])]],
                           nk=512, scale=NA_DH ** -0.5, bias=v["rel"][:, t, h, :], dv=NA_DH,
                           value=[v["nv"][:, j, h * 64:(h + 1) * 64] for j in range(4)],
                           out=v["y4"][:, t, h * 64:(h + 1) * 64]))
    phases["da"], phases["mla"], phases["na"] = da, mla, na
    return phases


def build_program(nc, plan, ins, out):
    x_d, ctx_d, chunks_d, cols_d, rows_d, tabs_d, modb_d, rel_d, brows_d, bgate_d, wgate_d, nrows_d, pT_d = ins
    ctx = ExitStack()
    with ctx:
        def sb(name, shape):
            return ctx.enter_context(nc.sbuf_tensor(name, shape, F32))

        def ev(name):
            return Event(ctx.enter_context(nc.semaphore(name)), name, plan)

        cs, ncols = spans(COLS)
        rs, nrows = spans(ROWS)
        ts, ntabs = spans(TABS)
        ring = sb("ring", [P, RING, CHUNK])
        X = sb("X", [P, 4, D])
        hT_ = sb("hT", [P, 4096])
        xn_ = sb("xn", [P, 4096])
        G = sb("G", [P, 4096])
        BIG = sb("BIG", [P, 20480])
        SCR = sb("SCR", [P, 2048])
        colt = sb("colt", [P, ncols])
        ROWS_ = sb("ROWS_", [P, 2048])
        rowt = ROWS_[:, 0:nrows]
        gt = ROWS_[0:4, :].rearrange("p (a t) -> p a t", a=8)
        tabt = sb("tabt", [P, ntabs])
        wgate = sb("wgate", [P, 2, KD, 8])
        bgate = sb("bgate", [4, 2, 2])
        pT = sb("pT", [P, 512])
        bias_ring = sb("bias_ring", [P, 2, NC_])
        stat = sb("stat", [P, 256])
        modc = sb("modc", [P, 48, 2])
        small = sb("small", [P, 64])
        PS = ctx.enter_context(nc.psum_tensor("PS", [P, 8, 512], F32))

        def col(name):
            return colt[:, cs[name][0]:cs[name][1]]

        def row(name):
            return rowt[:, rs[name][0]:rs[name][1]]

        def tab(name, parts=P):
            return tabt[0:parts, ts[name][0]:ts[name][1]]

        ident = tab("ident")
        hT = {4: hT_[:, :].rearrange("p (k t) -> p k t", k=KD), 2: hT_[:, 0:2048].rearrange("p (k t) -> p k t", k=KD)}
        xn = xn_[:, :].rearrange("p (t d) -> p t d", t=4)
        big = lambda a, n: BIG[:, a:a + n]
        z0 = big(0, 4 * EV_IN).rearrange("p (t c) -> p t c", t=4)
        v = {"z": z0, "y4": xn}
        v["dqT"] = big(7936, 2048).rearrange("p (h t) -> p h t", h=4)
        v["dkT"] = big(9984, 2048).rearrange("p (h t) -> p h t", h=4)
        v["qnT"], v["knT"] = v["dqT"], v["dkT"]
        v["qrT"] = big(12032, 2048).rearrange("p (h t) -> p h t", h=4)
        v["krT"] = big(14080, 512)
        cT = big(12032, 1536).rearrange("p (b t) -> p b t", b=3)
        q_l0 = z0[:, :, 0:768]
        v["kv"] = z0[:, :, 768:1792]
        prob4 = big(14592, 2048).rearrange("p (b i k) -> p b i k", b=2, i=2)
        mix4 = big(16640, 1024).rearrange("p (b k) -> p b k", b=2)
        probT4 = big(17664, 1024).rearrange("p (b k) -> p b k", b=2)
        nq = big(0, 2048).rearrange("p (t c) -> p t c", t=2)
        nk_ = big(2048, 4096).rearrange("p (t c) -> p t c", t=4)
        v["nv"] = big(6144, 4096).rearrange("p (t c) -> p t c", t=4)
        v["nqT"] = big(10240, 2048).rearrange("p (h t) -> p h t", h=8)
        v["nkT"] = hT_[:, :].rearrange("p (h t) -> p h t", h=8)
        v["rel"] = big(12288, 8192).rearrange("p (t h k) -> p t h k", t=2, h=NA_H)
        prob_na = X[:, 2, :].rearrange("p (b i k) -> p b i k", b=2, i=1)
        probT_na = X[:, 3, :].rearrange("p (b k) -> p b k", b=2)
        mod_bias = BIG[0:2, 14336:20480]
        mod_rows = BIG[0:2, 8192:14336]
        units = attention_units(v)
        mqkT = big(0, 4096).rearrange("p (c t) -> p c t", c=16)
        rqkT = big(4096, 4096).rearrange("p (c t) -> p c t", c=16)
        mv = big(8192, 2048).rearrange("p (t c) -> p t c", t=2)
        mo = big(10240, 2048).rearrange("p (t c) -> p t c", t=2)
        rv = big(12288, 4096).rearrange("p (t c) -> p t c", t=2)
        rg = big(16384, 4096).rearrange("p (t c) -> p t c", t=2)
        gm, gr = X[:, 2:4, :], xn[:, 2:4, :]
        hm = xn[:, 0:2, :]
        hr = big(0, 4096).rearrange("p (t c) -> p t c", t=2)
        ymT = big(4096, 2048).rearrange("p (c t) -> p c t", c=8)
        mergedT = big(6144, 2048).rearrange("p (c t) -> p c t", c=8)
        yrT = hT_[:, :].rearrange("p (c t) -> p c t", c=16)
        merged = mo
        ffT = {l: big(0, KF * n).rearrange("p (c t) -> p c t", c=KF) for l, n in ((0, 512), (1, 256))}
        ff2T = big(8192, 8192).rearrange("p (c t) -> p c t", c=32)

        tab_in, x_in, rel_in, wgate_in = ev("tab_in"), ev("x_in"), ev("rel_in"), ev("wgate_in")
        modb_in, nrows_in, pT_in = [ev("modb_in0"), ev("modb_in1")], ev("nrows_in"), ev("pT_in")
        w_in = [ev(f"w_in{i}") for i in range(RING)]
        bias_in = [ev(f"bias_in{i}") for i in range(2)]
        out_done = ev("out_done")
        vec_chain, act_chain = ev("vec_chain"), ev("act_chain")
        projected = ev("projected")
        stored = ev("stored")
        acted = ev("acted")
        turned = ev("turned")
        copied_v, copied_s = ev("copied_v"), ev("copied_s")
        x_ready, sums_ready, root_ready, normed = ev("x_ready"), ev("sums_ready"), ev("root_ready"), ev("normed")
        cond_ready, mod_row, mod_turned, mod_ready = ev("cond_ready"), ev("mod_row"), ev("mod_turned"), ev("mod_ready")
        gates_bc = ev("gates_bc")
        lam_logit, lam_exp = ev("lam_logit"), ev("lam_exp")
        const_ready = ev("const_ready")
        pre_turn = ev("pre_turn")
        scored, max_ready, exp_ready, probs_ready = ev("scored"), ev("max_ready"), ev("exp_ready"), ev("probs_ready")
        probs_turned, probsT_ready, attended, y_out = ev("probs_turned"), ev("probsT_ready"), ev("attended"), ev("y_out")
        y_ready = ev("y_ready")
        unit_acted, qk_ready, qk_ready_act = ev("unit_acted"), ev("qk_ready"), ev("qk_ready_act")
        ff_acted = ev("ff_acted")
        gate_abs, gate_act, gate_scan, gate_turned, gate_cols = (ev("gate_abs"), ev("gate_act"), ev("gate_scan"),
                                                                ev("gate_turned"), ev("gate_cols"))
        u_bc, exp_arg = ev("u_bc"), ev("exp_arg")
        tok_acted = ev("tok_acted")
        hidden = ev("hidden")

        def gate_list(l):
            who = ("sel_x", "sel_c") if l == 0 else ("sel_x",)
            return [(kind, w, half) for kind in (2, 5) for w in who for half in range(2)]

        def gate(l, kind, who):
            n = gate_list(l).index((kind, "sel_c" if who else "sel_x", 0))
            return G[:, n * 512:n * 512 + 1024]

        def copy_plan():
            plan_ = {}

            def add(key, nb, tiles, dst, width=P, affine=None):
                plan_[key] = (nb, tiles, width, dst, affine)
            for l, tiles in ((0, 4), (1, 4)):
                add(("mix", l), 8, tiles, lambda b: hT[4][:, b, :], affine=("mod", 0))
            add(("ffn", 0), 8, 4, lambda b: hT[4][:, b, :], affine=("mod", 3))
            add(("ffn", 1), 8, 2, lambda b: hT[2][:, b, :], affine=("mod", 3))
            add("daq", 4, 4, lambda b: v["dqT"][:, b, :])
            add("dak", 4, 4, lambda b: v["dkT"][:, b, :])
            add("mlac", 3, 4, lambda b: cT[:, b, :])
            add("mlakr", 1, 4, lambda b: v["krT"][0:64, :], 64)
            add("qn", 4, 4, lambda b: v["qnT"][:, b, :])
            add("qr", 4, 4, lambda b: v["qrT"][0:64, b, :], 64)
            add("kn", 4, 4, lambda b: v["knT"][:, b, :])
            add("y0", 8, 4, lambda b: hT[4][:, b, :])
            add("naq", 8, 2, lambda b: v["nqT"][:, b, :])
            add("nak", 8, 4, lambda b: v["nkT"][:, b, :])
            add("y1", 8, 2, lambda b: hT[2][:, b, :])
            for l in range(2):
                for k in ("n1", "n2", "n3"):
                    add((k, l), 8, 2, lambda b: hT[2][:, b, :], affine=("gain", k, l))
                add(("ym", l), 8, 2, lambda b: ymT[:, b, :])
                add(("yr", l), 16, 2, lambda b: yrT[:, b, :])
                add(("mg", l), 8, 2, lambda b: mergedT[:, b, :])
            return plan_

        copies = copy_plan()

        def copy_parts(key, b):
            nb, tiles, width, dst, affine = copies[key]
            src = PS[0:width, 4 + b % 4, 0:tiles * P]
            if affine is None:
                return [(dst(b), src, None, None)]
            if affine[0] == "gain":
                g = col(affine[1])[:, affine[2] * 8 + b:affine[2] * 8 + b + 1]
                return [(dst(b), src, g, None)]
            k = affine[1]
            return [(dst(b)[:, i * 256:(i + 1) * 256], src[:, i * 256:(i + 1) * 256], modc[:, (k + 1) * 8 + b, i:i + 1],
                     modc[:, k * 8 + b, i:i + 1]) for i in range(tiles // 2)]

        eps, ones, neg_lam = small[:, 61:62], small[:, 60:61], small[:, 62:63]

        block = ctx.enter_context(nc.Block())
        n_chunks = chunks_d.shape[0]

        @block.sync
        def _(sp):
            sp.dma_start(colt[:, :], cols_d).then_inc(*tab_in.now(by=16))
            sp.dma_start(tabt[:, :], tabs_d).then_inc(*tab_in.now(by=16))
            sp.dma_start(rowt, rows_d.partition_broadcast(P)).then_inc(*tab_in.now(by=16))
            sp.dma_start(mod_bias, modb_d[0].partition_broadcast(2)).then_inc(*modb_in[0].now(0, by=16))
            for c in range(n_chunks):
                if c == 4:
                    sp.dma_start(X[:, 0:2, :], x_d).then_inc(*x_in.now(by=16))
                    sp.dma_start(X[:, 2:4, :], ctx_d).then_inc(*x_in.now(by=16))
                    sp.dma_start(wgate[:, :, :, :], wgate_d).then_inc(*wgate_in.now(by=16))
                    sp.dma_start(bgate[:, :, :], bgate_d).then_inc(*wgate_in.now(by=16))
                if c >= RING:
                    sp.wait_ge(*projected.after("used", c - RING))
                sp.dma_start(ring[:, c % RING, :], chunks_d[c]).then_inc(*w_in[c % RING].now(c, by=16))
            sp.wait_ge(wgate_in.sem, wgate_in.count)
            sp.wait_ge(*x_ready.after("out"))
            sp.dma_start(out, xn[:, 0:2, :]).then_inc(*out_done.now(by=16))
            sp.wait_ge(out_done.sem, out_done.count)

        @block.gpsimd
        def _(pool):
            pool.wait_ge(*projected.after("ffn_out", 0, 1, 1))
            pool.dma_start(mod_bias, modb_d[1].partition_broadcast(2)).then_inc(*modb_in[1].now(1, by=16))
            pool.wait_ge(*gates_bc.after(1, 3))
            for t in range(TX):
                for half in range(2):
                    r = 2 * t + half
                    first = NA_KH - 1 - r
                    src = rel_d[:, :, first:first + NA_ROWS, :].rearrange("q h i c -> q h (i c)")
                    pool.dma_start(v["rel"][64 * half:64 * half + 64, t], src).then_inc(*rel_in.now(by=16))
            n = 0
            for l in range(2):
                pool.wait_ge(*(x_ready.after("ffn_out", 1) if l == 0 else projected.after("w_pe", 0, 1, 0)))
                pool.dma_start(G[:, 0:3072] if l else G[:, :],
                               nrows_d[l:l + 1, 0:3072].partition_broadcast(P)
                               if l else nrows_d[0:1, :].partition_broadcast(P)).then_inc(*nrows_in.now(l, by=16))
                pool.dma_start(pT[:, :], pT_d[:, l, :]).then_inc(*pT_in.now(l, by=16))
                for b in range(18):
                    if n >= 2:
                        pool.wait_ge(*stored.after("bias", n - 2))
                    pool.dma_start(bias_ring[:, n % 2, :], brows_d[n:n + 1, :].partition_broadcast(P)
                                   ).then_inc(*bias_in[n % 2].now(n, by=16))
                    n += 1

        @block.tensor
        def _(pe):
            reader = {}
            state = {"c": 0}

            def claim(*banks):
                for b in banks:
                    if b in reader:
                        pe.wait_ge(*reader.pop(b))

            def take_chunk():
                c = state["c"]
                state["c"] += 1
                pe.wait_ge(*w_in[c % RING].after(c))
                return c, ring[:, c % RING, :].rearrange("p (k n) -> p k n", k=KC)

            def project_tok(st, l, n, k_tiles, lhs, groups=1, freed=stored, n0=0):
                for j in range(n0, n0 + n):
                    for kg in range(-(-k_tiles // KC)):
                        c, w = take_chunk()
                        for g in range(groups):
                            pair = (j * groups + g) % 2
                            if kg == 0:
                                claim(2 * pair, 2 * pair + 1)
                            for t in range(2):
                                for kt in range(KC * kg, min(KC * kg + KC, k_tiles)):
                                    mm = pe.matmul(PS[:, 2 * pair + t, :], lhs(kt, 2 * g + t), w[:, kt - KC * kg, :],
                                                   start=kt == 0, stop=kt == k_tiles - 1)
                            if kg == (k_tiles - 1) // KC:
                                mm.then_inc(*projected.now(st, l, j, g))
                                reader[2 * pair] = reader[2 * pair + 1] = freed.after(st, l, j, g)
                            elif g == groups - 1:
                                mm.then_inc(*projected.now(("chunk", c)))
                        projected.alias("used", c)

            def project_feat(st, l, n, rhs, groups=1, freed=stored):
                for j in range(n):
                    for kg in range(2):
                        c, w = take_chunk()
                        for g in range(groups):
                            pair = (j * groups + g) % 2
                            if kg == 0:
                                claim(2 * pair, 2 * pair + 1)
                            for s in range(4):
                                for kt in range(KC * kg, KC * kg + KC):
                                    mm = pe.matmul(PS[:, 2 * pair + s // 2, (s % 2) * 256:(s % 2) * 256 + 256],
                                                   w[:, kt - KC * kg, s * P:(s + 1) * P], rhs[:, kt, g * 256:g * 256 + 256],
                                                   start=kt == 0 and s % 2 == 0, stop=kt == KD - 1,
                                                   skip_group_check=True)
                            if kg == 1:
                                mm.then_inc(*projected.now(st, l, j, g))
                                reader[2 * pair] = reader[2 * pair + 1] = freed.after(st, l, j, g)
                            elif g == groups - 1:
                                mm.then_inc(*projected.now(("chunk", c)))
                        projected.alias("used", c)

            def turn(key, nb, tiles, src, width=P, ready=None):
                for b in range(nb):
                    claim(4 + b % 4)
                    for t in range(tiles):
                        if ready and b == 0:
                            pe.wait_ge(*ready(t))
                        mm = pe.transpose(PS[0:width, 4 + b % 4, t * P:(t + 1) * P], src(b, t), ident)
                    mm.then_inc(*turned.now(key, b))
                    reader[4 + b % 4] = (copied_s if b % 2 else copied_v).after(key, b)

            def await_copies(key, nb):
                pe.wait_ge(*copied_v.after(key, (nb - 1) // 2 * 2))
                if nb > 1:
                    pe.wait_ge(*copied_s.after(key, nb // 2 * 2 - 1))

            def norm(key, tiles):
                turn(key, KD, tiles, lambda b, t: xn[:, t, b * P:(b + 1) * P], ready=lambda t: normed.after(key, t))
                await_copies(key, KD)

            def attend(ph, prob, probT):
                us = units[ph]

                def scores(u):
                    d = us[u]
                    s = 4 + 2 * (u % 2)
                    claim(s, s + 1)
                    for i, mats in enumerate(d["scores"]):
                        for m, (a, b) in enumerate(mats):
                            mm = pe.matmul(PS[:, s + i, 0:d["nk"]], a, b, start=m == 0, stop=m == len(mats) - 1)
                    mm.then_inc(*scored.now(ph, u))
                    reader[s] = reader[s + 1] = exp_ready.after(ph, u)

                def turn_probs(u):
                    pe.wait_ge(*probs_ready.after(ph, u))
                    claim(u % 2)
                    for j in range(us[u]["nk"] // P):
                        mm = pe.transpose(PS[:, u % 2, j * P:(j + 1) * P], prob(u)[:, j * P:(j + 1) * P], ident)
                    mm.then_inc(*probs_turned.now(ph, u))
                    reader[u % 2] = probsT_ready.after(ph, u)

                def values(u):
                    d = us[u]
                    pe.wait_ge(*probsT_ready.after(ph, u))
                    claim(2 + u % 2)
                    n = d["nk"] // P
                    for j in range(n):
                        mm = pe.matmul(PS[:, 2 + u % 2, 0:d["dv"]], probT[:, u % 2, j * P:(j + 1) * P], d["value"][j],
                                       start=j == 0, stop=j == n - 1)
                    mm.then_inc(*attended.now(ph, u))
                    reader[2 + u % 2] = y_out.after(ph, u)

                scores(0)
                for u in range(len(us)):
                    if u + 1 < len(us):
                        scores(u + 1)
                    if u >= 1:
                        values(u - 1)
                    turn_probs(u)
                values(len(us) - 1)

            def modulation(l):
                if l == 0:
                    pe.wait_ge(*cond_ready.after())
                cond = small[:, 0:16].rearrange("p (k c) -> p k c", c=2)
                for j in range(12):
                    for kg in range(2):
                        c, w = take_chunk()
                        if kg == 0:
                            claim(j % 2)
                        for kt in range(4 * kg, 4 * kg + 4):
                            mm = pe.matmul(PS[0:2, j % 2, :], cond[:, kt, :], w[:, kt - 4 * kg, :],
                                           start=kt == 0, stop=kt == 7)
                        if kg == 1:
                            mm.then_inc(*projected.now("mod", l, j, 0))
                            reader[j % 2] = mod_row.after(l, j)
                        else:
                            mm.then_inc(*projected.now(("chunk", c)))
                        projected.alias("used", c)
                pe.wait_ge(*mod_row.after(l, 11))
                claim(4)
                for k in range(48):
                    mm = pe.transpose(PS[:, 4, 2 * k:2 * k + 2], mod_rows[:, k * P:(k + 1) * P], ident[0:2, 0:2])
                mm.then_inc(*mod_turned.now(l))
                reader[4] = mod_ready.after(l)
                for n, (kind, who, half) in enumerate(gate_list(l)):
                    b = 5 + n % 3
                    claim(b)
                    pe.matmul(PS[:, b, :], tab(who, 2), mod_rows[:, kind * D + half * 512:kind * D + half * 512 + 512],
                              start=True, stop=True).then_inc(*gates_bc.now(l, n))
                    reader[b] = acted.after("gates", l, n)

            def even_attention():
                pe.wait_ge(*pre_turn.after("da"))
                turn("daq", 4, 4, lambda b, t: z0[:, t, b * P:(b + 1) * P])
                turn("dak", 4, 4, lambda b, t: z0[:, t, 512 + b * P:512 + (b + 1) * P])
                await_copies("daq", 4)
                await_copies("dak", 4)
                attend("da", lambda u: mix4[:, u % 2, :], probT4)
                pe.wait_ge(*pre_turn.after("mla_c"))
                turn("mlac", 3, 4, lambda b, t: z0[:, t, 1536 + b * P:1536 + (b + 1) * P])
                turn("mlakr", 1, 4, lambda b, t: z0[:, t, 1920:1984], width=64)
                await_copies("mlac", 3)
                await_copies("mlakr", 1)
                c, _ = take_chunk()
                w = ring[:, c % RING, 0:1536].rearrange("p (k n) -> p k n", k=2)
                for t in range(4):
                    pair = t % 2
                    claim(2 * pair, 2 * pair + 1)
                    for half in range(2):
                        lo, hi = half * 384, half * 384 + 384
                        for kt in range(2):
                            mm = pe.matmul(PS[:, 2 * pair + half, 0:384], cT[:, kt, t * P:(t + 1) * P], w[:, kt, lo:hi],
                                           start=kt == 0, stop=kt == 1)
                    mm.then_inc(*projected.now("uq", 0, t, 0))
                    reader[2 * pair] = reader[2 * pair + 1] = stored.after("uq", 0, t, 0)
                projected.alias("used", c)
                c, _ = take_chunk()
                for t in range(4):
                    pair = t % 2
                    claim(2 * pair, 2 * pair + 1)
                    for half in range(2):
                        mm = pe.matmul(PS[:, 2 * pair + half, :], cT[:, 2, t * P:(t + 1) * P],
                                       ring[:, c % RING, half * 512:half * 512 + 512], start=True, stop=True)
                    mm.then_inc(*projected.now("ukv", 0, t, 0))
                    reader[2 * pair] = reader[2 * pair + 1] = stored.after("ukv", 0, t, 0)
                projected.alias("used", c)
                pe.wait_ge(*pre_turn.after("mla_q"))
                turn("qn", 4, 4, lambda b, t: q_l0[:, t, b * 192:b * 192 + 128])
                turn("qr", 4, 4, lambda b, t: q_l0[:, t, b * 192 + 128:b * 192 + 192], width=64)
                turn("kn", 4, 4, lambda b, t: v["kv"][:, t, b * 256:b * 256 + 128])
                for k in ("qn", "qr", "kn"):
                    await_copies(k, 4)
                attend("mla", lambda u: prob4[:, u % 2, 0, :], probT4)

            def swiglu(l, tiles):
                g = tiles // 2
                norm(("ffn", l), tiles)
                project_feat("ffn_in", l, 11, hT[tiles], g)
                pe.wait_ge(*stored.after("ffn_in", l, 10, g - 1))
                project_tok("ffn_out", l, 2, KF, lambda kt, t: ffT[l][:, kt, t * P:(t + 1) * P], g)

            pe.wait_ge(tab_in.sem, 16 * 3)
            modulation(0)
            norm(("mix", 0), 4)
            project_tok("ev_in", 0, 4, KD, lambda kt, t: hT[4][:, kt, t * P:(t + 1) * P], 2)
            even_attention()
            turn("y0", KD, 4, lambda b, t: xn[:, t, b * P:(b + 1) * P], ready=lambda t: y_ready.after("ev", 0))
            await_copies("y0", KD)
            project_tok("w_out", 0, 2, KD, lambda kt, t: hT[4][:, kt, t * P:(t + 1) * P], 2)
            swiglu(0, 4)
            modulation(1)
            norm(("mix", 1), 4)
            project_tok("od_q", 1, 2, KD, lambda kt, t: hT[4][:, kt, t * P:(t + 1) * P], 1)
            project_tok("od_kv", 1, 4, KD, lambda kt, t: hT[4][:, kt, t * P:(t + 1) * P], 2)
            pe.wait_ge(*pre_turn.after("na"))
            turn("naq", 8, 2, lambda b, t: nq[:, t, b * P:(b + 1) * P])
            turn("nak", 8, 4, lambda b, t: nk_[:, t, b * P:(b + 1) * P])
            await_copies("naq", 8)
            await_copies("nak", 8)
            attend("na", lambda u: prob_na[:, u % 2, 0, :], probT_na)
            turn("y1", KD, 2, lambda b, t: xn[:, t, b * P:(b + 1) * P], ready=lambda t: y_out.after("na", 31))
            await_copies("y1", KD)
            project_tok("w_out", 1, 2, KD, lambda kt, t: hT[2][:, kt, t * P:(t + 1) * P])
            swiglu(1, 2)

            def pair_attention(l, kind, qkT, val, dv):
                for h in range(R_H):
                    b = 4 + h % 2
                    claim(b)
                    for s in range(2):
                        cols = slice(0, 256) if s == 0 else slice(256, 384)
                        for j in range(2):
                            mm = pe.matmul(PS[:, b, cols], qkT[:, 8 + 2 * h + j, s * P:(s + 1) * P],
                                           qkT[:, 2 * h + j, s * P:256], start=j == 0, stop=j == 1)
                    mm.then_inc(*scored.now(kind, l, h))
                    reader[b] = probs_ready.after(kind, l, h)
                    if kind == "m":
                        claim(6 + h % 2)
                        pe.matmul(PS[:, 6 + h % 2, 0:256], tab("sel_h", 4)[:, h * P:(h + 1) * P], gt[:, 3, :],
                                  start=True, stop=True).then_inc(*u_bc.now(l, h))
                        reader[6 + h % 2] = exp_arg.after(l, h)
                    if h >= 1:
                        values_pair(l, kind, h - 1, val, dv)
                values_pair(l, kind, R_H - 1, val, dv)

            def values_pair(l, kind, h, val, dv):
                pe.wait_ge(*probs_ready.after(kind, l, h))
                pb = SCR[:, 384 * (h % 2):384 * (h % 2) + 384]
                o = 2 * (h % 2)
                claim(o, o + 1)
                for t in range(2):
                    blocks = [pb[:, 0:128]] if t == 0 else [pb[:, 128:256], pb[:, 256:384]]
                    for s, lhs in enumerate(blocks):
                        mm = pe.matmul(PS[:, o + t, 0:dv], lhs, val[:, s, h * dv:(h + 1) * dv],
                                       start=s == 0, stop=s == len(blocks) - 1)
                    if kind == "m":
                        for s, lhs in enumerate(blocks):
                            mm = pe.matmul(PS[:, o + t, 256:257], lhs, small[:, 60:61],
                                           start=s == 0, stop=s == len(blocks) - 1)
                mm.then_inc(*attended.now(kind, l, h))
                reader[o] = reader[o + 1] = y_out.after(kind, l, h)

            for l in range(2):
                lhs = lambda kt, t: hT[2][:, kt, t * P:(t + 1) * P]
                norm(("n1", l), 2)
                if l == 0:
                    pe.wait_ge(wgate_in.sem, wgate_in.count)
                claim(4)
                for gate in range(2):
                    for kt in range(KD):
                        mm = pe.matmul(PS[0:4, 4, gate * 256:gate * 256 + 256], wgate[:, l, kt, gate * 4:gate * 4 + 4],
                                       hT[2][:, kt, :], start=kt == 0, stop=kt == KD - 1)
                mm.then_inc(*projected.now("gates", l, 0, 0))
                reader[4] = gate_abs.after(l)
                project_feat("mqk", l, 4, hT[2], freed=qk_ready)
                pe.wait_ge(*gate_scan.after(l))
                claim(5)
                for i in range(2):
                    for t in range(2):
                        mm = pe.transpose(PS[:, 5, (2 * i + t) * 4:(2 * i + t) * 4 + 4], gt[:, 4 + i, t * P:(t + 1) * P],
                                          ident[0:4, 0:4])
                mm.then_inc(*gate_turned.now(l))
                reader[5] = gate_cols.after(l)
                project_tok("mv", l, 2, KD, lhs)
                project_tok("mo", l, 2, KD, lhs)
                project_feat("rqk", l, 4, hT[2], freed=qk_ready)
                project_tok("rv", l, 4, KD, lhs)
                project_tok("rg", l, 4, KD, lhs)
                project_tok("gm", l, 2, KD, lhs)
                project_tok("gr", l, 2, KD, lhs)
                pe.wait_ge(*qk_ready_act.after("m", l, 3))
                pe.wait_ge(*gate_cols.after(l))
                pair_attention(l, "m", mqkT, mv, 256)
                pe.wait_ge(*qk_ready.after("rqk", l, 3, 0))
                pair_attention(l, "r", rqkT, rv, 512)
                turn(("ym", l), 8, 2, lambda b, t: hm[:, t, b * P:(b + 1) * P], ready=lambda t: y_ready.after("ym", l))
                turn(("yr", l), 16, 2, lambda b, t: hr[:, t, b * P:(b + 1) * P], ready=lambda t: y_ready.after("yr", l))
                await_copies(("ym", l), 8)
                project_tok("w_bm", l, 2, KD, lambda kt, t: ymT[:, kt, t * P:(t + 1) * P])
                await_copies(("yr", l), 16)
                project_tok("w_br", l, 2, 16, lambda kt, t: yrT[:, kt, t * P:(t + 1) * P])
                turn(("mg", l), 8, 2, lambda b, t: merged[:, t, b * P:(b + 1) * P],
                     ready=lambda t: stored.after("w_br", l, 1, 0))
                await_copies(("mg", l), 8)
                project_tok("w_out2", l, 2, KD, lambda kt, t: mergedT[:, kt, t * P:(t + 1) * P], freed=x_ready)
                norm(("n2", l), 2)
                project_feat("ff1", l, 8, hT[2], freed=hidden)
                pe.wait_ge(*hidden.after("ff1", l, 7, 0))
                project_tok("ff2", l, 2, 32, lambda kt, t: ff2T[:, kt, t * P:(t + 1) * P])
                norm(("n3", l), 2)
                project_tok("pe_g", l, 2, KD, lhs, freed=tok_acted)
                c, _ = take_chunk()
                w = ring[:, c % RING, :].rearrange("p (k n) -> p k n", k=2)
                pe.wait_ge(*pT_in.after(l))
                for j in range(2):
                    claim(2 * j, 2 * j + 1)
                    for t in range(2):
                        for kt in range(2):
                            mm = pe.matmul(PS[:, 2 * j + t, :], pT[:, kt * 256 + t * P:kt * 256 + (t + 1) * P],
                                           w[:, kt, j * 512:(j + 1) * 512], start=kt == 0, stop=kt == 1)
                    mm.then_inc(*projected.now("w_pe", l, j, 0))
                    reader[2 * j] = reader[2 * j + 1] = stored.after("w_pe", l, j, 0)
                projected.alias("used", c)

        @block.scalar
        def _(act):
            def link(ins, e=act_chain, *key):
                ins.then_inc(*e.now(*key))
                act.wait_ge(e.sem, e.count)

            def copy_odd(key, nb):
                for b in range(1, nb, 2):
                    act.wait_ge(*turned.after(key, b))
                    for o, i, scale, shift in copy_parts(key, b):
                        if scale is None:
                            ins = act.activation(o, i, ACT.Copy)
                        elif shift is None:
                            ins = act.activation(o, i, ACT.Copy, scale=scale)
                        else:
                            ins = act.activation(o, i, ACT.Identity, scale=scale, bias=shift)
                    ins.then_inc(*copied_s.now(key, b))

            def norm(key, tiles, src_ready):
                if src_ready:
                    act.wait_ge(*src_ready)
                for t in range(tiles):
                    ins = act.activation(xn[:, t, :], X[:, t, :], ACT.Square, accum_out=stat[:, t:t + 1])
                    link(ins)
                link(act.activation(stat[:, 4:4 + tiles], stat[:, 0:tiles], ACT.Sqrt, bias=eps, scale=1.0 / D),
                     root_ready, key)
                if key != "out":
                    copy_odd(key, KD)

            def root(key, n, d):
                act.wait_ge(*sums_ready.after(key))
                link(act.activation(stat[:, 64:64 + n], stat[:, 0:n], ACT.Sqrt, bias=eps, scale=1.0 / d),
                     root_ready, key)

            def attend(ph, prob, probT):
                us = units[ph]

                def exps(u):
                    d, s = us[u], 4 + 2 * (u % 2)
                    act.wait_ge(*max_ready.after(ph, u))
                    for i in range(len(d["scores"])):
                        ins = act.activation(prob[:, u % 2, i, 0:d["nk"]], PS[:, s + i, 0:d["nk"]], ACT.Exp,
                                             bias=stat[:, 192 + 4 * (u % 2) + i:193 + 4 * (u % 2) + i], scale=d["scale"],
                                             accum_out=stat[:, 200 + 4 * (u % 2) + i:201 + 4 * (u % 2) + i])
                        link(ins, *((exp_ready, ph, u) if i == len(d["scores"]) - 1 else (act_chain,)))

                def copy_probs(u):
                    act.wait_ge(*probs_turned.after(ph, u))
                    act.activation(probT[:, u % 2, 0:us[u]["nk"]], PS[:, u % 2, 0:us[u]["nk"]],
                                   ACT.Copy).then_inc(*probsT_ready.now(ph, u))

                exps(0)
                for u in range(len(us)):
                    if u + 1 < len(us):
                        exps(u + 1)
                    copy_probs(u)

            def gates(l):
                for n in range(len(gate_list(l))):
                    act.wait_ge(*gates_bc.after(l, n))
                    act.activation(G[:, n * 512:(n + 1) * 512], PS[:, 5 + n % 3, :],
                                   ACT.Copy).then_inc(*acted.now("gates", l, n))

            def swiglu(l, tiles):
                norm(("ffn", l), tiles, x_ready.after("w_out", l))
                for j in range(11):
                    for g in range(tiles // 2):
                        pair = (j * (tiles // 2) + g) % 2
                        act.wait_ge(*projected.after("ffn_in", l, j, g))
                        if j * (tiles // 2) + g >= 2:
                            jj, gg = divmod(j * (tiles // 2) + g - 2, tiles // 2)
                            act.wait_ge(*stored.after("ffn_in", l, jj, gg))
                        act.activation(SCR[:, pair * 512:pair * 512 + 512], PS[:, 2 * pair, :],
                                       ACT.Silu).then_inc(*unit_acted.now("ffn_in", l, j, g))

            act.wait_ge(tab_in.sem, 16 * 3)
            act.activation(small[:, 0:16], col("cond"), ACT.Silu).then_inc(*cond_ready.now())
            act.wait_ge(*lam_logit.after())
            act.activation(small[:, 20:22], small[:, 18:20], ACT.Exp).then_inc(*lam_exp.now())
            gates(0)
            act.wait_ge(*const_ready.after())
            norm(("mix", 0), 4, (x_in.sem, 32))
            root("da", 64, 64)
            copy_odd("daq", 4)
            copy_odd("dak", 4)
            attend("da", prob4, probT4)
            root("cq", 4, 256)
            root("ckv", 4, 128)
            root("kr", 4, 64)
            copy_odd("mlac", 3)
            root("mlaq", 16, 192)
            root("mlak", 16, 128)
            copy_odd("qn", 4)
            copy_odd("qr", 4)
            copy_odd("kn", 4)
            attend("mla", prob4, probT4)
            root("dao", 16, 128)
            copy_odd("y0", 8)
            swiglu(0, 4)
            gates(1)
            norm(("mix", 1), 4, x_ready.after("ffn_out", 0))
            root("naq", 32, 64)
            root("nak", 64, 64)
            copy_odd("naq", 8)
            copy_odd("nak", 8)
            attend("na", prob_na, probT_na)
            copy_odd("y1", 8)
            swiglu(1, 2)

            def in_place(st, l, n, buf, func):
                for j in range(n):
                    act.wait_ge(*stored.after(st, l, j, 0))
                    act.activation(buf[:, :, j * 512:(j + 1) * 512], buf[:, :, j * 512:(j + 1) * 512],
                                   func).then_inc(*tok_acted.now(st, l, j, 0))

            for l in range(2):
                norm(("n1", l), 2, x_ready.after("ffn_out", 1) if l == 0 else x_ready.after("pe", 0))
                act.wait_ge(*gate_abs.after(l))
                link(act.activation(gt[:, 2, :], gt[:, 2, :], ACT.Exp, scale=-1.0))
                link(act.activation(gt[:, 2, :], gt[:, 2, :], ACT.Ln, bias=small[0:4, 60:61], scale=1.0), gate_act, l)
                conv_in = SCR[:, 0:1036].rearrange("p (s t) -> p s t", s=4)
                for j in range(4):
                    act.wait_ge(*projected.after("mqk", l, j, 0))
                    act.wait_ge(*(qk_ready.after("mqk", l, j - 1, 0) if j else const_ready.after("pad", l)))
                    for s in range(4):
                        ins = act.activation(conv_in[:, s, 3:259],
                                             PS[:, 2 * (j % 2) + s // 2, (s % 2) * 256:(s % 2) * 256 + 256], ACT.Identity,
                                             bias=col("b_mqk")[:, l * 16 + j * 4 + s:l * 16 + j * 4 + s + 1])
                    ins.then_inc(*unit_acted.now("mqk", l, j, 0))
                    act.wait_ge(*qk_ready.after("mqk", l, j, 0))
                    act.activation(mqkT[:, 4 * j:4 * j + 4, :], mqkT[:, 4 * j:4 * j + 4, :],
                                   ACT.Silu).then_inc(*qk_ready_act.now("m", l, j))
                act.wait_ge(*gate_turned.after(l))
                act.activation(small[:, 32:40], PS[:, 5, 8:16], ACT.Exp, scale=-1.0)
                act.activation(small[:, 24:32], PS[:, 5, 0:8], ACT.Copy).then_inc(*gate_cols.now(l))
                in_place("mo", l, 2, mo, ACT.Sigmoid)
                rope_in = SCR[:, 0:1024].rearrange("p (s t) -> p s t", s=4)
                for j in range(4):
                    act.wait_ge(*projected.after("rqk", l, j, 0))
                    act.wait_ge(*(qk_ready.after("rqk", l, j - 1, 0) if j else qk_ready.after("mqk", l, 3, 0)))
                    for s in range(4):
                        ins = act.activation(rope_in[:, s, :],
                                             PS[:, 2 * (j % 2) + s // 2, (s % 2) * 256:(s % 2) * 256 + 256], ACT.Identity,
                                             bias=col("b_rqk")[:, l * 16 + j * 4 + s:l * 16 + j * 4 + s + 1])
                    ins.then_inc(*unit_acted.now("rqk", l, j, 0))
                in_place("rg", l, 4, rg, ACT.Silu)
                in_place("gm", l, 2, gm, ACT.Sigmoid)
                in_place("gr", l, 2, gr, ACT.Sigmoid)
                for h in range(R_H):
                    act.wait_ge(*exp_arg.after(l, h))
                    e = SCR[:, 768 + 384 * (h % 2):1152 + 384 * (h % 2)]
                    act.activation(e, e, ACT.Exp).then_inc(*exp_ready.now("m", l, h))
                for k in ("hm", "hr"):
                    act.wait_ge(*sums_ready.after(k, l))
                    view = stat[:, 128:144].rearrange("p (n s) -> p n s", s=2)
                    link(act.activation(stat[:, 144:152], view[:, :, 1], ACT.Sqrt, bias=eps, scale=1.0), root_ready, k, l)
                copy_odd(("ym", l), 8)
                copy_odd(("yr", l), 16)
                copy_odd(("mg", l), 8)
                norm(("n2", l), 2, x_ready.after("w_out2", l, 1, 0))
                for j in range(8):
                    pair = j % 2
                    act.wait_ge(*projected.after("ff1", l, j, 0))
                    if j >= 2:
                        act.wait_ge(*hidden.after("ff1", l, j - 2, 0))
                    for s in range(4):
                        ins = act.activation(SCR[:, 1024 * pair + 256 * s:1024 * pair + 256 * s + 256],
                                             PS[:, 2 * pair + s // 2, (s % 2) * 256:(s % 2) * 256 + 256], ACT.Relu,
                                             bias=col("b_ff1")[:, l * 32 + j * 4 + s:l * 32 + j * 4 + s + 1])
                    ins.then_inc(*ff_acted.now(l, j))
                norm(("n3", l), 2, x_ready.after("ff2", l))
                for j in range(2):
                    act.wait_ge(*projected.after("pe_g", l, j, 0))
                    act.activation(gm[:, :, j * 512:(j + 1) * 512], PS[:, 2 * j:2 * j + 2, :],
                                   ACT.Sigmoid).then_inc(*tok_acted.now("pe_g", l, j, 0))
            norm("out", 2, x_ready.after("pe", 1))

        @block.vector
        def _(dve):
            def link(ins, e=vec_chain, *key):
                ins.then_inc(*e.now(*key))
                dve.wait_ge(e.sem, e.count)

            def copy_even(key, nb):
                for b in range(0, nb, 2):
                    dve.wait_ge(*turned.after(key, b))
                    for o, i, scale, shift in copy_parts(key, b):
                        if scale is None:
                            ins = dve.tensor_copy(o, i)
                        elif shift is None:
                            ins = dve.tensor_scalar(o, i, scale, None, ALU.mult)
                        else:
                            ins = dve.tensor_scalar(o, i, scale, shift, ALU.mult, ALU.add)
                    ins.then_inc(*copied_v.now(key, b))

            def norm(key, tiles):
                dve.wait_ge(*root_ready.after(key))
                link(dve.reciprocal(stat[:, 8:8 + tiles], stat[:, 4:4 + tiles]))
                for t in range(tiles):
                    dve.tensor_scalar(xn[:, t, :], X[:, t, :], stat[:, 8 + t:9 + t], None,
                                      ALU.mult).then_inc(*normed.now(key, t))
                if key != "out":
                    copy_even(key, KD)

            def bc(a, shape):
                while len(a.shape) < len(shape):
                    a = a.unsqueeze(1)
                return a.to_broadcast(shape)

            def group_rms(key, x4, sq, gains):
                _, t, g, d = x4.shape
                n = t * g
                sq4 = sq[:, 0:n * d].rearrange("p (t g d) -> p t g d", t=t, g=g)
                link(dve.tensor_tensor(sq4, x4, x4, ALU.mult))
                link(dve.tensor_reduce(stat[:, 0:n], sq[:, 0:n * d].rearrange("p (n d) -> p n d", d=d), AX_X, ALU.add),
                     sums_ready, key)
                dve.wait_ge(*root_ready.after(key))
                link(dve.reciprocal(stat[:, 128:128 + n], stat[:, 64:64 + n]))
                r4 = stat[:, 128:128 + n].rearrange("p (t g) -> p t g", t=t).unsqueeze(3).to_broadcast([P, t, g, d])
                link(dve.tensor_tensor(x4, x4, r4, ALU.mult))
                for lo, hi, gain in gains:
                    part = x4[:, :, lo:hi, :]
                    link(dve.tensor_tensor(part, part, bc(gain, [P, t, hi - lo, d]), ALU.mult))

            def rope(x5, t, tmp):
                g = x5.shape[1]
                cos = bc(tab("cos").rearrange("p (t r j) -> p t r j", t=2, r=2)[:, t], [P, g, 2, 16])
                sin = bc(tab("sin").rearrange("p (t r j) -> p t r j", t=2, r=2)[:, t], [P, g, 2, 16])
                a, b, c, d = (tmp[:, i * g * 32:(i + 1) * g * 32].rearrange("p (g r j) -> p g r j", g=g, r=2)
                              for i in range(4))
                x1, x2 = x5[:, :, :, 0, :], x5[:, :, :, 1, :]
                dve.tensor_tensor(a, x1, cos, ALU.mult)
                dve.tensor_tensor(b, x2, sin, ALU.mult)
                dve.tensor_tensor(c, x1, sin, ALU.mult)
                link(dve.tensor_tensor(d, x2, cos, ALU.mult))
                dve.tensor_tensor(x1, a, b, ALU.subtract)
                link(dve.tensor_tensor(x2, c, d, ALU.add))

            def halves(x3):
                return x3.rearrange("p g (r h j) -> p g r h j", r=2, h=2)

            def attend(ph, prob, mix):
                us = units[ph]

                def maxes(u):
                    d, s = us[u], 4 + 2 * (u % 2)
                    n = len(d["scores"])
                    dve.wait_ge(*scored.after(ph, u))
                    if d["bias"] is not None:
                        link(dve.scalar_tensor_tensor(PS[:, s, 0:256], d["bias"], 1.0 / d["scale"], PS[:, s, 0:256],
                                                      ALU.mult, ALU.add))
                    m = stat[:, 208:208 + n]
                    link(dve.tensor_reduce(m, PS[:, s:s + n, 0:d["nk"]], AX_X, ALU.max))
                    o = 192 + 4 * (u % 2)
                    link(dve.tensor_scalar(stat[:, o:o + n], m, -d["scale"], None, ALU.mult), max_ready, ph, u)

                def norms(u):
                    d, o = us[u], 200 + 4 * (u % 2)
                    n, nk = len(d["scores"]), d["nk"]
                    dve.wait_ge(*exp_ready.after(ph, u))
                    link(dve.reciprocal(stat[:, 212:212 + n], stat[:, o:o + n]))
                    p0 = prob[:, u % 2, 0, 0:nk]
                    if n == 1:
                        link(dve.tensor_scalar(p0, p0, stat[:, 212:213], None, ALU.mult), probs_ready, ph, u)
                        return
                    link(dve.tensor_scalar(stat[:, 213:214], stat[:, 213:214], neg_lam, None, ALU.mult))
                    link(dve.tensor_scalar(p0, p0, stat[:, 212:213], None, ALU.mult))
                    link(dve.scalar_tensor_tensor(mix[:, u % 2, 0:nk], prob[:, u % 2, 1, 0:nk], stat[:, 213:214], p0,
                                                  ALU.mult, ALU.add), probs_ready, ph, u)

                def outs(u):
                    d = us[u]
                    dve.wait_ge(*attended.after(ph, u))
                    dve.tensor_copy(d["out"], PS[:, 2 + u % 2, 0:d["dv"]]).then_inc(*y_out.now(ph, u))

                maxes(0)
                for u in range(len(us)):
                    if u + 1 < len(us):
                        maxes(u + 1)
                    norms(u)
                    if u >= 1:
                        outs(u - 1)
                outs(len(us) - 1)

            def pair_view(pair):
                return PS[:, 2 * pair:2 * pair + 2, :]

            def modulation(l):
                dve.wait_ge(*modb_in[l].after(l))
                for j in range(12):
                    dve.wait_ge(*projected.after("mod", l, j, 0))
                    dve.tensor_tensor(mod_rows[:, j * 512:(j + 1) * 512], PS[0:2, j % 2, :],
                                      mod_bias[:, j * 512:(j + 1) * 512], ALU.add).then_inc(*mod_row.now(l, j))
                dve.wait_ge(*mod_turned.after(l))
                link(dve.tensor_copy(modc[:, :, :], PS[:, 4, 0:96].rearrange("p (k c) -> p k c", c=2)))
                for kind, name in ((1, "mix_g"), (4, "ffn_g")):
                    m = modc[:, kind * 8:kind * 8 + 8, :]
                    g = col(name)[:, l * 8:l * 8 + 8].unsqueeze(2).to_broadcast([P, 8, 2])
                    link(dve.scalar_tensor_tensor(m, m, 1.0, g, ALU.add, ALU.mult),
                         *((mod_ready, l) if kind == 4 else (vec_chain,)))

            def residual(st, l, n, groups, gates):
                for j in range(n):
                    for g in range(groups):
                        pair = (j * groups + g) % 2
                        dve.wait_ge(*projected.after(st, l, j, g))
                        gt_ = bc(gates[g][:, j * 512:(j + 1) * 512], [P, 2, 512])
                        tmp = SCR[:, 0:1024].rearrange("p (t n) -> p t n", t=2)
                        link(dve.tensor_tensor(tmp, pair_view(pair), gt_, ALU.mult), stored, st, l, j, g)
                        xs = X[:, 2 * g:2 * g + 2, j * 512:(j + 1) * 512]
                        link(dve.tensor_tensor(xs, xs, tmp, ALU.add), x_ready, st, l)

            def store(st, l, n, groups, dst):
                for j in range(n):
                    for g in range(groups):
                        pair = (j * groups + g) % 2
                        o = dst(j, g)
                        dve.wait_ge(*projected.after(st, l, j, g))
                        dve.tensor_copy(o, pair_view(pair)[:, :, 0:o.shape[2]]).then_inc(*stored.now(st, l, j, g))

            def swiglu(l, tiles):
                g_n = tiles // 2
                norm(("ffn", l), tiles)
                for j in range(11):
                    for g in range(g_n):
                        pair = (j * g_n + g) % 2
                        dve.wait_ge(*unit_acted.after("ffn_in", l, j, g))
                        s = SCR[:, pair * 512:pair * 512 + 512].rearrange("p (s t) -> p s t", s=2)
                        up = PS[:, 2 * pair + 1, :].rearrange("p (s t) -> p s t", s=2)
                        dve.tensor_tensor(ffT[l][:, 2 * j:2 * j + 2, g * 256:(g + 1) * 256], s, up,
                                          ALU.mult).then_inc(*stored.now("ffn_in", l, j, g))
                dve.wait_ge(stored.sem, stored.count)
                residual("ffn_out", l, 2, g_n, [gate(l, 5, g) for g in range(g_n)])

            dve.memset(small[:, 60:61], 1.0)
            link(dve.memset(eps, EPS), const_ready)
            dve.wait_ge(tab_in.sem, 16 * 3)
            link(dve.tensor_tensor(SCR[:, 0:128], row("lq"), row("lk"), ALU.mult))
            link(dve.tensor_reduce(small[:, 18:20], SCR[:, 0:128].rearrange("p (a d) -> p a d", a=2), AX_X, ALU.add),
                 lam_logit)
            dve.wait_ge(*lam_exp.after())
            link(dve.tensor_tensor(small[:, 22:23], small[:, 21:22], small[:, 20:21], ALU.subtract))
            link(dve.tensor_scalar(neg_lam, small[:, 22:23], -LAM_INIT, None, ALU.add))
            modulation(0)
            norm(("mix", 0), 4)
            store("ev_in", 0, 4, 2, lambda j, g: z0[:, 2 * g:2 * g + 2, j * 512:min(j * 512 + 512, EV_IN)])
            dve.wait_ge(stored.sem, stored.count)
            qk = z0[:, :, 0:1024].rearrange("p t (g d) -> p t g d", d=64)
            group_rms("da", qk, xn_, [(0, 8, row("da_q_g")), (8, 16, row("da_k_g"))])
            for t in range(TX):
                rope(halves(qk[:, t]), t, xn_)
            link(dve.memset(small[:, 16:17], 0.0), pre_turn, "da")
            copy_even("daq", 4)
            copy_even("dak", 4)
            attend("da", prob4, mix4)
            group_rms("cq", z0[:, :, 1536:1792].unsqueeze(2), big(14592, 4096), [(0, 1, row("mla_q_a_g"))])
            group_rms("ckv", z0[:, :, 1792:1920].unsqueeze(2), big(14592, 4096), [(0, 1, row("mla_kv_a_g"))])
            kr = z0[:, :, 1920:1984].unsqueeze(2)
            group_rms("kr", kr, big(14592, 4096), [(0, 1, row("mla_kr_g"))])
            for t in range(TX):
                rope(halves(kr[:, t]), t, big(14592, 4096))
            link(dve.memset(small[:, 16:17], 0.0), pre_turn, "mla_c")
            copy_even("mlac", 3)
            copy_even("mlakr", 1)
            for st, dst, w in (("uq", q_l0, 384), ("ukv", v["kv"], 512)):
                for t in range(4):
                    dve.wait_ge(*projected.after(st, 0, t, 0))
                    dve.tensor_copy(dst[:, t, :].rearrange("p (s n) -> p s n", s=2),
                                    pair_view(t % 2)[:, :, 0:w]).then_inc(*stored.now(st, 0, t, 0))
            dve.wait_ge(stored.sem, stored.count)
            qh = q_l0.rearrange("p t (g d) -> p t g d", g=4)
            group_rms("mlaq", qh, big(14592, 4096), [(0, 4, row("mla_q_g"))])
            for t in range(TX):
                rope(halves(qh[:, t, :, 128:192]), t, big(14592, 4096))
            kh = v["kv"].rearrange("p t (g d) -> p t g d", g=4)[:, :, :, 0:128]
            group_rms("mlak", kh, big(14592, 4096), [(0, 4, row("mla_k_g"))])
            link(dve.memset(small[:, 16:17], 0.0), pre_turn, "mla_q")
            for k in ("qn", "qr", "kn"):
                copy_even(k, 4)
            attend("mla", prob4, None)
            dve.wait_ge(y_out.sem, y_out.count)
            yd = xn[:, :, 0:512].rearrange("p t (g d) -> p t g d", g=4)
            group_rms("dao", yd, big(14592, 4096), [(0, 4, row("da_out_g"))])
            link(dve.tensor_scalar(xn[:, :, 0:512], xn[:, :, 0:512], 1.0 - LAM_INIT, None, ALU.mult), y_ready, "ev", 0)
            copy_even("y0", 8)
            dve.wait_ge(*acted.after("gates", 0, 7))
            residual("w_out", 0, 2, 2, [gate(0, 2, 0), gate(0, 2, 1)])
            swiglu(0, 4)
            modulation(1)
            norm(("mix", 1), 4)
            store("od_q", 1, 2, 1, lambda j, g: nq[:, :, j * 512:(j + 1) * 512])
            store("od_kv", 1, 4, 2, lambda j, g: (nk_ if j < 2 else v["nv"])[:, 2 * g:2 * g + 2,
                                                                           (j % 2) * 512:(j % 2) * 512 + 512])
            dve.wait_ge(stored.sem, stored.count)
            group_rms("naq", nq.rearrange("p t (g d) -> p t g d", d=64), xn_, [(0, 16, row("na_q_g"))])
            group_rms("nak", nk_.rearrange("p t (g d) -> p t g d", d=64), xn_, [(0, 16, row("na_k_g"))])
            link(dve.memset(small[:, 16:17], 0.0), pre_turn, "na")
            dve.wait_ge(rel_in.sem, rel_in.count)
            rel = v["rel"].rearrange("p t h (i c) -> p (t h i) c", i=NA_ROWS)
            link(dve.tensor_tensor(rel, rel, bc(tab("na_mask"), [P, rel.shape[1], GRID_W]), ALU.add))
            copy_even("naq", 8)
            copy_even("nak", 8)
            attend("na", prob_na, None)
            copy_even("y1", 8)
            dve.wait_ge(*acted.after("gates", 1, 3))
            residual("w_out", 1, 2, 1, [gate(1, 2, 0)])
            swiglu(1, 2)

            state = {"b": 0}

            def biased(st, l, n, dst, then=None):
                for j in range(n):
                    b = state["b"]
                    state["b"] += 1
                    dve.wait_ge(*projected.after(st, l, j, 0))
                    dve.wait_ge(*bias_in[b % 2].after(b))
                    br = bc(bias_ring[:, b % 2, :], [P, 2, 512])
                    ins = dve.tensor_tensor(dst(j), pair_view(j % 2), br, ALU.add)
                    ins.then_inc(*stored.now(st, l, j, 0))
                    stored.alias("bias", b)
                    if then:
                        dve.wait_ge(stored.sem, stored.count)
                        then(j)

            def layer_norms(l, key, h_buf, width, gain, gate_buf):
                link(dve.memset(small[:, 16:17], 0.0), sums_ready, key, l)
                dve.wait_ge(*root_ready.after(key, l))
                link(dve.reciprocal(stat[:, 152:160], stat[:, 144:152]))
                for t in range(2):
                    for h in range(R_H):
                        i = t * R_H + h
                        s = h_buf[:, t, h * width:(h + 1) * width]
                        ins = dve.tensor_scalar(s, s, stat[:, 128 + 2 * i:129 + 2 * i], stat[:, 152 + i:153 + i],
                                                ALU.subtract, ALU.mult)
                link(ins)
                w = R_H * width
                link(dve.tensor_tensor(h_buf, h_buf, bc(gain, [P, 2, w]), ALU.mult))
                dve.wait_ge(*tok_acted.after("mo" if key == "hm" else "rg", l, w // 512 - 1, 0))
                link(dve.tensor_tensor(h_buf, h_buf, gate_buf, ALU.mult), y_ready, "ym" if key == "hm" else "yr", l)

            for l in range(2):
                norm(("n1", l), 2)
                dve.wait_ge(*projected.after("gates", l, 0, 0))
                dve.tensor_scalar(gt[:, 0, :], PS[0:4, 4, 0:256], bgate[:, l, 0:1], None, ALU.add)
                link(dve.tensor_scalar(gt[:, 1, :], PS[0:4, 4, 256:512], bgate[:, l, 1:2], None, ALU.add))
                link(dve.scalar_tensor_tensor(gt[:, 2, :], gt[:, 1, :], -1.0, gt[:, 1, :], ALU.mult, ALU.max), gate_abs, l)
                conv_in = SCR[:, 0:1036].rearrange("p (s t) -> p s t", s=4)
                link(dve.memset(conv_in[:, :, 0:3], 0.0), const_ready, "pad", l)
                dve.wait_ge(*gate_act.after(l))
                link(dve.scalar_tensor_tensor(gt[:, 1, :], gt[:, 1, :], 0.0, gt[:, 2, :], ALU.min, ALU.subtract))
                link(dve.memset(gt[:, 7, :], 0.0))
                link(dve.tensor_tensor_scan(gt[:, 6, :], gt[:, 1, :], gt[:, 7, :], 0.0, ALU.add, ALU.add))
                link(dve.tensor_tensor(gt[:, 4, :], gt[:, 0, :], gt[:, 6, :], ALU.subtract))
                link(dve.tensor_tensor_scan(gt[:, 5, :], gt[:, 4, :], gt[:, 7, :], 0.0, ALU.max, ALU.max))
                link(dve.tensor_scalar(gt[:, 3, :], gt[:, 5, :], -1.0, None, ALU.mult))
                link(dve.tensor_tensor(gt[:, 5, :], gt[:, 5, :], gt[:, 6, :], ALU.add), gate_scan, l)
                cw = col("conv_w")
                for j in range(4):
                    dve.wait_ge(*unit_acted.after("mqk", l, j, 0))
                    for k in range(4):
                        for s in range(4):
                            ch = j * 4 + s
                            o = mqkT[:, ch, :]
                            wk = cw[:, (l * 4 + k) * 16 + ch:(l * 4 + k) * 16 + ch + 1]
                            i = conv_in[:, s, k:k + 256]
                            if k == 0:
                                ins = dve.tensor_scalar(o, i, wk, col("conv_b")[:, l * 16 + ch:l * 16 + ch + 1],
                                                        ALU.mult, ALU.add)
                            else:
                                ins = dve.scalar_tensor_tensor(o, i, wk, o, ALU.mult, ALU.add)
                        if k < 3:
                            link(ins)
                    ins.then_inc(*qk_ready.now("mqk", l, j, 0))
                biased("mv", l, 2, lambda j: mv[:, :, j * 512:(j + 1) * 512])
                biased("mo", l, 2, lambda j: mo[:, :, j * 512:(j + 1) * 512])
                cosT, sinT = (bc(tab(n), [P, 2, 256]) for n in ("cosT", "sinT"))
                rope_in = SCR[:, 0:1024].rearrange("p (h s t) -> p h s t", h=2, s=2)
                tmp = SCR[:, 1024:2048].rearrange("p (a h t) -> p a h t", a=2, h=2)
                for j in range(4):
                    dve.wait_ge(*unit_acted.after("rqk", l, j, 0))
                    x1, x2 = rope_in[:, :, 0, :], rope_in[:, :, 1, :]
                    o = rqkT[:, 4 * j:4 * j + 4, :].rearrange("p (h s) t -> p h s t", s=2)
                    dve.tensor_tensor(tmp[:, 0], x1, cosT, ALU.mult)
                    link(dve.tensor_tensor(tmp[:, 1], x2, sinT, ALU.mult))
                    link(dve.tensor_tensor(o[:, :, 0, :], tmp[:, 0], tmp[:, 1], ALU.subtract))
                    dve.tensor_tensor(tmp[:, 0], x1, sinT, ALU.mult)
                    link(dve.tensor_tensor(tmp[:, 1], x2, cosT, ALU.mult))
                    ins = dve.tensor_tensor(o[:, :, 1, :], tmp[:, 0], tmp[:, 1], ALU.add)
                    ins.then_inc(*qk_ready.now("rqk", l, j, 0))
                    dve.wait_ge(qk_ready.sem, qk_ready.count)
                biased("rv", l, 4, lambda j: rv[:, :, j * 512:(j + 1) * 512])
                biased("rg", l, 4, lambda j: rg[:, :, j * 512:(j + 1) * 512])
                biased("gm", l, 2, lambda j: gm[:, :, j * 512:(j + 1) * 512])
                biased("gr", l, 2, lambda j: gr[:, :, j * 512:(j + 1) * 512])
                dve.wait_ge(*gate_cols.after(l))
                dve.wait_ge(*nrows_in.after(l))
                mask = tab("mask")

                def head_stats(key, h, h_buf, width):
                    for t in range(2):
                        i = t * R_H + h
                        link(dve.bn_stats(stat[:, 160 + 6 * t:166 + 6 * t], h_buf[:, t, h * width:(h + 1) * width]))
                        link(dve.bn_aggr(stat[:, 128 + 2 * i:130 + 2 * i], stat[:, 160 + 6 * t:166 + 6 * t]))

                def m_out(h):
                    o = 2 * (h % 2)
                    dve.wait_ge(*attended.after("m", l, h))
                    for t in range(2):
                        den, floor = small[:, 40 + t:41 + t], small[:, 32 + 4 * t + h:33 + 4 * t + h]
                        link(dve.tensor_scalar(den, PS[:, o + t, 256:257], -1.0, floor, ALU.mult, ALU.max))
                        link(dve.tensor_tensor(den, den, PS[:, o + t, 256:257], ALU.max))
                    link(dve.reciprocal(small[:, 42:44], small[:, 40:42]))
                    for t in range(2):
                        ins = dve.tensor_scalar(hm[:, t, h * 256:(h + 1) * 256], PS[:, o + t, 0:256],
                                                small[:, 42 + t:43 + t], None, ALU.mult)
                    link(ins, y_out, "m", l, h)
                    head_stats("hm", h, hm, 256)

                def r_out(h):
                    o = 2 * (h % 2)
                    dve.wait_ge(*attended.after("r", l, h))
                    link(dve.tensor_copy(hr[:, :, h * 512:(h + 1) * 512], PS[:, o:o + 2, :]), y_out, "r", l, h)
                    head_stats("hr", h, hr, 512)

                def arg(h):
                    dve.wait_ge(*u_bc.after(l, h))
                    e = SCR[:, 768 + 384 * (h % 2):1152 + 384 * (h % 2)]
                    ub = PS[:, 6 + h % 2, 0:256]
                    dve.scalar_tensor_tensor(e[:, 0:256], ub, small[:, 24 + h:25 + h], mask[:, 0:256], ALU.add, ALU.add)
                    link(dve.scalar_tensor_tensor(e[:, 256:384], ub[:, 128:256], small[:, 28 + h:29 + h],
                                                  mask[:, 256:384], ALU.add, ALU.add), exp_arg, l, h)

                arg(0)
                for h in range(R_H):
                    if h < 3:
                        arg(h + 1)
                    if h == 0:
                        dve.wait_ge(*scored.after("m", l, h))
                    dve.wait_ge(*exp_ready.after("m", l, h))
                    link(dve.scalar_tensor_tensor(SCR[:, 384 * (h % 2):384 * (h % 2) + 384], PS[:, 4 + h % 2, 0:384],
                                                  QK_SCALE, SCR[:, 768 + 384 * (h % 2):1152 + 384 * (h % 2)],
                                                  ALU.mult, ALU.mult), probs_ready, "m", l, h)
                    if h >= 1:
                        m_out(h - 1)
                m_out(R_H - 1)
                layer_norms(l, "hm", hm, 256, G[:, 0:1024], mo)
                decay = tab("decay").rearrange("p (h n) -> p h n", h=R_H)
                for h in range(R_H):
                    dve.wait_ge(*scored.after("r", l, h))
                    link(dve.scalar_tensor_tensor(SCR[:, 384 * (h % 2):384 * (h % 2) + 384], PS[:, 4 + h % 2, 0:384],
                                                  QK_SCALE, decay[:, h, :], ALU.mult, ALU.mult),
                         probs_ready, "r", l, h)
                    if h >= 1:
                        r_out(h - 1)
                r_out(R_H - 1)
                layer_norms(l, "hr", hr, 512, G[:, 1024:3072], rg)
                copy_even(("ym", l), 8)
                copy_even(("yr", l), 16)
                for j in range(2):
                    dve.wait_ge(*projected.after("w_bm", l, j, 0))
                    if j == 0:
                        dve.wait_ge(*tok_acted.after("gr", l, 1, 0))
                    cols = slice(j * 512, (j + 1) * 512)
                    dve.tensor_tensor(merged[:, :, cols], pair_view(j), gm[:, :, cols],
                                      ALU.mult).then_inc(*stored.now("w_bm", l, j, 0))
                for j in range(2):
                    dve.wait_ge(*projected.after("w_br", l, j, 0))
                    cols = slice(j * 512, (j + 1) * 512)
                    tmp2 = SCR[:, 0:1024].rearrange("p (t n) -> p t n", t=2)
                    link(dve.tensor_tensor(tmp2, pair_view(j), gr[:, :, cols], ALU.mult))
                    link(dve.tensor_tensor(merged[:, :, cols], merged[:, :, cols], tmp2, ALU.add),
                         stored, "w_br", l, j, 0)
                copy_even(("mg", l), 8)
                for j in range(2):
                    dve.wait_ge(*projected.after("w_out2", l, j, 0))
                    xs = X[:, 0:2, j * 512:(j + 1) * 512]
                    ins = dve.tensor_tensor(xs, xs, pair_view(j), ALU.add)
                    link(ins, x_ready, "w_out2", l, j, 0)
                norm(("n2", l), 2)
                for j in range(8):
                    dve.wait_ge(*ff_acted.after(l, j))
                    s = SCR[:, 1024 * (j % 2):1024 * (j % 2) + 1024].rearrange("p (s t) -> p s t", s=4)
                    ins = dve.tensor_tensor(ff2T[:, 4 * j:4 * j + 4, :], s, s, ALU.mult)
                    ins.then_inc(*hidden.now("ff1", l, j, 0))
                dve.wait_ge(hidden.sem, hidden.count)

                def add_x(j):
                    xs = X[:, 0:2, j * 512:(j + 1) * 512]
                    t2 = SCR[:, 0:1024].rearrange("p (t n) -> p t n", t=2)
                    link(dve.tensor_tensor(xs, xs, t2, ALU.add), x_ready, "ff2", l)
                biased("ff2", l, 2, lambda j: SCR[:, 0:1024].rearrange("p (t n) -> p t n", t=2), add_x)
                norm(("n3", l), 2)
                for j in range(2):
                    dve.wait_ge(*projected.after("w_pe", l, j, 0))
                    cols = slice(j * 512, (j + 1) * 512)
                    t2 = SCR[:, 0:1024].rearrange("p (t n) -> p t n", t=2)
                    link(dve.tensor_tensor(t2, pair_view(j), gm[:, :, cols], ALU.mult), stored, "w_pe", l, j, 0)
                    link(dve.tensor_tensor(X[:, 0:2, cols], X[:, 0:2, cols], t2, ALU.add), x_ready, "pe", l)
            norm("out", 2)
            dve.wait_ge(normed.sem, normed.count)
            link(dve.tensor_tensor(xn[:, 0:2, :], xn[:, 0:2, :], bc(G[:, 3072:4096], [P, 2, D]), ALU.mult),
                 x_ready, "out")


def weight_chunks(w):
    k, n = w.shape
    kg, nb = -(-k // (KC * P)), -(-n // NC_)
    full = np.zeros((kg * KC * P, nb * NC_), w.dtype)
    full[:k, :n] = w
    return full.reshape(kg, KC, P, nb, NC_).transpose(3, 0, 2, 1, 4).reshape(nb * kg, P, CHUNK)


def flat_chunk(w):
    k, n = w.shape
    out = np.zeros((1, P, CHUNK), w.dtype)
    out[0, :, :k // P * n] = w.reshape(k // P, P, n).transpose(1, 0, 2).reshape(P, -1)
    return out


def paired(w):
    g, u = w[:, :D_FF], w[:, D_FF:]
    return np.stack([g.reshape(-1, D_FF // 256, 256), u.reshape(-1, D_FF // 256, 256)], 2).reshape(w.shape)


def feature_cols(a):
    return a.reshape(-1, a.shape[-1] // P, P).transpose(2, 0, 1).reshape(P, -1)


def lay_out(i):
    chunks = []
    for l in range(2):
        chunks.append(weight_chunks(i["mod_w"][l]))
        if l == 0:
            chunks += [weight_chunks(i["ev_w_in"][0]), flat_chunk(i["mla_w_uq"][0]), flat_chunk(i["mla_w_ukv"][0])]
        else:
            chunks.append(weight_chunks(i["od_w_in"][0]))
        chunks += [weight_chunks(i["w_out"][l]), weight_chunks(paired(i["ffn_w_in"][l])),
                   weight_chunks(i["ffn_w_out"][l])]
    cuts = [0, 2048, 3072, 4096, 4104, 6152, 8200, 10248, 11272, 12296]
    brows = []
    for l in range(2):
        w, b = i["w_in_2"][l], i["b_in_2"][l]
        for n in (0, 1, 2, 4, 5, 6, 7, 8):
            chunks.append(weight_chunks(w[:, cuts[n]:cuts[n + 1]]))
            if n not in (0, 4):
                brows.append(b[cuts[n]:cuts[n + 1]])
        brows.append(i["b_ff2_2"][l])
        chunks += [weight_chunks(i[k][l]) for k in ("w_bm_2", "w_br_2", "w_out_2", "w_ff1_2", "w_ff2_2", "w_pe_gate_2")]
        chunks.append(flat_chunk(i["w_pe_2"][l]))
    cols = [np.stack([i["c"][0], i["c_ctx"]]).reshape(2, KD, P).transpose(2, 1, 0).reshape(P, -1)]
    cols += [feature_cols(i[k]) for k in ("norm_mix_g", "norm_ffn_g", "norm1_g_2", "norm2_g_2", "norm3_g_2")]
    b_in = i["b_in_2"]
    cols += [feature_cols(b_in[:, 0:2048]), feature_cols(b_in[:, 4104:6152]), feature_cols(i["conv_w_2"]),
             feature_cols(i["conv_b_2"]), feature_cols(i["b_ff1_2"])]
    rows = [i["da_q_g"], i["da_k_g"], i["da_lq1"], i["da_lq2"], i["da_lk1"], i["da_lk2"], i["da_out_g"],
            i["mla_q_a_g"], i["mla_kv_a_g"], i["mla_q_g"], i["mla_k_g"], i["mla_kr_g"], i["na_q_g"], i["na_k_g"]]
    padded = np.zeros((NA_H, 2 * NA_KH - 1, REL_W), np.float32)
    padded[:, :, GRID_W - NA_KW:GRID_W + NA_KW - 1] = i["na_rpb"][0]
    rel = np.stack([padded[:, :, GRID_W - 1 - q:REL_W - q] for q in range(GRID_W)])
    wg = i["w_in_2"][:, :, 4096:4104].reshape(2, KD, P, 8).transpose(2, 0, 1, 3)
    nrows = np.zeros((2, 4096), np.float32)
    nrows[:, 0:1024], nrows[:, 1024:3072], nrows[:, 3072:] = i["m_norm_g_2"], i["r_norm_g_2"], i["final_g_2"]
    tiles = lambda a: a.reshape(TX, P, D).transpose(1, 0, 2)
    arrays = [tiles(i["x"]), tiles(i["ctx"]), np.concatenate(chunks), np.concatenate(cols, 1),
              np.concatenate([r.reshape(-1) for r in rows]), tables(), i["mod_b"], rel,
              np.concatenate(brows).reshape(-1, NC_), b_in[:, 4096:4104].reshape(2, 2, 4).transpose(2, 0, 1), wg, nrows,
              i["p_2"][:, 0].reshape(2, SEQ, 2, P).transpose(3, 0, 2, 1).reshape(P, 2, 512)]
    return [np.ascontiguousarray(a) for a in arrays]


NAMES = ["x", "ctx", "chunks", "cols", "rows", "tabs", "modb", "rel", "brows", "bgate", "wgate", "nrows", "pT"]


def kernel(**inputs):
    import concourse.bacc as bacc
    from concourse.bass_utils import run_bass_kernel_spmd

    arrays = lay_out({k: np.asarray(a) for k, a in inputs.items()})
    plan = {}
    for _ in range(2):
        nc = bacc.Bacc("TRN2", target_bir_lowering=False, num_devices=1, dynamic_dma_scratch_size=8192)
        ins = [nc.dram_tensor(n + "_in", a.shape, F32, kind="ExternalInput").ap() for n, a in zip(NAMES, arrays)]
        out = nc.dram_tensor("out", (1, SEQ, D), F32, kind="ExternalOutput").ap()
        build_program(nc, plan, ins, out.rearrange("b (t p) d -> p (b t) d", p=P))
    r = run_bass_kernel_spmd(nc, [{n + "_in": a for n, a in zip(NAMES, arrays)}], core_ids=[0])
    return r.results[0]["out"]
```

```python
from contextlib import ExitStack

import numpy as np

import concourse.bass as bass
from concourse import mybir

ALU = mybir.AluOpType
ACT = mybir.ActivationFunctionType
F32 = mybir.dt.float32
F32R = mybir.dt.float32r
AX_X = mybir.AxisListType.X

P = 128
D = 1024
KD = D // P
SEQ = 256
TX = SEQ // P
GRID_W = 64
DA_H, DA_DK, DA_DV = 4, 64, 128
ML_H, ML_NOPE, ML_ROPE, ML_V = 4, 128, 64, 128
ML_QL, ML_KVL = 256, 128
ML_QK = ML_NOPE + ML_ROPE
EV_IN = 3 * DA_H * 2 * DA_DK + ML_QL + ML_KVL + ML_ROPE
NA_H, NA_DH, NA_KH, NA_KW = 16, 64, 8, 16
NA_ROWS = SEQ // GRID_W
D_FF = 2816
KF = D_FF // P
EPS = 1e-6
LAM_INIT = 0.2
R_H = 4
QK_SCALE = 1.0 / 16.0
NEG = -1e30

NC_ = 512
KC = 4
CHUNK = KC * NC_
FF_PARTS = ((4, 4, 3), (11,))
MOD_PARTS = ((12,), (3, 4, 3, 2))
RING = 4
HI_RING = 3
AHEAD = HI_RING - 1
REL_W = 2 * GRID_W - 1

COLS = [("cond", 2 * KD), ("mix_g", 2 * KD), ("ffn_g", 2 * KD), ("n1", 2 * KD), ("n2", 2 * KD), ("n3", 2 * KD),
        ("b_mqk", 32), ("b_rqk", 32), ("conv_w", 128), ("conv_b", 32), ("b_ff1", 64)]
ROWS = [("da_q_g", 64), ("da_k_g", 64), ("lq", 128), ("lk", 128), ("da_out_g", 128), ("mla_q_a_g", 256),
        ("mla_kv_a_g", 128), ("mla_q_g", 192), ("mla_k_g", 128), ("mla_kr_g", 64), ("na_q_g", 64), ("na_k_g", 64)]
TABS = [("ident", 128), ("cos", 64), ("sin", 64), ("cosT", 256), ("sinT", 256), ("decay", 4 * 384), ("mask", 384),
        ("ones", 128), ("sel_h", 4 * 128), ("na_mask", GRID_W)]


def spans(items):
    at, out = 0, {}
    for name, n in items:
        out[name] = (at, at + n)
        at += n
    return out, at


def tables():
    s, n = spans(TABS)
    t = np.zeros((P, n), np.float32)

    def put(name, a):
        t[:a.shape[0], s[name][0]:s[name][1]] = a.reshape(a.shape[0], -1)

    put("ident", np.eye(P))
    tok = np.arange(SEQ)
    half = DA_DK // 2
    inv = (np.float32(10000.0) ** (-np.arange(0, half, 2, dtype=np.float32) / np.float32(half))).astype(np.float32)
    ang = np.stack([(tok // GRID_W).astype(np.float32)[:, None] * inv,
                    (tok % GRID_W).astype(np.float32)[:, None] * inv], 1).astype(np.float32)
    by_tile = ang.reshape(TX, P, 2, half // 2).transpose(1, 0, 2, 3)
    put("cos", np.cos(by_tile))
    put("sin", np.sin(by_tile))
    inv2 = (np.float32(10000.0) ** (-np.arange(0, 256, 2, dtype=np.float32) / np.float32(256))).astype(np.float32)
    ang2 = (inv2[:, None] * tok.astype(np.float32)[None, :]).astype(np.float32)
    put("cosT", np.cos(ang2))
    put("sinT", np.sin(ang2))
    p = np.arange(P)
    s_of = np.concatenate([np.zeros(256), np.full(128, 128)])[None, :] + p[:, None]
    t_of = np.concatenate([np.arange(256), np.arange(128, 256)])[None, :] + 0 * p[:, None]
    lg = np.log(1.0 - np.exp2(-5.0 - np.arange(R_H)))
    put("decay", np.stack([np.where(t_of >= s_of, np.exp((t_of - s_of) * g), 0.0) for g in lg], 1))
    put("mask", np.where(t_of >= s_of, 0.0, NEG))
    put("ones", np.ones((P, P)))
    put("sel_h", np.repeat(np.eye(R_H)[:, :, None], P, 2))
    qc, kc = (p % GRID_W)[:, None], np.arange(GRID_W)[None, :]
    start = np.clip(qc - NA_KW // 2, 0, GRID_W - NA_KW)
    put("na_mask", np.where((kc >= start) & (kc < start + NA_KW), 0.0, NEG))
    return t


class Event:

    def __init__(self, sem, name, plan):
        self.sem, self.name, self.plan, self.count = sem, name, plan, 0

    def now(self, *step, by=1):
        self.count += by
        self.plan[(self.name, step)] = self.count
        return self.sem, by

    def after(self, *step):
        return self.sem, self.plan.get((self.name, step), 1)

    def alias(self, *step):
        self.plan[(self.name, step)] = self.count


def attention_units(v):
    phases = {}
    da, mla, na = [], [], []
    for h in range(DA_H):
        for t in range(4):
            k0, nk = (0, 512) if t < TX else (256, 256)
            da.append(dict(scores=[[(v["dqT"][64 * i:64 * i + 64, h, t * P:(t + 1) * P],
                                     v["dkT"][64 * i:64 * i + 64, h, k0:k0 + nk])] for i in range(2)],
                           nk=nk, scale=DA_DK ** -0.5, bias=None, dv=DA_DV,
                           value=[v["z"][:, (k0 // P) + j, 1024 + h * 128:1024 + (h + 1) * 128] for j in range(nk // P)],
                           out=v["y4"][:, t, h * 128:(h + 1) * 128]))
    for h in range(ML_H):
        for t in range(4):
            k0, nk = (0, 512) if t < TX else (256, 256)
            q = slice(t * P, (t + 1) * P)
            mla.append(dict(scores=[[(v["qnT"][:, h, q], v["knT"][:, h, k0:k0 + nk]),
                                     (v["qrT"][0:64, h, q], v["krT"][0:64, k0:k0 + nk])]],
                            nk=nk, scale=ML_QK ** -0.5, bias=None, dv=ML_V,
                            value=[v["kv"][:, (k0 // P) + j, h * 256 + 128:h * 256 + 256] for j in range(nk // P)],
                            out=v["y4"][:, t, 512 + h * 128:512 + (h + 1) * 128]))
    for h in range(NA_H):
        for t in range(TX):
            part = slice(64 * (h % 2), 64 * (h % 2) + 64)
            na.append(dict(scores=[[(v["nqT"][part, h // 2, t * P:(t + 1) * P], v["nkT"][part, h // 2, :])]],
                           nk=512, scale=NA_DH ** -0.5, bias=v["rel"][h // 8][:, t, h % 8, :], dv=NA_DH,
                           value=[v["nv"][:, j, h * 64:(h + 1) * 64] for j in range(4)],
                           out=v["y4"][:, t, h * 64:(h + 1) * 64]))
    phases["da"], phases["mla"], phases["na"] = da, mla, na
    return phases


def build_program(nc, plan, ins, out):
    x_d, ctx_d, chunks_d, cols_d, rows_d, tabs_d, modb_d, rel_d, brows_d, bgate_d, wgate_d, nrows_d, pT_d = ins
    ctx = ExitStack()
    with ctx:
        def sb(name, shape):
            return ctx.enter_context(nc.sbuf_tensor(name, shape, F32))

        def ev(name):
            return Event(ctx.enter_context(nc.semaphore(name)), name, plan)

        cs, ncols = spans(COLS)
        rs, nrows = spans(ROWS)
        ts, ntabs = spans(TABS)
        arena_floats = (nc.sbuf_usable_end - nc.sbuf_base) // 4 - 16
        arena = ctx.enter_context(nc.sbuf_tensor("arena", [P, arena_floats], F32))
        base = nc.sbuf_base - 4 * arena_floats
        cursor = [0]

        def place(name, n, dt=F32, at=None):
            start = cursor[0] if at is None else at
            if at is None:
                cursor[0] += -(-n // 8) * 8
            assert cursor[0] <= arena_floats, name
            return nc.alloc_sbuf_tensor_at(name, [P, n], dt, offset=base + 4 * start), start

        raw_, raw_at = place("raw", RING * CHUNK)
        wlo_, _ = place("w_lo", RING * CHUNK, F32R, raw_at)
        whi_, _ = place("w_hi", HI_RING * CHUNK, F32R)
        xhi_, xhi_at = place("x_hi", 4096, F32R)
        xlo_, xlo_at = place("x_lo", 4096, F32R)
        free_a, _ = place("free_a", 4096, F32, xhi_at)
        free_b, _ = place("free_b", 4096, F32, xlo_at)
        X = place("X", 4 * D)[0][:, :].rearrange("p (t d) -> p t d", t=4)
        xn_ = place("xn", 4 * D)[0]
        G = place("G", 4096)[0]
        SCR = place("SCR", 2048)[0]
        colt = place("colt", ncols)[0]
        rowt = place("rowt", nrows)[0]
        gt = rowt[0:4, 0:1280].rearrange("p (a t) -> p a t", a=5)
        tabt = place("tabt", ntabs)[0]
        wgate = place("wgate", 128)[0]
        wgh = place("wgate_hi", 128, F32R)[0]
        wgl = place("wgate_lo", 128, F32R)[0]
        pT = place("pT", 512)[0]
        bias_ = place("bias_ring", 2 * NC_)[0]
        bias_ring = bias_[:, :].rearrange("p (b n) -> p b n", b=2)
        modc = [bias_[:, l * 96:l * 96 + 96].rearrange("p (k c) -> p k c", c=2) for l in range(2)]
        mod_bias = bias_[:, 192:288].rearrange("p (l k) -> p l k", l=2)
        stat = place("stat", 216)[0]
        small = place("small", 64)[0]
        bgate = place("bgate", 4)[0][0:4, :].rearrange("p (l g) -> p l g", l=2)
        n_big = 12288
        BIG, big_at = place("BIG", n_big)
        BIGR, _ = place("BIGR", n_big, F32R, big_at)
        ring = raw_[:, :].rearrange("p (s n) -> p s n", s=RING)
        w_hi = whi_[:, :].rearrange("p (s n) -> p s n", s=HI_RING)
        w_lo = wlo_[:, :].rearrange("p (s n) -> p s n", s=RING)
        PS = ctx.enter_context(nc.psum_tensor("PS", [P, 8, 512], F32))

        def col(name):
            return colt[:, cs[name][0]:cs[name][1]]

        def row(name):
            return rowt[:, rs[name][0]:rs[name][1]]

        def tab(name, parts=P):
            return tabt[0:parts, ts[name][0]:ts[name][1]]

        ident = tab("ident")
        def pair_of(t, n, k):
            return tuple(a[:, 0:k * n].rearrange("p (k t) -> p k t", k=k) for a in t)

        hT = {4: pair_of((xhi_, xlo_), 512, KD), 2: pair_of((xhi_, xlo_), 256, KD)}
        xn = xn_[:, :].rearrange("p (t d) -> p t d", t=4)
        big = lambda a, n: BIG[:, a:a + n]
        bigr = lambda a, n: BIGR[:, a:a + n]
        z0 = big(0, 4 * EV_IN).rearrange("p (t c) -> p t c", t=4)
        v = {"z": z0, "y4": xn}
        v["dqT"] = big(7936, 2048).rearrange("p (h t) -> p h t", h=4)
        v["dkT"] = big(9984, 2048).rearrange("p (h t) -> p h t", h=4)
        v["qnT"], v["knT"] = v["dqT"], v["dkT"]
        v["qrT"] = free_b[:, 2048:4096].rearrange("p (h t) -> p h t", h=4)
        v["krT"] = free_a[:, 2048:2560]
        cT = pair_of((bigr(7936, 1536), bigr(9984, 1536)), 512, 3)
        q_l0 = z0[:, :, 0:768]
        v["kv"] = z0[:, :, 768:1792]
        prob4 = free_a[:, 0:2048].rearrange("p (b i k) -> p b i k", b=2, i=2)
        mix4 = free_a[:, 2048:3072].rearrange("p (b k) -> p b k", b=2)
        probT4 = free_a[:, 3072:4096].rearrange("p (b k) -> p b k", b=2)
        squares = free_b
        nq = big(0, 2048).rearrange("p (t c) -> p t c", t=2)
        nk_ = big(2048, 4096).rearrange("p (t c) -> p t c", t=4)
        v["nv"] = big(6144, 4096).rearrange("p (t c) -> p t c", t=4)
        v["nqT"] = big(10240, 2048).rearrange("p (h t) -> p h t", h=8)
        v["nkT"] = free_a[:, :].rearrange("p (h t) -> p h t", h=8)
        v["rel"] = [free_b[:, :].rearrange("p (t h k) -> p t h k", t=2, h=NA_H // 2),
                    big(2048, 4096).rearrange("p (t h k) -> p t h k", t=2, h=NA_H // 2)]
        prob_na = X[:, 2, :].rearrange("p (b i k) -> p b i k", b=2, i=1)
        probT_na = X[:, 3, :].rearrange("p (b k) -> p b k", b=2)
        units = attention_units(v)
        mqkT = big(0, 4096).rearrange("p (c t) -> p c t", c=16)
        rg = big(0, 4096).rearrange("p (t c) -> p t c", t=2)
        rqkT = big(4096, 4096).rearrange("p (c t) -> p c t", c=16)
        rv = big(8192, 4096).rearrange("p (t c) -> p t c", t=2)
        mv = free_a[:, 2048:4096].rearrange("p (t c) -> p t c", t=2)
        mo = free_b[:, 2048:4096].rearrange("p (t c) -> p t c", t=2)
        gm, gr = X[:, 2:4, :], xn[:, 2:4, :]
        hm = [xn[:, t, :] for t in range(2)]
        hr = [free_a[:, 2048:4096], free_b[:, 2048:4096]]
        ymT = pair_of((bigr(4096, 2048), bigr(6144, 2048)), 256, 8)
        yrT = pair_of((bigr(0, 4096), bigr(8192, 4096)), 256, 16)
        merged = SCR[:, :].rearrange("p (t c) -> p t c", t=2)
        ffT = {l: pair_of((bigr(0, k * n), bigr(k * n, k * n)), n, k) for l, n, k in ((0, 512, 8), (1, 256, 22))}
        ff2T = pair_of((bigr(0, 4096), bigr(4096, 4096)), 256, 16)
        pT2 = (bigr(0, 512), bigr(512, 512))

        tab_in, x_in, rel_in, wgate_in = ev("tab_in"), ev("x_in"), [ev("rel_in0"), ev("rel_in1")], ev("wgate_in")
        modb_in, nrows_in, pT_in = ev("modb_in"), ev("nrows_in"), ev("pT_in")
        w_in = [ev(f"w_in{i}") for i in range(RING)]
        bias_in = [ev(f"bias_in{i}") for i in range(2)]
        hi_ready, lo_ready = ev("hi_ready"), ev("lo_ready")
        shifted, pT_ready, wgate_ready = ev("shifted"), ev("pT_ready"), ev("wgate_ready")
        out_done = ev("out_done")
        vec_chain, act_chain = ev("vec_chain"), ev("act_chain")
        projected = ev("projected")
        stored = ev("stored")
        acted = ev("acted")
        turned = ev("turned")
        copied_v, copied_s = ev("copied_v"), ev("copied_s")
        x_ready, sums_ready, root_ready, normed = ev("x_ready"), ev("sums_ready"), ev("root_ready"), ev("normed")
        cond_ready, mod_rows, mod_turned = ev("cond_ready"), ev("mod_rows"), ev("mod_turned")
        mod_stored, mod_ready = ev("mod_stored"), ev("mod_ready")
        gate_diag, gates_bc = ev("gate_diag"), ev("gates_bc")
        lam_logit, lam_exp = ev("lam_logit"), ev("lam_exp")
        const_ready = ev("const_ready")
        pre_turn = ev("pre_turn")
        scored, max_ready, exp_ready, probs_ready = ev("scored"), ev("max_ready"), ev("exp_ready"), ev("probs_ready")
        probs_turned, probsT_ready, attended, y_out = ev("probs_turned"), ev("probsT_ready"), ev("attended"), ev("y_out")
        y_ready = ev("y_ready")
        unit_acted, qk_ready, qk_ready_act = ev("unit_acted"), ev("qk_ready"), ev("qk_ready_act")
        ff_acted = ev("ff_acted")
        gate_abs, gate_act, gate_scan, gate_turned, gate_cols = (ev("gate_abs"), ev("gate_act"), ev("gate_scan"),
                                                                ev("gate_turned"), ev("gate_cols"))
        u_bc, exp_arg = ev("u_bc"), ev("exp_arg")
        tok_acted = ev("tok_acted")
        hidden = ev("hidden")

        def gate_list(l):
            return [(kind, who, half) for kind in (2, 5) for who in range(2 - l) for half in range(2)]

        def gate(l, kind, who):
            n = gate_list(l).index((kind, who, 0))
            return G[:, n * 512:n * 512 + 1024]

        def copy_plan():
            plan_ = {}

            def add(key, nb, tiles, dst, width=P, kind="plain"):
                plan_[key] = (nb, tiles, width, dst, kind)

            def parts(pair):
                return lambda b: (pair[0][:, b, :], pair[1][:, b, :])
            for l, tiles in ((0, 4), (1, 4)):
                add(("mix", l), 8, tiles, parts(hT[4]), kind=("mod", 0))
            add(("ffn", 0), 8, 4, parts(hT[4]), kind=("mod", 3))
            add(("ffn", 1), 8, 2, parts(hT[2]), kind=("mod", 3))
            add("daq", 4, 4, lambda b: v["dqT"][:, b, :])
            add("dak", 4, 4, lambda b: v["dkT"][:, b, :])
            add("mlac", 3, 4, parts(cT), kind="parts")
            add("mlakr", 1, 4, lambda b: v["krT"][0:64, :], 64)
            add("qn", 4, 4, lambda b: v["qnT"][:, b, :])
            add("qr", 4, 4, lambda b: v["qrT"][0:64, b, :], 64)
            add("kn", 4, 4, lambda b: v["knT"][:, b, :])
            add("y0", 8, 4, parts(hT[4]), kind="parts")
            add("naq", 8, 2, lambda b: v["nqT"][:, b, :])
            add("nak", 8, 4, lambda b: v["nkT"][:, b, :])
            add("y1", 8, 2, parts(hT[2]), kind="parts")
            for l in range(2):
                for k in ("n1", "n2", "n3"):
                    add((k, l), 8, 2, parts(hT[2]), kind=("gain", k, l))
                add(("ym", l), 8, 2, parts(ymT), kind="parts")
                add(("yr", l), 16, 2, parts(yrT), kind="parts")
                add(("mg", l), 8, 2, parts(hT[2]), kind="parts")
            return plan_

        copies = copy_plan()

        def gain_of(key, b):
            kind = copies[key][4]
            return col(kind[1])[:, kind[2] * 8 + b:kind[2] * 8 + b + 1]

        eps, neg_lam = small[:, 61:62], small[:, 62:63]

        block = ctx.enter_context(nc.Block())
        n_chunks = chunks_d.shape[0]

        @block.tensor
        def _(pe):
            reader = {}
            state = {"c": 0, "b": 0}
            split = []

            def claim(*banks):
                for b in banks:
                    if b in reader:
                        pe.wait_ge(*reader.pop(b))

            def take_raw(st, l):
                c = state["c"]
                state["c"] += 1
                plan.setdefault(("first chunk", st, l), c)
                pe.wait_ge(*w_in[c % RING].after(c))
                return c, ring[:, c % RING, :].rearrange("p (k n) -> p k n", k=KC)

            def take_chunk(st, l, k_tiles=KC):
                c = state["c"]
                state["c"] += 1
                plan.setdefault(("first chunk", st, l), c)
                split.append(c)
                pe.wait_ge(*lo_ready.after(c))
                n = CHUNK // k_tiles
                return c, tuple(a.rearrange("p (k n) -> p k n", k=k_tiles) for a in (w_hi[:, c % HI_RING, :], w_lo[:, c % RING, :]))

            def used(c):
                projected.alias("used", c)

            def ends(mm, c, st, l, j, g=0):
                mm.then_inc(*projected.now(st, l, j, g))
                plan[("last chunk", st, l, j)] = c

            def product(o, lhs, rhs, start, stop, group=False):
                more = dict(skip_group_check=True) if group else {}
                pe.matmul(o, lhs[0], rhs[0], start=start, stop=False, **more)
                pe.matmul(o, lhs[0], rhs[1], start=False, stop=False, **more)
                return pe.matmul(o, lhs[1], rhs[0], start=False, stop=stop, **more)

            def tokens(pair):
                return lambda kt, t: tuple(a[:, kt, t * P:(t + 1) * P] for a in pair)

            def project_tok(st, l, n, k_tiles, lhs, groups=1, freed=stored, n0=0, biased=False):
                for j in range(n0, n0 + n):
                    if biased:
                        plan[("bias", state["c"])] = state["b"]
                        state["b"] += 1
                    for kg in range(-(-k_tiles // KC)):
                        c, w = take_chunk(st, l)
                        for g in range(groups):
                            pair = (j * groups + g) % 2
                            if kg == 0:
                                claim(2 * pair, 2 * pair + 1)
                            for t in range(2):
                                for kt in range(KC * kg, min(KC * kg + KC, k_tiles)):
                                    mm = product(PS[:, 2 * pair + t, :], lhs(kt, 2 * g + t),
                                                 [a[:, kt - KC * kg, :] for a in w], kt == 0, kt == k_tiles - 1)
                            if kg == (k_tiles - 1) // KC:
                                ends(mm, c, st, l, j, g)
                                reader[2 * pair] = reader[2 * pair + 1] = freed.after(st, l, j, g)
                            elif g == groups - 1:
                                mm.then_inc(*projected.now(("chunk", c)))
                        used(c)

            def project_feat(st, l, n, rhs, groups=1, freed=stored, n0=0):
                for j in range(n0, n0 + n):
                    for kg in range(2):
                        c, w = take_chunk(st, l)
                        for g in range(groups):
                            pair = (j * groups + g) % 2
                            if kg == 0:
                                claim(2 * pair, 2 * pair + 1)
                            for s in range(4):
                                for kt in range(KC * kg, KC * kg + KC):
                                    mm = product(PS[:, 2 * pair + s // 2, (s % 2) * 256:(s % 2) * 256 + 256],
                                                 [a[:, kt - KC * kg, s * P:(s + 1) * P] for a in w],
                                                 [a[:, kt, g * 256:g * 256 + 256] for a in rhs],
                                                 kt == 0 and s % 2 == 0, kt == KD - 1, True)
                            if kg == 1:
                                ends(mm, c, st, l, j, g)
                                reader[2 * pair] = reader[2 * pair + 1] = freed.after(st, l, j, g)
                            elif g == groups - 1:
                                mm.then_inc(*projected.now(("chunk", c)))
                        used(c)

            def turn(key, nb, tiles, src, width=P, ready=None):
                kind = copies[key][4]
                for b in range(nb):
                    claim(4 + b % 4)
                    for t in range(tiles):
                        if ready and b == 0:
                            pe.wait_ge(*ready(t))
                        mm = pe.transpose(PS[0:width, 4 + b % 4, t * P:(t + 1) * P], src(b, t), ident)
                    mm.then_inc(*turned.now(key, b))
                    if kind == "plain":
                        reader[4 + b % 4] = (copied_s if b % 2 else copied_v).after(key, b)
                    elif kind[0] == "mod":
                        reader[4 + b % 4] = shifted.after(key, b)
                    else:
                        reader[4 + b % 4] = copied_v.after(key, b)

            def await_copies(key, nb):
                if copies[key][4] != "plain":
                    pe.wait_ge(*copied_v.after(key, nb - 1))
                    return
                pe.wait_ge(*copied_v.after(key, (nb - 1) // 2 * 2))
                if nb > 1:
                    pe.wait_ge(*copied_s.after(key, nb // 2 * 2 - 1))

            def norm(key, tiles):
                turn(key, KD, tiles, lambda b, t: xn[:, t, b * P:(b + 1) * P], ready=lambda t: normed.after(key, t))
                await_copies(key, KD)

            def attend(ph, prob, probT):
                us = units[ph]

                def scores(u):
                    d = us[u]
                    s = 4 + 2 * (u % 2)
                    claim(s, s + 1)
                    for i, mats in enumerate(d["scores"]):
                        for m, (a, b) in enumerate(mats):
                            mm = pe.matmul(PS[:, s + i, 0:d["nk"]], a, b, start=m == 0, stop=m == len(mats) - 1)
                    mm.then_inc(*scored.now(ph, u))
                    reader[s] = reader[s + 1] = exp_ready.after(ph, u)

                def turn_probs(u):
                    pe.wait_ge(*(probs_ready if ph == "da" else exp_ready).after(ph, u))
                    claim(u % 2)
                    for j in range(us[u]["nk"] // P):
                        mm = pe.transpose(PS[:, u % 2, j * P:(j + 1) * P], prob(u)[:, j * P:(j + 1) * P], ident)
                    mm.then_inc(*probs_turned.now(ph, u))
                    reader[u % 2] = probsT_ready.after(ph, u)

                def values(u):
                    d = us[u]
                    pe.wait_ge(*probsT_ready.after(ph, u))
                    claim(2 + u % 2)
                    n = d["nk"] // P
                    for j in range(n):
                        mm = pe.matmul(PS[:, 2 + u % 2, 0:d["dv"]], probT[:, u % 2, j * P:(j + 1) * P], d["value"][j],
                                       start=j == 0, stop=j == n - 1)
                    mm.then_inc(*attended.now(ph, u))
                    reader[2 + u % 2] = y_out.after(ph, u)

                scores(0)
                for u in range(len(us)):
                    if u + 1 < len(us):
                        scores(u + 1)
                    if u >= 1:
                        values(u - 1)
                    turn_probs(u)
                values(len(us) - 1)

            def modulation(l, part):
                if l == 0:
                    pe.wait_ge(*cond_ready.after())
                cond = small[:, 0:16].rearrange("p (k c) -> p k c", c=2)

                def turn_rows(j):
                    pe.wait_ge(*mod_rows.after(l, j))
                    for s in range(4):
                        at = 8 * j + 2 * s
                        mm = pe.transpose(PS[:, 4, at:at + 2], SCR[0:2, (j % 4) * 512 + s * P:(j % 4) * 512 + s * P + P],
                                          ident[0:2, 0:2])
                    mm.then_inc(*mod_turned.now(l, j))

                j0 = sum(MOD_PARTS[l][:part])
                claim(4)
                for j in range(j0, j0 + MOD_PARTS[l][part]):
                    claim(j % 4)
                    for kg in range(2):
                        c, w = take_raw("mod", l)
                        for kt in range(4):
                            mm = pe.matmul(PS[0:2, j % 4, :], cond[:, 4 * kg + kt, :], w[:, kt, :],
                                           start=kg == 0 and kt == 0, stop=kg == 1 and kt == 3)
                        mm.then_inc(*projected.now("mod", l, j, kg))
                        used(c)
                    reader[j % 4] = mod_rows.after(l, j)
                    if j > j0:
                        turn_rows(j - 1)
                turn_rows(j)
                reader[4] = mod_stored.after(l, part)

            def gates(l):
                for n in range(len(gate_list(l))):
                    b = 5 + n % 3
                    pe.wait_ge(*gate_diag.after(l, n))
                    claim(b)
                    pe.matmul(PS[:, b, :], tab("ones"), G[:, n * 512:(n + 1) * 512],
                              start=True, stop=True).then_inc(*gates_bc.now(l, n))
                    reader[b] = acted.after("gates", l, n)

            def even_attention():
                gates(0)
                modulation(1, 0)
                pe.wait_ge(*pre_turn.after("da"))
                turn("daq", 4, 4, lambda b, t: z0[:, t, b * P:(b + 1) * P])
                turn("dak", 4, 4, lambda b, t: z0[:, t, 512 + b * P:512 + (b + 1) * P])
                await_copies("daq", 4)
                await_copies("dak", 4)
                attend("da", lambda u: mix4[:, u % 2, :], probT4)
                modulation(1, 1)
                pe.wait_ge(*pre_turn.after("mla_c"))
                turn("mlac", 3, 4, lambda b, t: z0[:, t, 1536 + b * P:1536 + (b + 1) * P])
                turn("mlakr", 1, 4, lambda b, t: z0[:, t, 1920:1984], width=64)
                await_copies("mlac", 3)
                await_copies("mlakr", 1)
                for st, first, k_tiles, width in (("uq", 0, 2, 384), ("ukv", 2, 1, 512)):
                    c, w = take_chunk(st, 0, 1)
                    for t in range(4):
                        pair = t % 2
                        claim(2 * pair, 2 * pair + 1)
                        for half in range(2):
                            for kt in range(k_tiles):
                                at = kt * 2 * width + half * width
                                mm = product(PS[:, 2 * pair + half, 0:width], tokens(cT)(first + kt, t),
                                             [a[:, 0, at:at + width] for a in w], kt == 0, kt == k_tiles - 1)
                        ends(mm, c, st, 0, t)
                        reader[2 * pair] = reader[2 * pair + 1] = stored.after(st, 0, t, 0)
                    used(c)
                modulation(1, 2)
                pe.wait_ge(*pre_turn.after("mla_q"))
                turn("qn", 4, 4, lambda b, t: q_l0[:, t, b * 192:b * 192 + 128])
                turn("qr", 4, 4, lambda b, t: q_l0[:, t, b * 192 + 128:b * 192 + 192], width=64)
                turn("kn", 4, 4, lambda b, t: v["kv"][:, t, b * 256:b * 256 + 128])
                for k in ("qn", "qr", "kn"):
                    await_copies(k, 4)
                attend("mla", lambda u: prob4[:, u % 2, 0, :], probT4)
                modulation(1, 3)

            def swiglu(l, tiles):
                g = tiles // 2
                norm(("ffn", l), tiles)
                n0 = 0
                for part, n in enumerate(FF_PARTS[l]):
                    project_feat("ffn_in", l, n, hT[tiles], g, n0=n0)
                    n0 += n
                    pe.wait_ge(*stored.after("hidden", l, n0 - 1, g - 1))
                    project_tok("ffn_out", l, 2, 2 * n, tokens(ffT[l]), g, n0=2 * part)

            pe.wait_ge(tab_in.sem, 16 * 3)
            modulation(0, 0)
            norm(("mix", 0), 4)
            project_tok("ev_in", 0, 4, KD, tokens(hT[4]), 2)
            even_attention()
            turn("y0", KD, 4, lambda b, t: xn[:, t, b * P:(b + 1) * P], ready=lambda t: y_ready.after("ev", 0))
            await_copies("y0", KD)
            project_tok("w_out", 0, 2, KD, tokens(hT[4]), 2)
            swiglu(0, 4)
            norm(("mix", 1), 4)
            project_tok("od_q", 1, 2, KD, tokens(hT[4]), 1)
            project_tok("od_kv", 1, 4, KD, tokens(hT[4]), 2)
            gates(1)
            pe.wait_ge(*pre_turn.after("na"))
            turn("naq", 8, 2, lambda b, t: nq[:, t, b * P:(b + 1) * P])
            turn("nak", 8, 4, lambda b, t: nk_[:, t, b * P:(b + 1) * P])
            await_copies("naq", 8)
            await_copies("nak", 8)
            attend("na", lambda u: prob_na[:, u % 2, 0, :], probT_na)
            turn("y1", KD, 2, lambda b, t: xn[:, t, b * P:(b + 1) * P], ready=lambda t: y_out.after("na", 31))
            await_copies("y1", KD)
            project_tok("w_out", 1, 2, KD, tokens(hT[2]))
            swiglu(1, 2)

            def scores_pair(l, kind, h, qkT):
                b = 4 if kind == "m" else 4 + h % 2
                claim(b)
                for s in range(2):
                    cols = slice(0, 256) if s == 0 else slice(256, 384)
                    for j in range(2):
                        mm = pe.matmul(PS[:, b, cols], qkT[:, 8 + 2 * h + j, s * P:(s + 1) * P],
                                       qkT[:, 2 * h + j, s * P:256], start=j == 0, stop=j == 1)
                mm.then_inc(*scored.now(kind, l, h))
                reader[b] = probs_ready.after(kind, l, h)
                if kind == "m":
                    claim(5)
                    pe.matmul(PS[:, 5, 0:256], tab("sel_h", 4)[:, h * P:(h + 1) * P], gt[:, 3, :],
                              start=True, stop=True).then_inc(*u_bc.now(l, h))
                    reader[5] = exp_arg.after(l, h)

            def values_pair(l, kind, h, val, dv):
                pe.wait_ge(*probs_ready.after(kind, l, h))
                pb = SCR[:, 384 * (h % 2):384 * (h % 2) + 384]
                claim(6, 7)
                for t in range(2):
                    blocks = [pb[:, 0:128]] if t == 0 else [pb[:, 128:256], pb[:, 256:384]]
                    for s, lhs in enumerate(blocks):
                        mm = pe.matmul(PS[:, 6 + t, 0:dv], lhs, val[:, s, h * dv:(h + 1) * dv],
                                       start=s == 0, stop=s == len(blocks) - 1)
                    if kind == "m":
                        for s, lhs in enumerate(blocks):
                            mm = pe.matmul(PS[:, 6 + t, 256:257], lhs, small[:, 60:61],
                                           start=s == 0, stop=s == len(blocks) - 1)
                mm.then_inc(*attended.now(kind, l, h))
                reader[6] = reader[7] = y_out.after(kind, l, h)

            for l in range(2):
                lhs = tokens(hT[2])
                norm(("n1", l), 2)
                if l == 0:
                    pe.wait_ge(*wgate_ready.after())
                claim(4)
                for gate in range(2):
                    for kt in range(KD):
                        at = (l * KD + kt) * 8 + 4 * gate
                        mm = product(PS[0:4, 4, gate * 256:gate * 256 + 256], (wgh[:, at:at + 4], wgl[:, at:at + 4]),
                                     [a[:, kt, :] for a in hT[2]], kt == 0, kt == KD - 1)
                mm.then_inc(*projected.now("gates", l, 0, 0))
                reader[4] = gate_abs.after(l)
                project_feat("mqk", l, 4, hT[2], freed=unit_acted)
                pe.wait_ge(*gate_scan.after(l))
                claim(5)
                for i in range(2):
                    for t in range(2):
                        mm = pe.transpose(PS[:, 5, (2 * i + t) * 4:(2 * i + t) * 4 + 4],
                                          gt[:, 4 * i, t * P:(t + 1) * P], ident[0:4, 0:4])
                mm.then_inc(*gate_turned.now(l))
                reader[5] = gate_cols.after(l)
                project_tok("mv", l, 2, KD, lhs, biased=True)
                project_tok("mo", l, 2, KD, lhs, biased=True)
                project_feat("rqk", l, 4, hT[2], freed=unit_acted)
                pe.wait_ge(*qk_ready_act.after("m", l, 3))
                for h in range(R_H):
                    scores_pair(l, "m", h, mqkT)
                    project_tok("rv", l, 1, KD, lhs, n0=h, biased=True)
                    if h >= 1:
                        values_pair(l, "m", h - 1, mv, 256)
                project_tok("rg", l, 1, KD, lhs, biased=True)
                values_pair(l, "m", R_H - 1, mv, 256)
                project_tok("rg", l, 3, KD, lhs, n0=1, biased=True)
                pe.wait_ge(*qk_ready.after("rqk", l, 3, 0))
                for h in range(R_H):
                    scores_pair(l, "r", h, rqkT)
                    project_tok("gm" if h < 2 else "gr", l, 1, KD, lhs, n0=h % 2, biased=True)
                    if h >= 1:
                        values_pair(l, "r", h - 1, rv, 512)
                values_pair(l, "r", R_H - 1, rv, 512)
                turn(("ym", l), 8, 2, lambda b, t: hm[t][:, b * P:(b + 1) * P], ready=lambda t: y_ready.after("ym", l))
                await_copies(("ym", l), 8)
                project_tok("w_bm", l, 2, KD, tokens(ymT))
                turn(("yr", l), 16, 2, lambda b, t: hr[t][:, b * P:(b + 1) * P], ready=lambda t: y_ready.after("yr", l))
                await_copies(("yr", l), 16)
                project_tok("w_br", l, 2, 16, tokens(yrT))
                turn(("mg", l), 8, 2, lambda b, t: merged[:, t, b * P:(b + 1) * P],
                     ready=lambda t: stored.after("w_br", l, 1, 0))
                await_copies(("mg", l), 8)
                project_tok("w_out2", l, 2, KD, lhs, freed=x_ready)
                norm(("n2", l), 2)
                for part in range(2):
                    project_feat("ff1", l, 4, hT[2], freed=ff_acted, n0=4 * part)
                    pe.wait_ge(*hidden.after("ff1", l, 4 * part + 3, 0))
                    for nb in range(2):
                        if part == 1:
                            plan[("bias", state["c"])] = state["b"]
                            state["b"] += 1
                        for kg in range(4):
                            c, w = take_chunk("ff2", l)
                            if part == 0 and kg == 0:
                                claim(4 + 2 * nb, 5 + 2 * nb)
                            for t in range(2):
                                for kt in range(KC * kg, KC * kg + KC):
                                    mm = product(PS[:, 4 + 2 * nb + t, :], tokens(ff2T)(kt, t),
                                                 [a[:, kt - KC * kg, :] for a in w],
                                                 part == 0 and kt == 0, part == 1 and kt == 15)
                            if part == 1 and kg == 3:
                                ends(mm, c, "ff2", l, nb)
                                reader[4 + 2 * nb] = reader[5 + 2 * nb] = stored.after("ff2", l, nb, 0)
                            else:
                                mm.then_inc(*projected.now(("chunk", c)))
                            used(c)
                norm(("n3", l), 2)
                project_tok("pe_g", l, 2, KD, lhs, freed=tok_acted)
                pe.wait_ge(*pT_ready.after(l))
                c, w = take_chunk("w_pe", l, 2)
                for j in range(2):
                    claim(2 * j, 2 * j + 1)
                    for t in range(2):
                        for kt in range(2):
                            at = kt * 256 + t * P
                            mm = product(PS[:, 2 * j + t, :], [a[:, at:at + P] for a in pT2],
                                         [a[:, kt, j * 512:(j + 1) * 512] for a in w], kt == 0, kt == 1)
                    ends(mm, c, "w_pe", l, j)
                    reader[2 * j] = reader[2 * j + 1] = stored.after("w_pe", l, j, 0)
                used(c)
            plan["split chunks"] = split

        @block.sync
        def _(sp):
            def first(st, l):
                return plan.get(("first chunk", st, l), -9)

            sp.dma_start(colt[:, :], cols_d).then_inc(*tab_in.now(by=16))
            sp.dma_start(tabt[:, :], tabs_d).then_inc(*tab_in.now(by=16))
            sp.dma_start(rowt[:, :], rows_d.partition_broadcast(P)).then_inc(*tab_in.now(by=16))
            sp.dma_start(mod_bias, modb_d).then_inc(*modb_in.now(by=16))
            n_bias = 0
            for c in range(n_chunks):
                if c == 4:
                    sp.dma_start(X[:, 0:2, :], x_d).then_inc(*x_in.now(by=16))
                    sp.dma_start(X[:, 2:4, :], ctx_d).then_inc(*x_in.now(by=16))
                    sp.dma_start(wgate[:, :], wgate_d).then_inc(*wgate_in.now(by=16))
                    sp.dma_start(bgate[:, :, :], bgate_d).then_inc(*wgate_in.now(by=16))
                if c >= RING:
                    sp.wait_ge(*projected.after("used", c - RING))
                if c == first("w_out", 1) + AHEAD:
                    for part in range(2):
                        if part == 0:
                            sp.wait_ge(*projected.after("od_kv", 1, 3, 1))
                        else:
                            sp.wait_ge(*turned.after("nak", 7))
                            sp.wait_ge(*copied_v.after("nak", 6))
                            sp.wait_ge(*copied_s.after("nak", 7))
                        heads = slice(part * 8, part * 8 + 8)
                        for t in range(TX):
                            for half in range(2):
                                row0 = NA_KH - 1 - (2 * t + half)
                                src = rel_d[:, heads, row0:row0 + NA_ROWS, :].rearrange("q h i c -> q h (i c)")
                                sp.dma_start(v["rel"][part][64 * half:64 * half + 64, t], src
                                             ).then_inc(*rel_in[part].now(by=16))
                for l in range(2):
                    if c == first("mqk", l) + RING:
                        sp.wait_ge(*(x_ready.after("ffn_out", 1) if l == 0 else x_ready.after("pe", 0)))
                        sp.dma_start(G[:, 0:3072] if l else G[:, :],
                                     nrows_d[l:l + 1, 0:3072].partition_broadcast(P) if l else
                                     nrows_d[0:1, :].partition_broadcast(P)).then_inc(*nrows_in.now(l, by=16))
                        sp.dma_start(pT[:, :], pT_d[:, l, :]).then_inc(*pT_in.now(l, by=16))
                sp.dma_start(ring[:, c % RING, :], chunks_d[c]).then_inc(*w_in[c % RING].now(c, by=16))
                if ("bias", c - 2) in plan:
                    b = plan[("bias", c - 2)]
                    if b >= 2:
                        sp.wait_ge(*stored.after("bias", b - 2))
                    sp.dma_start(bias_ring[:, b % 2, :], brows_d[b:b + 1, :].partition_broadcast(P)
                                 ).then_inc(*bias_in[b % 2].now(b, by=16))
            sp.wait_ge(*x_ready.after("out"))
            sp.dma_start(out, xn[:, 0:2, :]).then_inc(*out_done.now(by=16))
            sp.wait_ge(out_done.sem, out_done.count)

        @block.gpsimd
        def _(pool):
            def diagonals(l):
                pool.wait_ge(*(mod_ready.after(0) if l == 0 else x_ready.after("ffn_out", 0)))
                for n, (kind, who, half) in enumerate(gate_list(l)):
                    k = kind * 8 + 4 * half
                    columns = modc[l][:, k:k + 4, who:who + 1].to_broadcast([P, 4, P])
                    pool.tensor_tensor(G[:, n * 512:(n + 1) * 512].rearrange("p (k d) -> p k d", k=4),
                                       ident.unsqueeze(1).to_broadcast([P, 4, P]), columns,
                                       ALU.mult).then_inc(*gate_diag.now(l, n))

            for c in plan["split chunks"]:
                if c == plan.get(("first chunk", "uq", 0)):
                    diagonals(0)
                if c == plan.get(("first chunk", "w_out", 1)):
                    diagonals(1)
                pool.wait_ge(*hi_ready.after(c))
                pool.tensor_tensor(w_lo[:, c % RING, :], ring[:, c % RING, :], w_hi[:, c % HI_RING, :].bitcast(F32),
                                   ALU.subtract).then_inc(*lo_ready.now(c))

        @block.scalar
        def _(act):
            def link(ins, e=act_chain, *key):
                ins.then_inc(*e.now(*key))
                act.wait_ge(e.sem, e.count)

            chunks_left = list(plan["split chunks"])

            def split_to(c):
                while c is not None and chunks_left and chunks_left[0] <= c:
                    n = chunks_left.pop(0)
                    act.wait_ge(*w_in[n % RING].after(n))
                    if n >= HI_RING:
                        act.wait_ge(*projected.after("used", n - HI_RING))
                    act.activation(w_hi[:, n % HI_RING, :], ring[:, n % RING, :], ACT.Copy).then_inc(*hi_ready.now(n))

            def split_for(st, l, j):
                c = plan.get(("last chunk", st, l, j))
                split_to(c if c is None else c + AHEAD)

            def copy_turned(key):
                nb, tiles, width, dst, kind = copies[key]
                for b in range(nb):
                    src = PS[0:width, 4 + b % 4, 0:tiles * P]
                    if kind == "plain":
                        if b % 2:
                            act.wait_ge(*turned.after(key, b))
                            act.activation(dst(b), src, ACT.Copy).then_inc(*copied_s.now(key, b))
                    elif kind == "parts":
                        act.wait_ge(*turned.after(key, b))
                        act.activation(dst(b)[0], src, ACT.Copy).then_inc(*copied_s.now(key, b))
                    elif kind[0] == "gain":
                        act.wait_ge(*turned.after(key, b))
                        act.activation(dst(b)[0], src, ACT.Copy, scale=gain_of(key, b)).then_inc(*copied_s.now(key, b))
                    else:
                        act.wait_ge(*shifted.after(key, b))
                        act.activation(dst(b)[0], SCR[:, 512 * (b % 4):512 * (b % 4) + tiles * P],
                                       ACT.Copy).then_inc(*copied_s.now(key, b))

            def norm(key, tiles, src_ready):
                if src_ready:
                    act.wait_ge(*src_ready)
                for t in range(tiles):
                    ins = act.activation(xn[:, t, :], X[:, t, :], ACT.Square, accum_out=stat[:, t:t + 1])
                    link(ins)
                link(act.activation(stat[:, 4:4 + tiles], stat[:, 0:tiles], ACT.Sqrt, bias=eps, scale=1.0 / D),
                     root_ready, key)
                if key != "out":
                    copy_turned(key)

            def root(key, n, d):
                act.wait_ge(*sums_ready.after(key))
                link(act.activation(stat[:, 64:64 + n], stat[:, 0:n], ACT.Sqrt, bias=eps, scale=1.0 / d),
                     root_ready, key)

            def attend(ph, prob, probT):
                us = units[ph]

                def exps(u):
                    d, s = us[u], 4 + 2 * (u % 2)
                    act.wait_ge(*max_ready.after(ph, u))
                    for i in range(len(d["scores"])):
                        ins = act.activation(prob[:, u % 2, i, 0:d["nk"]], PS[:, s + i, 0:d["nk"]], ACT.Exp,
                                             bias=stat[:, 192 + 4 * (u % 2) + i:193 + 4 * (u % 2) + i], scale=d["scale"],
                                             accum_out=stat[:, 200 + 2 * (u % 4) + i:201 + 2 * (u % 4) + i])
                    ins.then_inc(*exp_ready.now(ph, u))

                def copy_probs(u):
                    act.wait_ge(*probs_turned.after(ph, u))
                    act.activation(probT[:, u % 2, 0:us[u]["nk"]], PS[:, u % 2, 0:us[u]["nk"]],
                                   ACT.Copy).then_inc(*probsT_ready.now(ph, u))

                exps(0)
                for u in range(len(us)):
                    if u + 1 < len(us):
                        exps(u + 1)
                    copy_probs(u)

            def gates(l):
                for n in range(len(gate_list(l))):
                    act.wait_ge(*gates_bc.after(l, n))
                    act.activation(G[:, n * 512:(n + 1) * 512], PS[:, 5 + n % 3, :],
                                   ACT.Copy).then_inc(*acted.now("gates", l, n))

            def modulation(l, j0, n):
                for j in range(j0, j0 + n):
                    act.wait_ge(*projected.after("mod", l, j, 1))
                    if j >= 4:
                        act.wait_ge(*mod_turned.after(l, j - 4))
                    act.activation(SCR[0:2, (j % 4) * 512:(j % 4) * 512 + 512], PS[0:2, j % 4, :],
                                   ACT.Copy).then_inc(*mod_rows.now(l, j))

            def swiglu(l, tiles):
                norm(("ffn", l), tiles, x_ready.after("w_out", l))
                for j in range(11):
                    for g in range(tiles // 2):
                        pair = (j * (tiles // 2) + g) % 2
                        split_for("ffn_in", l, j)
                        act.wait_ge(*projected.after("ffn_in", l, j, g))
                        if j * (tiles // 2) + g >= 2:
                            jj, gg = divmod(j * (tiles // 2) + g - 2, tiles // 2)
                            act.wait_ge(*stored.after("hidden", l, jj, gg))
                        act.activation(SCR[:, pair * 512:pair * 512 + 512], PS[:, 2 * pair, :],
                                       ACT.Silu).then_inc(*unit_acted.now("ffn_in", l, j, g))

            act.wait_ge(tab_in.sem, 16 * 3)
            act.activation(small[:, 0:16], col("cond"), ACT.Silu).then_inc(*cond_ready.now())
            act.wait_ge(*lam_logit.after())
            act.activation(small[:, 20:22], small[:, 18:20], ACT.Exp).then_inc(*lam_exp.now())
            modulation(0, 0, 12)
            act.wait_ge(*const_ready.after())
            split_to(plan.get(("first chunk", "ev_in", 0), -AHEAD) + AHEAD - 1)
            norm(("mix", 0), 4, (x_in.sem, 32))
            split_for("ev_in", 0, 3)
            gates(0)
            root("da", 64, 64)
            modulation(1, 0, 3)
            copy_turned("daq")
            copy_turned("dak")
            attend("da", prob4, probT4)
            root("cq", 4, 256)
            root("ckv", 4, 128)
            modulation(1, 3, 2)
            root("kr", 4, 64)
            modulation(1, 5, 2)
            split_for("ukv", 0, 3)
            copy_turned("mlac")
            root("mlaq", 16, 192)
            modulation(1, 7, 2)
            root("mlak", 16, 128)
            modulation(1, 9, 1)
            copy_turned("qn")
            copy_turned("qr")
            copy_turned("kn")
            attend("mla", prob4, probT4)
            split_to(plan.get(("first chunk", "w_out", 0), -AHEAD) + AHEAD - 1)
            root("dao", 16, 128)
            modulation(1, 10, 2)
            copy_turned("y0")
            split_for("w_out", 0, 1)
            swiglu(0, 4)
            split_for("ffn_out", 0, 5)
            norm(("mix", 1), 4, x_ready.after("ffn_out", 0))
            split_for("od_q", 1, 1)
            root("naq", 32, 64)
            split_for("od_kv", 1, 1)
            root("nak", 64, 64)
            split_for("od_kv", 1, 3)
            gates(1)
            copy_turned("naq")
            copy_turned("nak")
            attend("na", prob_na, probT_na)
            copy_turned("y1")
            split_for("w_out", 1, 1)
            swiglu(1, 2)
            split_for("ffn_out", 1, 1)

            def in_place(st, l, n, buf, func, n0=0):
                for j in range(n0, n0 + n):
                    split_for(st, l, j)
                    act.wait_ge(*stored.after(st, l, j, 0))
                    act.activation(buf[:, :, j * 512:(j + 1) * 512], buf[:, :, j * 512:(j + 1) * 512],
                                   func).then_inc(*tok_acted.now(st, l, j, 0))

            for l in range(2):
                norm(("n1", l), 2, x_ready.after("ffn_out", 1) if l == 0 else x_ready.after("pe", 0))
                act.wait_ge(*gate_abs.after(l))
                link(act.activation(gt[:, 2, :], gt[:, 2, :], ACT.Exp, scale=-1.0))
                link(act.activation(gt[:, 2, :], gt[:, 2, :], ACT.Ln, bias=small[0:4, 60:61], scale=1.0), gate_act, l)
                conv_in = SCR[:, 0:1036].rearrange("p (s t) -> p s t", s=4)
                for j in range(4):
                    split_for("mqk", l, j)
                    act.wait_ge(*projected.after("mqk", l, j, 0))
                    act.wait_ge(*(qk_ready.after("mqk", l, j - 1, 0) if j else const_ready.after("pad", l)))
                    for s in range(4):
                        ins = act.activation(conv_in[:, s, 3:259],
                                             PS[:, 2 * (j % 2) + s // 2, (s % 2) * 256:(s % 2) * 256 + 256], ACT.Identity,
                                             bias=col("b_mqk")[:, l * 16 + j * 4 + s:l * 16 + j * 4 + s + 1])
                    ins.then_inc(*unit_acted.now("mqk", l, j, 0))
                    act.wait_ge(*qk_ready.after("mqk", l, j, 0))
                    act.activation(mqkT[:, 4 * j:4 * j + 4, :], mqkT[:, 4 * j:4 * j + 4, :],
                                   ACT.Silu).then_inc(*qk_ready_act.now("m", l, j))
                act.wait_ge(*gate_turned.after(l))
                act.activation(small[:, 32:40], PS[:, 5, 8:16], ACT.Exp, scale=-1.0)
                act.activation(small[:, 24:32], PS[:, 5, 0:8], ACT.Copy).then_inc(*gate_cols.now(l))
                in_place("mo", l, 2, mo, ACT.Sigmoid)
                rope_in = SCR[:, 0:1024].rearrange("p (s t) -> p s t", s=4)
                for j in range(4):
                    split_for("rqk", l, j)
                    act.wait_ge(*projected.after("rqk", l, j, 0))
                    act.wait_ge(*(qk_ready.after("rqk", l, j - 1, 0) if j else qk_ready.after("mqk", l, 3, 0)))
                    for s in range(4):
                        ins = act.activation(rope_in[:, s, :],
                                             PS[:, 2 * (j % 2) + s // 2, (s % 2) * 256:(s % 2) * 256 + 256], ACT.Identity,
                                             bias=col("b_rqk")[:, l * 16 + j * 4 + s:l * 16 + j * 4 + s + 1])
                    ins.then_inc(*unit_acted.now("rqk", l, j, 0))
                def root_of(k):
                    act.wait_ge(*sums_ready.after(k, l))
                    view = stat[:, 128:144].rearrange("p (n s) -> p n s", s=2)
                    link(act.activation(stat[:, 144:152], view[:, :, 1], ACT.Sqrt, bias=eps, scale=1.0), root_ready, k, l)

                for h in range(R_H):
                    if h:
                        split_for("rv", l, h - 1)
                    act.wait_ge(*exp_arg.after(l, h))
                    e = SCR[:, 768 + 384 * (h % 2):1152 + 384 * (h % 2)]
                    act.activation(e, e, ACT.Exp).then_inc(*exp_ready.now("m", l, h))
                in_place("rg", l, 1, rg, ACT.Silu)
                root_of("hm")
                in_place("rg", l, 3, rg, ACT.Silu, 1)
                in_place("gm", l, 2, gm, ACT.Sigmoid)
                in_place("gr", l, 2, gr, ACT.Sigmoid)
                copy_turned(("ym", l))
                root_of("hr")
                split_for("w_bm", l, 1)
                copy_turned(("yr", l))
                split_for("w_br", l, 1)
                copy_turned(("mg", l))
                split_for("w_out2", l, 1)
                norm(("n2", l), 2, x_ready.after("w_out2", l, 1, 0))
                for j in range(8):
                    pair = j % 2
                    split_for("ff1", l, j)
                    act.wait_ge(*projected.after("ff1", l, j, 0))
                    if j >= 2:
                        act.wait_ge(*hidden.after("ff1", l, j - 2, 0))
                    for s in range(4):
                        ins = act.activation(SCR[:, 1024 * pair + 256 * s:1024 * pair + 256 * s + 256],
                                             PS[:, 2 * pair + s // 2, (s % 2) * 256:(s % 2) * 256 + 256], ACT.Relu,
                                             bias=col("b_ff1")[:, l * 32 + j * 4 + s:l * 32 + j * 4 + s + 1])
                    ins.then_inc(*ff_acted.now("ff1", l, j, 0))
                split_for("ff2", l, 1)
                norm(("n3", l), 2, x_ready.after("ff2", l))
                for j in range(2):
                    split_for("pe_g", l, j)
                    act.wait_ge(*projected.after("pe_g", l, j, 0))
                    act.activation(gm[:, :, j * 512:(j + 1) * 512], PS[:, 2 * j:2 * j + 2, :],
                                   ACT.Sigmoid).then_inc(*tok_acted.now("pe_g", l, j, 0))
                split_for("w_pe", l, 1)
            split_to(n_chunks)
            norm("out", 2, x_ready.after("pe", 1))

        @block.vector
        def _(dve):
            def link(ins, e=vec_chain, *key):
                ins.then_inc(*e.now(*key))
                dve.wait_ge(e.sem, e.count)

            def copy_turned(key):
                nb, tiles, width, dst, kind = copies[key]

                def shift(b):
                    dve.wait_ge(*turned.after(key, b))
                    k, m = kind[1], modc[key[1]]
                    for i in range(tiles // 2):
                        at = 512 * (b % 4) + 256 * i
                        ins = dve.tensor_scalar(SCR[:, at:at + 256], PS[:, 4 + b % 4, 256 * i:256 * i + 256],
                                                m[:, (k + 1) * 8 + b, i:i + 1], m[:, k * 8 + b, i:i + 1],
                                                ALU.mult, ALU.add)
                    ins.then_inc(*shifted.now(key, b))

                for b in range(nb):
                    src = PS[0:width, 4 + b % 4, 0:tiles * P]
                    if kind == "plain":
                        if b % 2 == 0:
                            dve.wait_ge(*turned.after(key, b))
                            dve.tensor_copy(dst(b), src).then_inc(*copied_v.now(key, b))
                        continue
                    if kind[0] == "mod":
                        if b == 0:
                            shift(0)
                        if b + 1 < nb:
                            shift(b + 1)
                    dve.wait_ge(*copied_s.after(key, b))
                    hi, lo = dst(b)
                    if kind == "parts":
                        ins = dve.tensor_tensor(lo, src, hi.bitcast(F32), ALU.subtract)
                    elif kind[0] == "gain":
                        ins = dve.scalar_tensor_tensor(lo, src, gain_of(key, b), hi.bitcast(F32), ALU.mult, ALU.subtract)
                    else:
                        ins = dve.tensor_tensor(lo, SCR[:, 512 * (b % 4):512 * (b % 4) + tiles * P], hi.bitcast(F32),
                                                ALU.subtract)
                    ins.then_inc(*copied_v.now(key, b))

            def split(pair, src):
                link(dve.tensor_copy(pair[0], src))
                return dve.tensor_tensor(pair[1], src, pair[0].bitcast(F32), ALU.subtract)

            def norm(key, tiles):
                dve.wait_ge(*root_ready.after(key))
                link(dve.reciprocal(stat[:, 8:8 + tiles], stat[:, 4:4 + tiles]))
                for t in range(tiles):
                    dve.tensor_scalar(xn[:, t, :], X[:, t, :], stat[:, 8 + t:9 + t], None,
                                      ALU.mult).then_inc(*normed.now(key, t))
                if key != "out":
                    copy_turned(key)

            def bc(a, shape):
                while len(a.shape) < len(shape):
                    a = a.unsqueeze(1)
                return a.to_broadcast(shape)

            def group_rms(key, x4, sq, gains):
                _, t, g, d = x4.shape
                n = t * g
                sq4 = sq[:, 0:n * d].rearrange("p (t g d) -> p t g d", t=t, g=g)
                link(dve.tensor_tensor(sq4, x4, x4, ALU.mult))
                link(dve.tensor_reduce(stat[:, 0:n], sq[:, 0:n * d].rearrange("p (n d) -> p n d", d=d), AX_X, ALU.add),
                     sums_ready, key)
                dve.wait_ge(*root_ready.after(key))
                link(dve.reciprocal(stat[:, 128:128 + n], stat[:, 64:64 + n]))
                r4 = stat[:, 128:128 + n].rearrange("p (t g) -> p t g", t=t).unsqueeze(3).to_broadcast([P, t, g, d])
                link(dve.tensor_tensor(x4, x4, r4, ALU.mult))
                for lo, hi, gain in gains:
                    part = x4[:, :, lo:hi, :]
                    link(dve.tensor_tensor(part, part, bc(gain, [P, t, hi - lo, d]), ALU.mult))

            def rope(x5, t, tmp):
                g = x5.shape[1]
                cos = bc(tab("cos").rearrange("p (t r j) -> p t r j", t=2, r=2)[:, t], [P, g, 2, 16])
                sin = bc(tab("sin").rearrange("p (t r j) -> p t r j", t=2, r=2)[:, t], [P, g, 2, 16])
                a, b, c, d = (tmp[:, i * g * 32:(i + 1) * g * 32].rearrange("p (g r j) -> p g r j", g=g, r=2)
                              for i in range(4))
                x1, x2 = x5[:, :, :, 0, :], x5[:, :, :, 1, :]
                dve.tensor_tensor(a, x1, cos, ALU.mult)
                dve.tensor_tensor(b, x2, sin, ALU.mult)
                dve.tensor_tensor(c, x1, sin, ALU.mult)
                link(dve.tensor_tensor(d, x2, cos, ALU.mult))
                dve.tensor_tensor(x1, a, b, ALU.subtract)
                link(dve.tensor_tensor(x2, c, d, ALU.add))

            def halves(x3):
                return x3.rearrange("p g (r h j) -> p g r h j", r=2, h=2)

            def attend(ph, prob, mix):
                us = units[ph]

                def maxes(u):
                    d, s = us[u], 4 + 2 * (u % 2)
                    n = len(d["scores"])
                    if ph == "na" and u == len(us) // 2:
                        add_mask(1)
                    dve.wait_ge(*scored.after(ph, u))
                    if d["bias"] is not None:
                        link(dve.scalar_tensor_tensor(PS[:, s, 0:256], d["bias"], 1.0 / d["scale"], PS[:, s, 0:256],
                                                      ALU.mult, ALU.add))
                    m = stat[:, 208:208 + n]
                    link(dve.tensor_reduce(m, PS[:, s:s + n, 0:d["nk"]], AX_X, ALU.max))
                    o = 192 + 4 * (u % 2)
                    link(dve.tensor_scalar(stat[:, o:o + n], m, -d["scale"], None, ALU.mult), max_ready, ph, u)

                def norms(u):
                    d, o = us[u], 200 + 2 * (u % 4)
                    n, nk = len(d["scores"]), d["nk"]
                    if n == 1:
                        return
                    dve.wait_ge(*exp_ready.after(ph, u))
                    link(dve.reciprocal(stat[:, 212:212 + n], stat[:, o:o + n]))
                    p0 = prob[:, u % 2, 0, 0:nk]
                    link(dve.tensor_scalar(stat[:, 213:214], stat[:, 213:214], neg_lam, None, ALU.mult))
                    link(dve.tensor_scalar(p0, p0, stat[:, 212:213], None, ALU.mult))
                    link(dve.scalar_tensor_tensor(mix[:, u % 2, 0:nk], prob[:, u % 2, 1, 0:nk], stat[:, 213:214], p0,
                                                  ALU.mult, ALU.add), probs_ready, ph, u)

                def outs(u):
                    d = us[u]
                    if len(d["scores"]) == 2:
                        dve.wait_ge(*attended.after(ph, u))
                        dve.tensor_copy(d["out"], PS[:, 2 + u % 2, 0:d["dv"]]).then_inc(*y_out.now(ph, u))
                        return
                    o = 200 + 2 * (u % 4)
                    dve.wait_ge(*exp_ready.after(ph, u))
                    r = stat[:, 212 + u % 4:213 + u % 4]
                    link(dve.reciprocal(r, stat[:, o:o + 1]))
                    dve.wait_ge(*attended.after(ph, u))
                    dve.tensor_scalar(d["out"], PS[:, 2 + u % 2, 0:d["dv"]], r, None,
                                      ALU.mult).then_inc(*y_out.now(ph, u))

                maxes(0)
                for u in range(len(us)):
                    if u + 1 < len(us):
                        maxes(u + 1)
                    norms(u)
                    if u >= 1:
                        outs(u - 1)
                outs(len(us) - 1)

            def pair_view(pair):
                return PS[:, 2 * pair:2 * pair + 2, :]

            def modulation(l, part):
                if l == 0:
                    dve.wait_ge(*modb_in.after())
                j0 = sum(MOD_PARTS[l][:part])
                n = MOD_PARTS[l][part]
                dve.wait_ge(*mod_turned.after(l, j0 + n - 1))
                m = modc[l][:, 4 * j0:4 * (j0 + n), :]
                bias = mod_bias[:, l, 4 * j0:4 * (j0 + n)].unsqueeze(2).to_broadcast([P, 4 * n, 2])
                link(dve.tensor_tensor(m, PS[:, 4, 8 * j0:8 * (j0 + n)].rearrange("p (k c) -> p k c", c=2), bias, ALU.add),
                     mod_stored, l, part)
                if part + 1 < len(MOD_PARTS[l]):
                    return
                for kind, name in ((1, "mix_g"), (4, "ffn_g")):
                    m = modc[l][:, kind * 8:kind * 8 + 8, :]
                    g = col(name)[:, l * 8:l * 8 + 8].unsqueeze(2).to_broadcast([P, 8, 2])
                    link(dve.scalar_tensor_tensor(m, m, 1.0, g, ALU.add, ALU.mult),
                         *((mod_ready, l) if kind == 4 else (vec_chain,)))

            def residual(st, l, n, groups, gates, n0=0):
                for j in range(n0, n0 + n):
                    for g in range(groups):
                        pair = (j * groups + g) % 2
                        cols = slice((j % 2) * 512, (j % 2) * 512 + 512)
                        dve.wait_ge(*projected.after(st, l, j, g))
                        gt_ = bc(gates[g][:, cols], [P, 2, 512])
                        tmp = SCR[:, 1024:2048].rearrange("p (t n) -> p t n", t=2)
                        link(dve.tensor_tensor(tmp, pair_view(pair), gt_, ALU.mult), stored, st, l, j, g)
                        xs = X[:, 2 * g:2 * g + 2, cols]
                        link(dve.tensor_tensor(xs, xs, tmp, ALU.add), x_ready, st, l)

            def store(st, l, n, groups, dst, n0=0):
                for j in range(n0, n0 + n):
                    for g in range(groups):
                        pair = (j * groups + g) % 2
                        o = dst(j, g)
                        dve.wait_ge(*projected.after(st, l, j, g))
                        dve.tensor_copy(o, pair_view(pair)[:, :, 0:o.shape[2]]).then_inc(*stored.now(st, l, j, g))

            def swiglu(l, tiles):
                g_n = tiles // 2
                norm(("ffn", l), tiles)
                n0 = 0
                for part, n in enumerate(FF_PARTS[l]):
                    for j in range(n0, n0 + n):
                        for g in range(g_n):
                            pair = (j * g_n + g) % 2
                            dve.wait_ge(*unit_acted.after("ffn_in", l, j, g))
                            s = SCR[:, pair * 512:pair * 512 + 512]
                            link(dve.tensor_tensor(s, s, PS[:, 2 * pair + 1, :], ALU.mult), stored, "ffn_in", l, j, g)
                            k = 2 * (j - n0)
                            split([a[:, k:k + 2, g * 256:(g + 1) * 256] for a in ffT[l]],
                                  s.rearrange("p (s t) -> p s t", s=2)).then_inc(*stored.now("hidden", l, j, g))
                    n0 += n
                    residual("ffn_out", l, 2, g_n, [gate(l, 5, g) for g in range(g_n)], 2 * part)

            def add_mask(part):
                dve.wait_ge(*rel_in[part].after())
                rel = v["rel"][part].rearrange("p t h (i c) -> p (t h i) c", i=NA_ROWS)
                link(dve.tensor_tensor(rel, rel, bc(tab("na_mask"), [P, rel.shape[1], GRID_W]), ALU.add))

            dve.memset(small[:, 60:61], 1.0)
            link(dve.memset(eps, EPS), const_ready)
            dve.wait_ge(tab_in.sem, 16 * 3)
            link(dve.tensor_tensor(SCR[:, 0:128], row("lq"), row("lk"), ALU.mult))
            link(dve.tensor_reduce(small[:, 18:20], SCR[:, 0:128].rearrange("p (a d) -> p a d", a=2), AX_X, ALU.add),
                 lam_logit)
            dve.wait_ge(*lam_exp.after())
            link(dve.tensor_tensor(small[:, 22:23], small[:, 21:22], small[:, 20:21], ALU.subtract))
            link(dve.tensor_scalar(neg_lam, small[:, 22:23], -LAM_INIT, None, ALU.add))
            modulation(0, 0)
            norm(("mix", 0), 4)
            store("ev_in", 0, 4, 2, lambda j, g: z0[:, 2 * g:2 * g + 2, j * 512:min(j * 512 + 512, EV_IN)])
            dve.wait_ge(stored.sem, stored.count)
            qk = z0[:, :, 0:1024].rearrange("p t (g d) -> p t g d", d=64)
            group_rms("da", qk, squares, [(0, 8, row("da_q_g")), (8, 16, row("da_k_g"))])
            for t in range(TX):
                rope(halves(qk[:, t]), t, squares)
            link(dve.memset(small[:, 16:17], 0.0), pre_turn, "da")
            modulation(1, 0)
            copy_turned("daq")
            copy_turned("dak")
            attend("da", prob4, mix4)
            group_rms("cq", z0[:, :, 1536:1792].unsqueeze(2), squares, [(0, 1, row("mla_q_a_g"))])
            group_rms("ckv", z0[:, :, 1792:1920].unsqueeze(2), squares, [(0, 1, row("mla_kv_a_g"))])
            kr = z0[:, :, 1920:1984].unsqueeze(2)
            group_rms("kr", kr, squares, [(0, 1, row("mla_kr_g"))])
            for t in range(TX):
                rope(halves(kr[:, t]), t, squares)
            link(dve.memset(small[:, 16:17], 0.0), pre_turn, "mla_c")
            modulation(1, 1)
            copy_turned("mlac")
            copy_turned("mlakr")
            for st, dst, w in (("uq", q_l0, 384), ("ukv", v["kv"], 512)):
                for t in range(4):
                    dve.wait_ge(*projected.after(st, 0, t, 0))
                    dve.tensor_copy(dst[:, t, :].rearrange("p (s n) -> p s n", s=2),
                                    pair_view(t % 2)[:, :, 0:w]).then_inc(*stored.now(st, 0, t, 0))
            dve.wait_ge(stored.sem, stored.count)
            qh = q_l0.rearrange("p t (g d) -> p t g d", g=4)
            group_rms("mlaq", qh, squares, [(0, 4, row("mla_q_g"))])
            for t in range(TX):
                rope(halves(qh[:, t, :, 128:192]), t, squares)
            kh = v["kv"].rearrange("p t (g d) -> p t g d", g=4)[:, :, :, 0:128]
            group_rms("mlak", kh, squares, [(0, 4, row("mla_k_g"))])
            link(dve.memset(small[:, 16:17], 0.0), pre_turn, "mla_q")
            modulation(1, 2)
            for k in ("qn", "qr", "kn"):
                copy_turned(k)
            attend("mla", prob4, None)
            dve.wait_ge(y_out.sem, y_out.count)
            yd = xn[:, :, 0:512].rearrange("p t (g d) -> p t g d", g=4)
            group_rms("dao", yd, squares, [(0, 4, row("da_out_g"))])
            link(dve.tensor_scalar(xn[:, :, 0:512], xn[:, :, 0:512], 1.0 - LAM_INIT, None, ALU.mult), y_ready, "ev", 0)
            modulation(1, 3)
            copy_turned("y0")
            dve.wait_ge(*acted.after("gates", 0, 7))
            residual("w_out", 0, 2, 2, [gate(0, 2, 0), gate(0, 2, 1)])
            swiglu(0, 4)
            norm(("mix", 1), 4)
            store("od_q", 1, 2, 1, lambda j, g: nq[:, :, j * 512:(j + 1) * 512])
            dve.wait_ge(stored.sem, stored.count)
            group_rms("naq", nq.rearrange("p t (g d) -> p t g d", d=64), xn_, [(0, 16, row("na_q_g"))])
            kv_view = lambda j, g: (nk_ if j < 2 else v["nv"])[:, 2 * g:2 * g + 2, (j % 2) * 512:(j % 2) * 512 + 512]
            store("od_kv", 1, 2, 2, kv_view)
            dve.wait_ge(stored.sem, stored.count)
            group_rms("nak", nk_.rearrange("p t (g d) -> p t g d", d=64), xn_, [(0, 16, row("na_k_g"))])
            store("od_kv", 1, 2, 2, kv_view, 2)
            link(dve.memset(small[:, 16:17], 0.0), pre_turn, "na")
            copy_turned("naq")
            copy_turned("nak")
            add_mask(0)
            attend("na", prob_na, None)
            copy_turned("y1")
            dve.wait_ge(*acted.after("gates", 1, 3))
            residual("w_out", 1, 2, 1, [gate(1, 2, 0)])
            swiglu(1, 2)

            state = {"b": 0}

            def biased(st, l, n, dst, n0=0, first_bank=0):
                for j in range(n0, n0 + n):
                    b = state["b"]
                    state["b"] += 1
                    dve.wait_ge(*projected.after(st, l, j, 0))
                    dve.wait_ge(*bias_in[b % 2].after(b))
                    br = bc(bias_ring[:, b % 2, :], [P, 2, 512])
                    bank = first_bank + 2 * (j % 2)
                    ins = dve.tensor_tensor(dst(j), PS[:, bank:bank + 2, :], br, ALU.add)
                    ins.then_inc(*stored.now(st, l, j, 0))
                    stored.alias("bias", b)

            def layer_norms(l, key, h_buf, width, gain, gate_buf):
                link(dve.memset(small[:, 16:17], 0.0), sums_ready, key, l)
                dve.wait_ge(*root_ready.after(key, l))
                link(dve.reciprocal(stat[:, 152:160], stat[:, 144:152]))
                for t in range(2):
                    for h in range(R_H):
                        i = t * R_H + h
                        s = h_buf[t][:, h * width:(h + 1) * width]
                        ins = dve.tensor_scalar(s, s, stat[:, 128 + 2 * i:129 + 2 * i], stat[:, 152 + i:153 + i],
                                                ALU.subtract, ALU.mult)
                link(ins)
                for t in range(2):
                    ins = dve.tensor_tensor(h_buf[t], h_buf[t], gain, ALU.mult)
                link(ins)
                dve.wait_ge(*tok_acted.after("mo" if key == "hm" else "rg", l, R_H * width // 512 - 1, 0))
                for t in range(2):
                    ins = dve.tensor_tensor(h_buf[t], h_buf[t], gate_buf[:, t, :], ALU.mult)
                link(ins, y_ready, "ym" if key == "hm" else "yr", l)

            def wide(buf):
                return lambda j: buf[:, :, j * 512:(j + 1) * 512]

            dve.wait_ge(*wgate_in.after())
            split((wgh[:, :], wgl[:, :]), wgate[:, :]).then_inc(*wgate_ready.now())
            for l in range(2):
                norm(("n1", l), 2)
                dve.wait_ge(*projected.after("gates", l, 0, 0))
                dve.tensor_scalar(gt[:, 0, :], PS[0:4, 4, 0:256], bgate[:, l, 0:1], None, ALU.add)
                link(dve.tensor_scalar(gt[:, 1, :], PS[0:4, 4, 256:512], bgate[:, l, 1:2], None, ALU.add))
                link(dve.scalar_tensor_tensor(gt[:, 2, :], gt[:, 1, :], -1.0, gt[:, 1, :], ALU.mult, ALU.max), gate_abs, l)
                conv_in = SCR[:, 0:1036].rearrange("p (s t) -> p s t", s=4)
                link(dve.memset(conv_in[:, :, 0:3], 0.0), const_ready, "pad", l)
                dve.wait_ge(*gate_act.after(l))
                link(dve.scalar_tensor_tensor(gt[:, 1, :], gt[:, 1, :], 0.0, gt[:, 2, :], ALU.min, ALU.subtract))
                link(dve.memset(gt[:, 4, :], 0.0))
                link(dve.tensor_tensor_scan(gt[:, 2, :], gt[:, 1, :], gt[:, 4, :], 0.0, ALU.add, ALU.add))
                link(dve.tensor_tensor(gt[:, 0, :], gt[:, 0, :], gt[:, 2, :], ALU.subtract))
                link(dve.tensor_tensor_scan(gt[:, 4, :], gt[:, 0, :], gt[:, 0, :], 0.0, ALU.max, ALU.max))
                link(dve.tensor_scalar(gt[:, 3, :], gt[:, 4, :], -1.0, None, ALU.mult))
                link(dve.tensor_tensor(gt[:, 4, :], gt[:, 4, :], gt[:, 2, :], ALU.add), gate_scan, l)
                cw = col("conv_w")
                for j in range(4):
                    dve.wait_ge(*unit_acted.after("mqk", l, j, 0))
                    for k in range(4):
                        for s in range(4):
                            ch = j * 4 + s
                            o = mqkT[:, ch, :]
                            wk = cw[:, (l * 4 + k) * 16 + ch:(l * 4 + k) * 16 + ch + 1]
                            i = conv_in[:, s, k:k + 256]
                            if k == 0:
                                ins = dve.tensor_scalar(o, i, wk, col("conv_b")[:, l * 16 + ch:l * 16 + ch + 1],
                                                        ALU.mult, ALU.add)
                            else:
                                ins = dve.scalar_tensor_tensor(o, i, wk, o, ALU.mult, ALU.add)
                        if k < 3:
                            link(ins)
                    ins.then_inc(*qk_ready.now("mqk", l, j, 0))
                biased("mv", l, 2, wide(mv))
                biased("mo", l, 2, wide(mo))
                cosT, sinT = (bc(tab(n), [P, 2, 256]) for n in ("cosT", "sinT"))
                rope_in = SCR[:, 0:1024].rearrange("p (h s t) -> p h s t", h=2, s=2)
                tmp = SCR[:, 1024:2048].rearrange("p (a h t) -> p a h t", a=2, h=2)
                for j in range(4):
                    dve.wait_ge(*unit_acted.after("rqk", l, j, 0))
                    x1, x2 = rope_in[:, :, 0, :], rope_in[:, :, 1, :]
                    o = rqkT[:, 4 * j:4 * j + 4, :].rearrange("p (h s) t -> p h s t", s=2)
                    dve.tensor_tensor(tmp[:, 0], x1, cosT, ALU.mult)
                    link(dve.tensor_tensor(tmp[:, 1], x2, sinT, ALU.mult))
                    link(dve.tensor_tensor(o[:, :, 0, :], tmp[:, 0], tmp[:, 1], ALU.subtract))
                    dve.tensor_tensor(tmp[:, 0], x1, sinT, ALU.mult)
                    link(dve.tensor_tensor(tmp[:, 1], x2, cosT, ALU.mult))
                    ins = dve.tensor_tensor(o[:, :, 1, :], tmp[:, 0], tmp[:, 1], ALU.add)
                    ins.then_inc(*qk_ready.now("rqk", l, j, 0))
                    dve.wait_ge(qk_ready.sem, qk_ready.count)
                dve.wait_ge(*gate_cols.after(l))
                dve.wait_ge(*nrows_in.after(l))
                mask = tab("mask")

                def head_stats(key, h, h_buf, width):
                    for t in range(2):
                        i = t * R_H + h
                        link(dve.bn_stats(stat[:, 160 + 6 * t:166 + 6 * t], h_buf[t][:, h * width:(h + 1) * width]))
                        link(dve.bn_aggr(stat[:, 128 + 2 * i:130 + 2 * i], stat[:, 160 + 6 * t:166 + 6 * t]))

                def m_out(h):
                    dve.wait_ge(*attended.after("m", l, h))
                    for t in range(2):
                        den, floor = small[:, 40 + t:41 + t], small[:, 32 + 4 * t + h:33 + 4 * t + h]
                        link(dve.tensor_scalar(den, PS[:, 6 + t, 256:257], -1.0, floor, ALU.mult, ALU.max))
                        link(dve.tensor_tensor(den, den, PS[:, 6 + t, 256:257], ALU.max))
                    link(dve.reciprocal(small[:, 42:44], small[:, 40:42]))
                    for t in range(2):
                        ins = dve.tensor_scalar(hm[t][:, h * 256:(h + 1) * 256], PS[:, 6 + t, 0:256],
                                                small[:, 42 + t:43 + t], None, ALU.mult)
                    link(ins, y_out, "m", l, h)
                    head_stats("hm", h, hm, 256)

                def r_out(h):
                    dve.wait_ge(*attended.after("r", l, h))
                    for t in range(2):
                        ins = dve.tensor_copy(hr[t][:, h * 512:(h + 1) * 512], PS[:, 6 + t, :])
                    link(ins, y_out, "r", l, h)
                    head_stats("hr", h, hr, 512)

                def arg(h):
                    dve.wait_ge(*u_bc.after(l, h))
                    e = SCR[:, 768 + 384 * (h % 2):1152 + 384 * (h % 2)]
                    ub = PS[:, 5, 0:256]
                    dve.scalar_tensor_tensor(e[:, 0:256], ub, small[:, 24 + h:25 + h], mask[:, 0:256], ALU.add, ALU.add)
                    link(dve.scalar_tensor_tensor(e[:, 256:384], ub[:, 128:256], small[:, 28 + h:29 + h],
                                                  mask[:, 256:384], ALU.add, ALU.add), exp_arg, l, h)

                for h in range(R_H):
                    arg(h)
                    biased("rv", l, 1, wide(rv), h)
                    dve.wait_ge(*exp_ready.after("m", l, h))
                    link(dve.scalar_tensor_tensor(SCR[:, 384 * (h % 2):384 * (h % 2) + 384], PS[:, 4, 0:384],
                                                  QK_SCALE, SCR[:, 768 + 384 * (h % 2):1152 + 384 * (h % 2)],
                                                  ALU.mult, ALU.mult), probs_ready, "m", l, h)
                    if h >= 1:
                        m_out(h - 1)
                biased("rg", l, 1, wide(rg))
                m_out(R_H - 1)
                layer_norms(l, "hm", hm, 256, G[:, 0:1024], mo)
                biased("rg", l, 3, wide(rg), 1)
                decay = tab("decay").rearrange("p (h n) -> p h n", h=R_H)
                for h in range(R_H):
                    dve.wait_ge(*scored.after("r", l, h))
                    link(dve.scalar_tensor_tensor(SCR[:, 384 * (h % 2):384 * (h % 2) + 384], PS[:, 4 + h % 2, 0:384],
                                                  QK_SCALE, decay[:, h, :], ALU.mult, ALU.mult),
                         probs_ready, "r", l, h)
                    if h < 2:
                        biased("gm", l, 1, wide(gm), h)
                    else:
                        biased("gr", l, 1, wide(gr), h - 2)
                    if h >= 1:
                        r_out(h - 1)
                r_out(R_H - 1)
                copy_turned(("ym", l))
                layer_norms(l, "hr", hr, 512, G[:, 1024:3072], rg)
                for j in range(2):
                    dve.wait_ge(*projected.after("w_bm", l, j, 0))
                    if j == 0:
                        dve.wait_ge(*tok_acted.after("gr", l, 1, 0))
                    cols = slice(j * 512, (j + 1) * 512)
                    dve.tensor_tensor(merged[:, :, cols], pair_view(j), gm[:, :, cols],
                                      ALU.mult).then_inc(*stored.now("w_bm", l, j, 0))
                copy_turned(("yr", l))
                for j in range(2):
                    dve.wait_ge(*projected.after("w_br", l, j, 0))
                    cols = slice(j * 512, (j + 1) * 512)
                    link(dve.tensor_tensor(gr[:, :, cols], pair_view(j), gr[:, :, cols], ALU.mult))
                    link(dve.tensor_tensor(merged[:, :, cols], merged[:, :, cols], gr[:, :, cols], ALU.add),
                         stored, "w_br", l, j, 0)
                copy_turned(("mg", l))
                for j in range(2):
                    dve.wait_ge(*projected.after("w_out2", l, j, 0))
                    xs = X[:, 0:2, j * 512:(j + 1) * 512]
                    ins = dve.tensor_tensor(xs, xs, pair_view(j), ALU.add)
                    link(ins, x_ready, "w_out2", l, j, 0)
                norm(("n2", l), 2)
                for j in range(8):
                    dve.wait_ge(*ff_acted.after("ff1", l, j, 0))
                    s = SCR[:, 1024 * (j % 2):1024 * (j % 2) + 1024]
                    link(dve.tensor_tensor(s, s, s, ALU.mult))
                    k = 4 * (j % 4)
                    split([a[:, k:k + 4, :] for a in ff2T],
                          s.rearrange("p (s t) -> p s t", s=4)).then_inc(*hidden.now("ff1", l, j, 0))
                t2 = SCR[:, 0:1024].rearrange("p (t n) -> p t n", t=2)
                for j in range(2):
                    biased("ff2", l, 1, lambda j: t2, j, 4)
                    dve.wait_ge(stored.sem, stored.count)
                    xs = X[:, 0:2, j * 512:(j + 1) * 512]
                    link(dve.tensor_tensor(xs, xs, t2, ALU.add), x_ready, "ff2", l)
                dve.wait_ge(*pT_in.after(l))
                split(pT2, pT[:, :]).then_inc(*pT_ready.now(l))
                norm(("n3", l), 2)
                for j in range(2):
                    dve.wait_ge(*projected.after("w_pe", l, j, 0))
                    cols = slice(j * 512, (j + 1) * 512)
                    link(dve.tensor_tensor(t2, pair_view(j), gm[:, :, cols], ALU.mult), stored, "w_pe", l, j, 0)
                    link(dve.tensor_tensor(X[:, 0:2, cols], X[:, 0:2, cols], t2, ALU.add), x_ready, "pe", l)
            norm("out", 2)
            dve.wait_ge(normed.sem, normed.count)
            link(dve.tensor_tensor(xn[:, 0:2, :], xn[:, 0:2, :], bc(G[:, 3072:4096], [P, 2, D]), ALU.mult),
                 x_ready, "out")


def weight_chunks(w):
    k, n = w.shape
    kg, nb = -(-k // (KC * P)), -(-n // NC_)
    full = np.zeros((kg * KC * P, nb * NC_), w.dtype)
    full[:k, :n] = w
    return full.reshape(kg, KC, P, nb, NC_).transpose(3, 0, 2, 1, 4).reshape(nb * kg, P, CHUNK)


def flat_chunk(w):
    k, n = w.shape
    out = np.zeros((1, P, CHUNK), w.dtype)
    out[0, :, :k // P * n] = w.reshape(k // P, P, n).transpose(1, 0, 2).reshape(P, -1)
    return out


def paired(w):
    g, u = w[:, :D_FF], w[:, D_FF:]
    return np.stack([g.reshape(-1, D_FF // 256, 256), u.reshape(-1, D_FF // 256, 256)], 2).reshape(w.shape)


def feature_cols(a):
    return a.reshape(-1, a.shape[-1] // P, P).transpose(2, 0, 1).reshape(P, -1)


def lay_out(i):
    chunks = []
    mod = [weight_chunks(i["mod_w"][1])[2 * sum(MOD_PARTS[1][:n]):2 * sum(MOD_PARTS[1][:n + 1])] for n in range(4)]
    for l in range(2):
        if l == 0:
            chunks += [weight_chunks(i["mod_w"][0]), weight_chunks(i["ev_w_in"][0]), mod[0], mod[1],
                       flat_chunk(i["mla_w_uq"][0]), flat_chunk(i["mla_w_ukv"][0]), mod[2], mod[3]]
        else:
            chunks.append(weight_chunks(i["od_w_in"][0]))
        chunks.append(weight_chunks(i["w_out"][l]))
        n0 = 0
        for n in FF_PARTS[l]:
            chunks += [weight_chunks(paired(i["ffn_w_in"][l])[:, 512 * n0:512 * (n0 + n)]),
                       weight_chunks(i["ffn_w_out"][l][256 * n0:256 * (n0 + n)])]
            n0 += n
    cuts = [0, 2048, 3072, 4096, 4104, 6152, 8200, 10248, 11272, 12296]
    brows = []
    for l in range(2):
        w, b = i["w_in_2"][l], i["b_in_2"][l]
        for n in (0, 1, 2, 4, 5, 6, 7, 8):
            chunks.append(weight_chunks(w[:, cuts[n]:cuts[n + 1]]))
            if n not in (0, 4):
                brows.append(b[cuts[n]:cuts[n + 1]])
        brows.append(i["b_ff2_2"][l])
        chunks += [weight_chunks(i[k][l]) for k in ("w_bm_2", "w_br_2", "w_out_2")]
        for half in (slice(0, 2048), slice(2048, 4096)):
            chunks += [weight_chunks(i["w_ff1_2"][l][:, half]), weight_chunks(i["w_ff2_2"][l][half])]
        chunks.append(weight_chunks(i["w_pe_gate_2"][l]))
        chunks.append(flat_chunk(i["w_pe_2"][l]))
    cols = [np.stack([i["c"][0], i["c_ctx"]]).reshape(2, KD, P).transpose(2, 1, 0).reshape(P, -1)]
    cols += [feature_cols(i[k]) for k in ("norm_mix_g", "norm_ffn_g", "norm1_g_2", "norm2_g_2", "norm3_g_2")]
    b_in = i["b_in_2"]
    cols += [feature_cols(b_in[:, 0:2048]), feature_cols(b_in[:, 4104:6152]), feature_cols(i["conv_w_2"]),
             feature_cols(i["conv_b_2"]), feature_cols(i["b_ff1_2"])]
    rows = [i["da_q_g"], i["da_k_g"], i["da_lq1"], i["da_lq2"], i["da_lk1"], i["da_lk2"], i["da_out_g"],
            i["mla_q_a_g"], i["mla_kv_a_g"], i["mla_q_g"], i["mla_k_g"], i["mla_kr_g"], i["na_q_g"], i["na_k_g"]]
    padded = np.zeros((NA_H, 2 * NA_KH - 1, REL_W), np.float32)
    padded[:, :, GRID_W - NA_KW:GRID_W + NA_KW - 1] = i["na_rpb"][0]
    rel = np.stack([padded[:, :, GRID_W - 1 - q:REL_W - q] for q in range(GRID_W)])
    wg = i["w_in_2"][:, :, 4096:4104].reshape(2, KD, P, 8).transpose(2, 0, 1, 3).reshape(P, -1)
    nrows = np.zeros((2, 4096), np.float32)
    nrows[:, 0:1024], nrows[:, 1024:3072], nrows[:, 3072:] = i["m_norm_g_2"], i["r_norm_g_2"], i["final_g_2"]
    tiles = lambda a: a.reshape(TX, P, D).transpose(1, 0, 2)
    arrays = [tiles(i["x"]), tiles(i["ctx"]), np.concatenate(chunks), np.concatenate(cols, 1),
              np.concatenate([r.reshape(-1) for r in rows]), tables(), feature_cols(i["mod_b"]).reshape(P, 2, -1), rel,
              np.concatenate(brows).reshape(-1, NC_), b_in[:, 4096:4104].reshape(2, 2, 4).transpose(2, 0, 1), wg, nrows,
              i["p_2"][:, 0].reshape(2, SEQ, 2, P).transpose(3, 0, 2, 1).reshape(P, 2, 512)]
    return [np.ascontiguousarray(a) for a in arrays]


NAMES = ["x", "ctx", "chunks", "cols", "rows", "tabs", "modb", "rel", "brows", "bgate", "wgate", "nrows", "pT"]


def kernel(**inputs):
    import concourse.bacc as bacc
    from concourse.bass_utils import run_bass_kernel_spmd

    arrays = lay_out({k: np.asarray(a) for k, a in inputs.items()})
    plan = {}
    for _ in range(2):
        nc = bacc.Bacc("TRN2", target_bir_lowering=False, num_devices=1, dynamic_dma_scratch_size=2048)
        ins = [nc.dram_tensor(n + "_in", a.shape, F32, kind="ExternalInput").ap() for n, a in zip(NAMES, arrays)]
        out = nc.dram_tensor("out", (1, SEQ, D), F32, kind="ExternalOutput").ap()
        build_program(nc, plan, ins, out.rearrange("b (t p) d -> p (b t) d", p=P))
    r = run_bass_kernel_spmd(nc, [{n + "_in": a for n, a in zip(NAMES, arrays)}], core_ids=[0])
    return r.results[0]["out"]
```

```python
from contextlib import ExitStack

import numpy as np

import concourse.bass as bass
from concourse import mybir

ALU = mybir.AluOpType
ACT = mybir.ActivationFunctionType
F32 = mybir.dt.float32
F32R = mybir.dt.float32r
AX_X = mybir.AxisListType.X

P = 128
D = 1024
KD = D // P
SEQ = 256
TX = SEQ // P
GRID_W = 64
DA_H, DA_DK, DA_DV = 4, 64, 128
ML_H, ML_NOPE, ML_ROPE, ML_V = 4, 128, 64, 128
ML_QL, ML_KVL = 256, 128
ML_QK = ML_NOPE + ML_ROPE
EV_IN = 3 * DA_H * 2 * DA_DK + ML_QL + ML_KVL + ML_ROPE
NA_H, NA_DH, NA_KH, NA_KW = 16, 64, 8, 16
NA_ROWS = SEQ // GRID_W
D_FF = 2816
EPS = 1e-6
LAM_INIT = 0.2
R_H = 4
QK_SCALE = 1.0 / 16.0
NEG = -1e30

NC_ = 512
KC = 4
CHUNK = KC * NC_
FF_PARTS = ((4, 4, 3), (11,))
MOD_PARTS = ((12,), (3, 4, 3, 2))
RING = 4
HI_RING = 3
AHEAD = HI_RING - 1
REL_W = 2 * GRID_W - 1

COLS = [("cond", 2 * KD), ("mix_g", 2 * KD), ("ffn_g", 2 * KD), ("n1", 2 * KD), ("n2", 2 * KD), ("n3", 2 * KD),
        ("b_mqk", 32), ("b_rqk", 32), ("conv_w", 128), ("conv_b", 32), ("b_ff1", 64)]
ROWS = [("da_q_g", 64), ("da_k_g", 64), ("lq", 128), ("lk", 128), ("da_out_g", 128), ("mla_q_a_g", 256),
        ("mla_kv_a_g", 128), ("mla_q_g", 192), ("mla_k_g", 128), ("mla_kr_g", 64), ("na_q_g", 64), ("na_k_g", 64)]
TABS = [("ident", 128), ("cos", 64), ("sin", 64), ("cosT", 256), ("sinT", 256), ("decay", 4 * 384), ("mask", 384),
        ("ones", 128), ("sel_h", 4 * 128), ("na_mask", GRID_W)]


def spans(items):
    at, out = 0, {}
    for name, n in items:
        out[name] = (at, at + n)
        at += n
    return out, at


def tables():
    s, n = spans(TABS)
    t = np.zeros((P, n), np.float32)

    def put(name, a):
        t[:a.shape[0], s[name][0]:s[name][1]] = a.reshape(a.shape[0], -1)

    put("ident", np.eye(P))
    tok = np.arange(SEQ)
    half = DA_DK // 2
    inv = (np.float32(10000.0) ** (-np.arange(0, half, 2, dtype=np.float32) / np.float32(half))).astype(np.float32)
    ang = np.stack([(tok // GRID_W).astype(np.float32)[:, None] * inv,
                    (tok % GRID_W).astype(np.float32)[:, None] * inv], 1).astype(np.float32)
    by_tile = ang.reshape(TX, P, 2, half // 2).transpose(1, 0, 2, 3)
    put("cos", np.cos(by_tile))
    put("sin", np.sin(by_tile))
    inv2 = (np.float32(10000.0) ** (-np.arange(0, 256, 2, dtype=np.float32) / np.float32(256))).astype(np.float32)
    ang2 = (inv2[:, None] * tok.astype(np.float32)[None, :]).astype(np.float32)
    put("cosT", np.cos(ang2))
    put("sinT", np.sin(ang2))
    p = np.arange(P)
    s_of = np.concatenate([np.zeros(256), np.full(128, 128)])[None, :] + p[:, None]
    t_of = np.concatenate([np.arange(256), np.arange(128, 256)])[None, :] + 0 * p[:, None]
    lg = np.log(1.0 - np.exp2(-5.0 - np.arange(R_H)))
    put("decay", np.stack([np.where(t_of >= s_of, np.exp((t_of - s_of) * g), 0.0) for g in lg], 1))
    put("mask", np.where(t_of >= s_of, 0.0, NEG))
    put("ones", np.ones((P, P)))
    put("sel_h", np.repeat(np.eye(R_H)[:, :, None], P, 2))
    qc, kc = (p % GRID_W)[:, None], np.arange(GRID_W)[None, :]
    start = np.clip(qc - NA_KW // 2, 0, GRID_W - NA_KW)
    put("na_mask", np.where((kc >= start) & (kc < start + NA_KW), 0.0, NEG))
    return t


class Event:

    def __init__(self, sem, name, plan):
        self.sem, self.name, self.plan, self.count = sem, name, plan, 0

    def now(self, *step, by=1):
        self.count += by
        self.plan[(self.name, step)] = self.count
        return self.sem, by

    def after(self, *step):
        return self.sem, self.plan.get((self.name, step), 1)

    def alias(self, *step):
        self.plan[(self.name, step)] = self.count


def attention_banks(ph, u):
    return (2 + 2 * (u % 3), 0, 1, u % 3) if ph == "da" else (4 + u % 4, u % 2, 2 + u % 2, u % 4)


def attention_units(v):
    phases = {}
    da, mla, na = [], [], []
    for h in range(DA_H):
        for t in range(4):
            k0, nk = (0, 512) if t < TX else (256, 256)
            da.append(dict(scores=[[(v["dqT"][64 * i:64 * i + 64, h, t * P:(t + 1) * P],
                                     v["dkT"][64 * i:64 * i + 64, h, k0:k0 + nk])] for i in range(2)],
                           nk=nk, scale=DA_DK ** -0.5, bias=None, dv=DA_DV,
                           value=[v["z"][:, (k0 // P) + j, 1024 + h * 128:1024 + (h + 1) * 128] for j in range(nk // P)],
                           out=v["y4"][:, t, h * 128:(h + 1) * 128]))
    for h in range(ML_H):
        for t in range(4):
            k0, nk = (0, 512) if t < TX else (256, 256)
            q = slice(t * P, (t + 1) * P)
            mla.append(dict(scores=[[(v["qnT"][:, h, q], v["knT"][:, h, k0:k0 + nk]),
                                     (v["qrT"][0:64, h, q], v["krT"][0:64, k0:k0 + nk])]],
                            nk=nk, scale=ML_QK ** -0.5, bias=None, dv=ML_V,
                            value=[v["kv"][:, (k0 // P) + j, h * 256 + 128:h * 256 + 256] for j in range(nk // P)],
                            out=v["y4"][:, t, 512 + h * 128:512 + (h + 1) * 128]))
    for h in range(NA_H):
        for t in range(TX):
            part = slice(64 * (h % 2), 64 * (h % 2) + 64)
            na.append(dict(scores=[[(v["nqT"][part, h // 2, t * P:(t + 1) * P], v["nkT"][part, h // 2, :])]],
                           nk=512, scale=NA_DH ** -0.5, bias=v["rel"][h // 8][:, t, h % 8, :], dv=NA_DH,
                           value=[v["nv"][:, j, h // 2 * 128:h // 2 * 128 + 128] for j in range(4)],
                           out=(part, h // 2, slice(t * P, (t + 1) * P))))
    phases["da"], phases["mla"], phases["na"] = da, mla, na
    return phases


def build_program(nc, plan, ins, out):
    x_d, ctx_d, chunks_d, cols_d, rows_d, tabs_d, modb_d, rel_d, brows_d, bgate_d, wgate_d, nrows_d, pT_d = ins
    ctx = ExitStack()
    with ctx:
        def sb(name, shape):
            return ctx.enter_context(nc.sbuf_tensor(name, shape, F32))

        def ev(name):
            return Event(ctx.enter_context(nc.semaphore(name)), name, plan)

        cs, ncols = spans(COLS)
        rs, nrows = spans(ROWS)
        ts, ntabs = spans(TABS)
        arena_floats = (nc.sbuf_usable_end - nc.sbuf_base) // 4 - 16
        arena = ctx.enter_context(nc.sbuf_tensor("arena", [P, arena_floats], F32))
        base = nc.sbuf_base - 4 * arena_floats
        cursor = [0]

        def place(name, n, dt=F32, at=None):
            start = cursor[0] if at is None else at
            if at is None:
                cursor[0] += -(-n // 8) * 8
            assert cursor[0] <= arena_floats, name
            return nc.alloc_sbuf_tensor_at(name, [P, n], dt, offset=base + 4 * start), start

        raw_, raw_at = place("raw", RING * CHUNK)
        wlo_, _ = place("w_lo", RING * CHUNK, F32R, raw_at)
        whi_, _ = place("w_hi", HI_RING * CHUNK, F32R)
        xhi_, xhi_at = place("x_hi", 4096, F32R)
        xlo_, xlo_at = place("x_lo", 4096, F32R)
        free_a, _ = place("free_a", 4096, F32, xhi_at)
        free_b, _ = place("free_b", 4096, F32, xlo_at)
        X = place("X", 4 * D)[0][:, :].rearrange("p (t d) -> p t d", t=4)
        xn_, xn_at = place("xn", 4 * D)
        xnr_, _ = place("xn_r", 4 * D, F32R, xn_at)
        G = place("G", 4096)[0]
        SCR = place("SCR", 2048)[0]
        colt = place("colt", ncols)[0]
        rowt = place("rowt", nrows)[0]
        gt = rowt[0:4, 0:1280].rearrange("p (a t) -> p a t", a=5)
        tabt = place("tabt", ntabs)[0]
        wgate = place("wgate", 128)[0]
        wgh = place("wgate_hi", 128, F32R)[0]
        wgl = place("wgate_lo", 128, F32R)[0]
        pT = place("pT", 512)[0]
        bias_ = place("bias_ring", 2 * NC_)[0]
        bias_ring = bias_[:, :].rearrange("p (b n) -> p b n", b=2)
        modc = [bias_[:, l * 96:l * 96 + 96].rearrange("p (k c) -> p k c", c=2) for l in range(2)]
        mod_bias = bias_[:, 192:288].rearrange("p (l k) -> p l k", l=2)
        stat = place("stat", 216)[0]
        small = place("small", 64)[0]
        bgate = place("bgate", 4)[0][0:4, :].rearrange("p (l g) -> p l g", l=2)
        n_big = 12288
        BIG, big_at = place("BIG", n_big)
        BIGR, _ = place("BIGR", n_big, F32R, big_at)
        ring = raw_[:, :].rearrange("p (s n) -> p s n", s=RING)
        w_hi = whi_[:, :].rearrange("p (s n) -> p s n", s=HI_RING)
        w_lo = wlo_[:, :].rearrange("p (s n) -> p s n", s=RING)
        PS = ctx.enter_context(nc.psum_tensor("PS", [P, 8, 512], F32))

        def col(name):
            return colt[:, cs[name][0]:cs[name][1]]

        def row(name):
            return rowt[:, rs[name][0]:rs[name][1]]

        def tab(name, parts=P):
            return tabt[0:parts, ts[name][0]:ts[name][1]]

        ident = tab("ident")
        def pair_of(t, n, k):
            return tuple(a[:, 0:k * n].rearrange("p (k t) -> p k t", k=k) for a in t)

        hT = {4: pair_of((xhi_, xlo_), 512, KD), 2: pair_of((xhi_, xlo_), 256, KD)}
        xn = xn_[:, :].rearrange("p (t d) -> p t d", t=4)
        big = lambda a, n: BIG[:, a:a + n]
        bigr = lambda a, n: BIGR[:, a:a + n]
        z0 = big(0, 4 * EV_IN).rearrange("p (t c) -> p t c", t=4)
        v = {"z": z0, "y4": xn}
        v["dqT"] = big(7936, 2048).rearrange("p (h t) -> p h t", h=4)
        v["dkT"] = big(9984, 2048).rearrange("p (h t) -> p h t", h=4)
        v["qnT"], v["knT"] = v["dqT"], v["dkT"]
        v["qrT"] = free_b[:, 2048:4096].rearrange("p (h t) -> p h t", h=4)
        v["krT"] = free_a[:, 2048:2560]
        cT = pair_of((bigr(7936, 1536), bigr(9984, 1536)), 512, 3)
        q_l0 = z0[:, :, 0:768]
        v["kv"] = z0[:, :, 768:1792]
        probs = {"da": free_a[:, 0:3072].rearrange("p (b i k) -> p b i k", b=3, i=2),
                 "mla": free_a[:, 0:2048].rearrange("p (b i k) -> p b i k", b=4, i=1),
                 "na": SCR[:, 0:2048].rearrange("p (b i k) -> p b i k", b=4, i=1)}
        mix4 = free_a[:, 3072:4096].rearrange("p (b k) -> p b k", b=2)
        probsT = {"da": SCR[:, 0:1024], "mla": free_a[:, 3072:4096], "na": X[:, 2, :]}
        squares = free_b
        nq = big(0, 2048).rearrange("p (t c) -> p t c", t=2)
        nk_ = big(2048, 4096).rearrange("p (t c) -> p t c", t=4)
        v["nv"] = big(6144, 4096).rearrange("p (t c) -> p t c", t=4)
        v["nqT"] = big(10240, 2048).rearrange("p (h t) -> p h t", h=8)
        v["nkT"] = free_a[:, :].rearrange("p (h t) -> p h t", h=8)
        v["rel"] = [free_b[:, :].rearrange("p (t h k) -> p t h k", t=2, h=NA_H // 2),
                    big(2048, 4096).rearrange("p (t h k) -> p t h k", t=2, h=NA_H // 2)]
        diag = bias_[:, 288:544].rearrange("p (b k) -> p b k", b=2)
        yT_na = pair_of((xnr_[:, 0:2048], xnr_[:, 2048:4096]), 256, 8)
        units = attention_units(v)
        mqkT = big(0, 4096).rearrange("p (c t) -> p c t", c=16)
        rg = big(0, 4096).rearrange("p (t c) -> p t c", t=2)
        conv_ins = [big(4096 + 1040 * i, 1036).rearrange("p (s t) -> p s t", s=4) for i in range(2)]
        rqkT = big(4096, 4096).rearrange("p (c t) -> p c t", c=16)
        rv = big(8192, 4096).rearrange("p (t c) -> p t c", t=2)
        mv = free_a[:, 2048:4096].rearrange("p (t c) -> p t c", t=2)
        mo = free_b[:, 2048:4096].rearrange("p (t c) -> p t c", t=2)
        gm, gr = X[:, 2:4, :], xn[:, 2:4, :]
        hm = [xn[:, t, :] for t in range(2)]
        hr = [free_a[:, 2048:4096], free_b[:, 2048:4096]]
        ymT = pair_of((bigr(4096, 2048), bigr(6144, 2048)), 256, 8)
        yrT = pair_of((bigr(0, 4096), bigr(8192, 4096)), 256, 16)
        merged = SCR[:, :].rearrange("p (t c) -> p t c", t=2)
        ffT = {l: pair_of((bigr(0, k * n), bigr(k * n, k * n)), n, k) for l, n, k in ((0, 512, 8), (1, 256, 22))}
        ff2T = pair_of((bigr(0, 4096), bigr(4096, 4096)), 256, 16)
        pT2 = (bigr(0, 512), bigr(512, 512))

        cols_in = ev("cols_in")
        tab_in, x_in, rel_in, wgate_in = ev("tab_in"), ev("x_in"), [ev("rel_in0"), ev("rel_in1")], ev("wgate_in")
        modb_in, nrows_in, pT_in = ev("modb_in"), ev("nrows_in"), ev("pT_in")
        w_in = [ev(f"w_in{i}") for i in range(RING)]
        bias_in = [ev(f"bias_in{i}") for i in range(2)]
        hi_ready, lo_ready = ev("hi_ready"), ev("lo_ready")
        shifted, pT_ready, wgate_ready = ev("shifted"), ev("pT_ready"), ev("wgate_ready")
        out_done = ev("out_done")
        vec_chain, act_chain = ev("vec_chain"), ev("act_chain")
        projected = ev("projected")
        stored = ev("stored")
        acted = ev("acted")
        turned = ev("turned")
        copied_v, copied_s = ev("copied_v"), ev("copied_s")
        x_ready, sums_ready, root_ready, normed = ev("x_ready"), ev("sums_ready"), ev("root_ready"), ev("normed")
        cond_ready, mod_rows, mod_turned = ev("cond_ready"), ev("mod_rows"), ev("mod_turned")
        mod_stored, mod_ready = ev("mod_stored"), ev("mod_ready")
        gate_diag, gates_bc = ev("gate_diag"), ev("gates_bc")
        lam_logit, lam_exp = ev("lam_logit"), ev("lam_exp")
        const_ready = ev("const_ready")
        pre_turn = ev("pre_turn")
        scored, max_ready, exp_ready, probs_ready = ev("scored"), ev("max_ready"), ev("exp_ready"), ev("probs_ready")
        probs_turned, probsT_ready, attended, y_out = ev("probs_turned"), ev("probsT_ready"), ev("attended"), ev("y_out")
        y_ready = ev("y_ready")
        unit_acted, qk_ready, qk_ready_act = ev("unit_acted"), ev("qk_ready"), ev("qk_ready_act")
        ff_acted, tap_ready = ev("ff_acted"), ev("tap_ready")
        gate_abs, gate_act, gate_scan, gate_turned, gate_cols = (ev("gate_abs"), ev("gate_act"), ev("gate_scan"),
                                                                ev("gate_turned"), ev("gate_cols"))
        u_bc, exp_arg = ev("u_bc"), ev("exp_arg")
        tok_acted = ev("tok_acted")
        hidden = ev("hidden")

        def gate_list(l):
            return [(kind, who, half) for kind in (2, 5) for who in range(2 - l) for half in range(2)]

        def gate(l, kind, who):
            n = gate_list(l).index((kind, who, 0))
            return G[:, n * 512:n * 512 + 1024]

        def copy_plan():
            plan_ = {}

            def add(key, nb, tiles, dst, width=P, kind="plain"):
                plan_[key] = (nb, tiles, width, dst, kind)

            def parts(pair):
                return lambda b: (pair[0][:, b, :], pair[1][:, b, :])
            for l, tiles in ((0, 4), (1, 4)):
                add(("mix", l), 8, tiles, parts(hT[4]), kind=("mod", 0))
            add(("ffn", 0), 8, 4, parts(hT[4]), kind=("mod", 3))
            add(("ffn", 1), 8, 2, parts(hT[2]), kind=("mod", 3))
            add("daq", 4, 4, lambda b: v["dqT"][:, b, :])
            add("dak", 4, 4, lambda b: v["dkT"][:, b, :])
            add("mlac", 3, 4, parts(cT), kind="parts")
            add("mlakr", 1, 4, lambda b: v["krT"][0:64, :], 64)
            add("qn", 4, 4, lambda b: v["qnT"][:, b, :])
            add("qr", 4, 4, lambda b: v["qrT"][0:64, b, :], 64)
            add("kn", 4, 4, lambda b: v["knT"][:, b, :])
            add("y0", 8, 4, parts(hT[4]), kind="parts")
            add("naq", 8, 2, lambda b: v["nqT"][:, b, :])
            add("nak", 8, 4, lambda b: v["nkT"][:, b, :])
            for l in range(2):
                for k in ("n1", "n2", "n3"):
                    add((k, l), 8, 2, parts(hT[2]), kind=("gain", k, l))
                add(("ym", l), 8, 2, parts(ymT), kind="parts")
                add(("yr", l), 16, 2, parts(yrT), kind="parts")
                add(("mg", l), 8, 2, parts(hT[2]), kind="parts")
            return plan_

        copies = copy_plan()

        def gain_of(key, b):
            kind = copies[key][4]
            return col(kind[1])[:, kind[2] * 8 + b:kind[2] * 8 + b + 1]

        eps, neg_lam = small[:, 61:62], small[:, 62:63]

        block = ctx.enter_context(nc.Block())
        n_chunks = chunks_d.shape[0]

        @block.tensor
        def _(pe):
            reader = {}
            state = {"c": 0, "b": 0}
            split = []

            def claim(*banks):
                for b in banks:
                    if b in reader:
                        pe.wait_ge(*reader.pop(b))

            def take_raw(st, l):
                c = state["c"]
                state["c"] += 1
                plan.setdefault(("first chunk", st, l), c)
                pe.wait_ge(*w_in[c % RING].after(c))
                return c, ring[:, c % RING, :].rearrange("p (k n) -> p k n", k=KC)

            def take_chunk(st, l, k_tiles=KC):
                c = state["c"]
                state["c"] += 1
                plan.setdefault(("first chunk", st, l), c)
                split.append(c)
                pe.wait_ge(*lo_ready.after(c))
                n = CHUNK // k_tiles
                return c, tuple(a.rearrange("p (k n) -> p k n", k=k_tiles) for a in (w_hi[:, c % HI_RING, :], w_lo[:, c % RING, :]))

            def used(c):
                projected.alias("used", c)

            def ends(mm, c, st, l, j, g=0):
                mm.then_inc(*projected.now(st, l, j, g))
                plan[("last chunk", st, l, j)] = c

            def product(o, lhs, rhs, start, stop, group=False):
                more = dict(skip_group_check=True) if group else {}
                pe.matmul(o, lhs[0], rhs[0], start=start, stop=False, **more)
                pe.matmul(o, lhs[0], rhs[1], start=False, stop=False, **more)
                return pe.matmul(o, lhs[1], rhs[0], start=False, stop=stop, **more)

            def tokens(pair):
                return lambda kt, t: tuple(a[:, kt, t * P:(t + 1) * P] for a in pair)

            def project_tok(st, l, n, k_tiles, lhs, groups=1, freed=stored, n0=0, biased=False, need=None):
                for j in range(n0, n0 + n):
                    if biased:
                        plan[("bias", state["c"])] = state["b"]
                        state["b"] += 1
                    for kg in range(-(-k_tiles // KC)):
                        if need and j == n0:
                            pe.wait_ge(*need(kg))
                        c, w = take_chunk(st, l)
                        for g in range(groups):
                            pair = (j * groups + g) % 2
                            if kg == 0:
                                claim(2 * pair, 2 * pair + 1)
                            for t in range(2):
                                for kt in range(KC * kg, min(KC * kg + KC, k_tiles)):
                                    mm = product(PS[:, 2 * pair + t, :], lhs(kt, 2 * g + t),
                                                 [a[:, kt - KC * kg, :] for a in w], kt == 0, kt == k_tiles - 1)
                            if kg == (k_tiles - 1) // KC:
                                ends(mm, c, st, l, j, g)
                                reader[2 * pair] = reader[2 * pair + 1] = freed.after(st, l, j, g)
                            elif g == groups - 1:
                                mm.then_inc(*projected.now(("chunk", c)))
                        used(c)

            def project_feat(st, l, n, rhs, groups=1, freed=stored, n0=0, need=None):
                for j in range(n0, n0 + n):
                    for kg in range(2):
                        if need and j == n0:
                            pe.wait_ge(*need(kg))
                        c, w = take_chunk(st, l)
                        for g in range(groups):
                            pair = (j * groups + g) % 2
                            if kg == 0:
                                claim(2 * pair, 2 * pair + 1)
                            for s in range(4):
                                for kt in range(KC * kg, KC * kg + KC):
                                    mm = product(PS[:, 2 * pair + s // 2, (s % 2) * 256:(s % 2) * 256 + 256],
                                                 [a[:, kt - KC * kg, s * P:(s + 1) * P] for a in w],
                                                 [a[:, kt, g * 256:g * 256 + 256] for a in rhs],
                                                 kt == 0 and s % 2 == 0, kt == KD - 1, True)
                            if kg == 1:
                                ends(mm, c, st, l, j, g)
                                reader[2 * pair] = reader[2 * pair + 1] = freed.after(st, l, j, g)
                            elif g == groups - 1:
                                mm.then_inc(*projected.now(("chunk", c)))
                        used(c)

            def turn(key, nb, tiles, src, width=P, ready=None):
                kind = copies[key][4]
                for b in range(nb):
                    claim(4 + b % 4)
                    for t in range(tiles):
                        if ready and b == 0:
                            pe.wait_ge(*ready(t))
                        mm = pe.transpose(PS[0:width, 4 + b % 4, t * P:(t + 1) * P], src(b, t), ident)
                    mm.then_inc(*turned.now(key, b))
                    if kind == "plain":
                        reader[4 + b % 4] = (copied_s if b % 2 else copied_v).after(key, b)
                    elif kind[0] == "mod":
                        reader[4 + b % 4] = shifted.after(key, b)
                    else:
                        reader[4 + b % 4] = copied_v.after(key, b)

            def await_copies(key, nb):
                pe.wait_ge(*copied_v.after(key, (nb - 1) // 2 * 2))
                if nb > 1:
                    pe.wait_ge(*copied_s.after(key, nb // 2 * 2 - 1))

            def copied(key):
                return lambda kg: copied_v.after(key, min(KC * kg + KC, copies[key][0]) - 1)

            def norm(key, tiles):
                turn(key, KD, tiles, lambda b, t: xn[:, t, b * P:(b + 1) * P], ready=lambda t: normed.after(key, t))
                return copied(key)

            def attend(ph):
                us = units[ph]
                probT = probsT[ph].rearrange("p (b k) -> p b k", b=2)

                def scores(u):
                    d = us[u]
                    s = attention_banks(ph, u)[0]
                    n = len(d["scores"])
                    claim(*range(s, s + n))
                    for i, mats in enumerate(d["scores"]):
                        for m, (a, b) in enumerate(mats):
                            mm = pe.matmul(PS[:, s + i, 0:d["nk"]], a, b, start=m == 0, stop=m == len(mats) - 1)
                    mm.then_inc(*scored.now(ph, u))
                    for i in range(n):
                        reader[s + i] = exp_ready.after(ph, u)

                def turn_probs(u):
                    _, b, _, slot = attention_banks(ph, u)
                    pe.wait_ge(*(exp_ready if ph == "mla" else probs_ready).after(ph, u))
                    claim(b)
                    for j in range(us[u]["nk"] // P):
                        keys = slice(j * P, (j + 1) * P)
                        if ph == "na":
                            mm = pe.matmul(PS[:, b, keys], probs[ph][:, slot, 0, keys], diag[:, u % 2, :],
                                           start=True, stop=True)
                        else:
                            prob = mix4[:, u % 2, :] if ph == "da" else probs[ph][:, slot, 0, :]
                            mm = pe.transpose(PS[:, b, keys], prob[:, keys], ident)
                    mm.then_inc(*probs_turned.now(ph, u))
                    reader[b] = probsT_ready.after(ph, u)

                def values(u):
                    d = us[u]
                    b = attention_banks(ph, u)[2]
                    pe.wait_ge(*probsT_ready.after(ph, u))
                    claim(b)
                    n = d["nk"] // P
                    for j in range(n):
                        pT_, val = probT[:, u % 2, j * P:(j + 1) * P], d["value"][j]
                        lhs, rhs = (val, pT_) if ph == "na" else (pT_, val)
                        mm = pe.matmul(PS[:, b, 0:P], lhs, rhs, start=j == 0, stop=j == n - 1)
                    mm.then_inc(*attended.now(ph, u))
                    reader[b] = y_out.after(ph, u)

                scores(0)
                scores(1)
                for u in range(len(us)):
                    if u + 2 < len(us):
                        scores(u + 2)
                    if u >= 1:
                        values(u - 1)
                    turn_probs(u)
                values(len(us) - 1)

            def modulation(l, part):
                if l == 0:
                    pe.wait_ge(*cond_ready.after())
                cond = small[:, 0:16].rearrange("p (k c) -> p k c", c=2)

                def turn_rows(j):
                    if (l, j) == (0, 0):
                        pe.wait_ge(*tab_in.after())
                    pe.wait_ge(*mod_rows.after(l, j))
                    for s in range(4):
                        at = 8 * j + 2 * s
                        mm = pe.transpose(PS[:, 4, at:at + 2], SCR[0:2, (j % 4) * 512 + s * P:(j % 4) * 512 + s * P + P],
                                          ident[0:2, 0:2])
                    mm.then_inc(*mod_turned.now(l, j))

                j0 = sum(MOD_PARTS[l][:part])
                claim(4)
                for j in range(j0, j0 + MOD_PARTS[l][part]):
                    claim(j % 4)
                    for kg in range(2):
                        c, w = take_raw("mod", l)
                        for kt in range(4):
                            mm = pe.matmul(PS[0:2, j % 4, :], cond[:, 4 * kg + kt, :], w[:, kt, :],
                                           start=kg == 0 and kt == 0, stop=kg == 1 and kt == 3)
                        mm.then_inc(*projected.now("mod", l, j, kg))
                        used(c)
                    reader[j % 4] = mod_rows.after(l, j)
                    if j > j0:
                        turn_rows(j - 1)
                turn_rows(j)
                reader[4] = mod_stored.after(l, part)

            def gates(l):
                for n in range(len(gate_list(l))):
                    b = 5 + n % 3
                    pe.wait_ge(*gate_diag.after(l, n))
                    claim(b)
                    pe.matmul(PS[:, b, :], tab("ones"), G[:, n * 512:(n + 1) * 512],
                              start=True, stop=True).then_inc(*gates_bc.now(l, n))
                    reader[b] = acted.after("gates", l, n)

            def even_attention():
                gates(0)
                modulation(1, 0)
                pe.wait_ge(*pre_turn.after("da"))
                turn("daq", 4, 4, lambda b, t: z0[:, t, b * P:(b + 1) * P])
                turn("dak", 4, 4, lambda b, t: z0[:, t, 512 + b * P:512 + (b + 1) * P])
                await_copies("daq", 4)
                await_copies("dak", 4)
                attend("da")
                modulation(1, 1)
                pe.wait_ge(*pre_turn.after("mla_c"))
                turn("mlac", 3, 4, lambda b, t: z0[:, t, 1536 + b * P:1536 + (b + 1) * P])
                turn("mlakr", 1, 4, lambda b, t: z0[:, t, 1920:1984], width=64)
                pe.wait_ge(*copied_v.after("mlac", 2))
                await_copies("mlakr", 1)
                for st, first, k_tiles, width in (("uq", 0, 2, 384), ("ukv", 2, 1, 512)):
                    c, w = take_chunk(st, 0, 1)
                    for t in range(4):
                        pair = t % 2
                        claim(2 * pair, 2 * pair + 1)
                        for half in range(2):
                            for kt in range(k_tiles):
                                at = kt * 2 * width + half * width
                                mm = product(PS[:, 2 * pair + half, 0:width], tokens(cT)(first + kt, t),
                                             [a[:, 0, at:at + width] for a in w], kt == 0, kt == k_tiles - 1)
                        ends(mm, c, st, 0, t)
                        reader[2 * pair] = reader[2 * pair + 1] = stored.after(st, 0, t, 0)
                    used(c)
                modulation(1, 2)
                pe.wait_ge(*pre_turn.after("mla_q"))
                turn("qn", 4, 4, lambda b, t: q_l0[:, t, b * 192:b * 192 + 128])
                turn("qr", 4, 4, lambda b, t: q_l0[:, t, b * 192 + 128:b * 192 + 192], width=64)
                turn("kn", 4, 4, lambda b, t: v["kv"][:, t, b * 256:b * 256 + 128])
                for k in ("qn", "qr", "kn"):
                    await_copies(k, 4)
                attend("mla")
                modulation(1, 3)

            def swiglu(l, tiles):
                g = tiles // 2
                need = norm(("ffn", l), tiles)
                n0 = 0
                for part, n in enumerate(FF_PARTS[l]):
                    project_feat("ffn_in", l, n, hT[tiles], g, n0=n0, need=need)
                    project_tok("ffn_out", l, 2, 2 * n, tokens(ffT[l]), g, n0=2 * part,
                                need=lambda kg: stored.after("hidden", l, n0 + min(2 * kg + 2, n) - 1, g - 1))
                    n0 += n
                    need = None

            modulation(0, 0)
            need = norm(("mix", 0), 4)
            project_tok("ev_in", 0, 4, KD, tokens(hT[4]), 2, need=need)
            even_attention()
            turn("y0", KD, 4, lambda b, t: xn[:, t, b * P:(b + 1) * P], ready=lambda t: y_ready.after("ev", 0))
            project_tok("w_out", 0, 2, KD, tokens(hT[4]), 2, need=copied("y0"))
            swiglu(0, 4)
            need = norm(("mix", 1), 4)
            project_tok("od_q", 1, 2, KD, tokens(hT[4]), 1, need=need)
            project_tok("od_kv", 1, 4, KD, tokens(hT[4]), 2)
            gates(1)
            pe.wait_ge(*pre_turn.after("na"))
            turn("naq", 8, 2, lambda b, t: nq[:, t, b * P:(b + 1) * P])
            turn("nak", 8, 4, lambda b, t: nk_[:, t, b * P:(b + 1) * P])
            await_copies("naq", 8)
            await_copies("nak", 8)
            attend("na")
            project_tok("w_out", 1, 2, KD, tokens(yT_na), need=lambda kg: y_out.after("na", 16 * kg + 15))
            swiglu(1, 2)

            def scores_pair(l, kind, h, qkT):
                b = 4 if kind == "m" else 4 + h % 2
                claim(b)
                for s in range(2):
                    cols = slice(0, 256) if s == 0 else slice(256, 384)
                    for j in range(2):
                        mm = pe.matmul(PS[:, b, cols], qkT[:, 8 + 2 * h + j, s * P:(s + 1) * P],
                                       qkT[:, 2 * h + j, s * P:256], start=j == 0, stop=j == 1)
                mm.then_inc(*scored.now(kind, l, h))
                reader[b] = probs_ready.after(kind, l, h)
                if kind == "m":
                    claim(5)
                    pe.matmul(PS[:, 5, 0:256], tab("sel_h", 4)[:, h * P:(h + 1) * P], gt[:, 3, :],
                              start=True, stop=True).then_inc(*u_bc.now(l, h))
                    reader[5] = exp_arg.after(l, h)

            def values_pair(l, kind, h, val, dv):
                pe.wait_ge(*probs_ready.after(kind, l, h))
                pb = SCR[:, 384 * (h % 2):384 * (h % 2) + 384]
                claim(6, 7)
                for t in range(2):
                    blocks = [pb[:, 0:128]] if t == 0 else [pb[:, 128:256], pb[:, 256:384]]
                    for s, lhs in enumerate(blocks):
                        mm = pe.matmul(PS[:, 6 + t, 0:dv], lhs, val[:, s, h * dv:(h + 1) * dv],
                                       start=s == 0, stop=s == len(blocks) - 1)
                    if kind == "m":
                        for s, lhs in enumerate(blocks):
                            mm = pe.matmul(PS[:, 6 + t, 256:257], lhs, small[:, 60:61],
                                           start=s == 0, stop=s == len(blocks) - 1)
                mm.then_inc(*attended.now(kind, l, h))
                reader[6] = reader[7] = y_out.after(kind, l, h)

            for l in range(2):
                lhs = tokens(hT[2])
                pe.wait_ge(*norm(("n1", l), 2)(1))
                if l == 0:
                    pe.wait_ge(*wgate_ready.after())
                claim(4)
                for gate in range(2):
                    for kt in range(KD):
                        at = (l * KD + kt) * 8 + 4 * gate
                        mm = product(PS[0:4, 4, gate * 256:gate * 256 + 256], (wgh[:, at:at + 4], wgl[:, at:at + 4]),
                                     [a[:, kt, :] for a in hT[2]], kt == 0, kt == KD - 1)
                mm.then_inc(*projected.now("gates", l, 0, 0))
                reader[4] = gate_abs.after(l)
                project_feat("mqk", l, 4, hT[2], freed=unit_acted)
                pe.wait_ge(*gate_scan.after(l))
                claim(5)
                for i in range(2):
                    for t in range(2):
                        mm = pe.transpose(PS[:, 5, (2 * i + t) * 4:(2 * i + t) * 4 + 4],
                                          gt[:, 4 * i, t * P:(t + 1) * P], ident[0:4, 0:4])
                mm.then_inc(*gate_turned.now(l))
                reader[5] = gate_cols.after(l)
                project_tok("mv", l, 2, KD, lhs, biased=True)
                project_tok("mo", l, 2, KD, lhs, biased=True)
                project_feat("rqk", l, 4, hT[2], freed=unit_acted)
                pe.wait_ge(*qk_ready_act.after("m", l, 3))
                for h in range(R_H):
                    scores_pair(l, "m", h, mqkT)
                    project_tok("rv", l, 1, KD, lhs, n0=h, biased=True)
                    if h >= 1:
                        values_pair(l, "m", h - 1, mv, 256)
                project_tok("rg", l, 1, KD, lhs, biased=True)
                values_pair(l, "m", R_H - 1, mv, 256)
                project_tok("rg", l, 3, KD, lhs, n0=1, biased=True)
                pe.wait_ge(*qk_ready.after("rqk", l, 3, 0))
                for h in range(R_H):
                    scores_pair(l, "r", h, rqkT)
                    project_tok("gm" if h < 2 else "gr", l, 1, KD, lhs, n0=h % 2, biased=True)
                    if h >= 1:
                        values_pair(l, "r", h - 1, rv, 512)
                values_pair(l, "r", R_H - 1, rv, 512)
                turn(("ym", l), 8, 2, lambda b, t: hm[t][:, b * P:(b + 1) * P], ready=lambda t: y_ready.after("ym", l))
                project_tok("w_bm", l, 2, KD, tokens(ymT), need=copied(("ym", l)))
                turn(("yr", l), 16, 2, lambda b, t: hr[t][:, b * P:(b + 1) * P], ready=lambda t: y_ready.after("yr", l))
                project_tok("w_br", l, 2, 16, tokens(yrT), need=copied(("yr", l)))
                turn(("mg", l), 8, 2, lambda b, t: merged[:, t, b * P:(b + 1) * P],
                     ready=lambda t: stored.after("w_br", l, 1, 0))
                project_tok("w_out2", l, 2, KD, lhs, freed=x_ready, need=copied(("mg", l)))
                need = norm(("n2", l), 2)
                for part in range(2):
                    project_feat("ff1", l, 4, hT[2], freed=ff_acted, n0=4 * part, need=need)
                    need = None
                    for nb in range(2):
                        if part == 1:
                            plan[("bias", state["c"])] = state["b"]
                            state["b"] += 1
                        for kg in range(4):
                            if nb == 0:
                                pe.wait_ge(*hidden.after("ff1", l, 4 * part + kg, 0))
                            c, w = take_chunk("ff2", l)
                            if part == 0 and kg == 0:
                                claim(4 + 2 * nb, 5 + 2 * nb)
                            for t in range(2):
                                for kt in range(KC * kg, KC * kg + KC):
                                    mm = product(PS[:, 4 + 2 * nb + t, :], tokens(ff2T)(kt, t),
                                                 [a[:, kt - KC * kg, :] for a in w],
                                                 part == 0 and kt == 0, part == 1 and kt == 15)
                            if part == 1 and kg == 3:
                                ends(mm, c, "ff2", l, nb)
                                reader[4 + 2 * nb] = reader[5 + 2 * nb] = stored.after("ff2", l, nb, 0)
                            else:
                                mm.then_inc(*projected.now(("chunk", c)))
                            used(c)
                need = norm(("n3", l), 2)
                project_tok("pe_g", l, 2, KD, lhs, freed=tok_acted, need=need)
                pe.wait_ge(*pT_ready.after(l))
                c, w = take_chunk("w_pe", l, 2)
                for j in range(2):
                    claim(2 * j, 2 * j + 1)
                    for t in range(2):
                        for kt in range(2):
                            at = kt * 256 + t * P
                            mm = product(PS[:, 2 * j + t, :], [a[:, at:at + P] for a in pT2],
                                         [a[:, kt, j * 512:(j + 1) * 512] for a in w], kt == 0, kt == 1)
                    ends(mm, c, "w_pe", l, j)
                    reader[2 * j] = reader[2 * j + 1] = stored.after("w_pe", l, j, 0)
                used(c)
            plan["split chunks"] = split

        @block.sync
        def _(sp):
            def first(st, l):
                return plan.get(("first chunk", st, l), -9)

            sp.dma_start(colt[:, :], cols_d).then_inc(*cols_in.now(by=16))
            sp.dma_start(ring[:, 0, :], chunks_d[0]).then_inc(*w_in[0].now(0, by=16))
            sp.dma_start(tabt[:, :], tabs_d).then_inc(*tab_in.now(by=16))
            sp.dma_start(rowt[:, :], rows_d.partition_broadcast(P)).then_inc(*tab_in.now(by=16))
            sp.dma_start(mod_bias, modb_d).then_inc(*modb_in.now(by=16))
            for c in range(1, n_chunks):
                if c == 8:
                    sp.dma_start(X[:, 0:2, :], x_d).then_inc(*x_in.now(by=16))
                    sp.dma_start(X[:, 2:4, :], ctx_d).then_inc(*x_in.now(by=16))
                    sp.dma_start(wgate[:, :], wgate_d).then_inc(*wgate_in.now(by=16))
                    sp.dma_start(bgate[:, :, :], bgate_d).then_inc(*wgate_in.now(by=16))
                if c >= RING:
                    sp.wait_ge(*projected.after("used", c - RING))
                if c == first("w_out", 1) + AHEAD:
                    for part in range(2):
                        if part == 0:
                            sp.wait_ge(*projected.after("od_kv", 1, 3, 1))
                        else:
                            sp.wait_ge(*turned.after("nak", 7))
                            sp.wait_ge(*copied_v.after("nak", 6))
                            sp.wait_ge(*copied_s.after("nak", 7))
                        heads = slice(part * 8, part * 8 + 8)
                        for t in range(TX):
                            for half in range(2):
                                row0 = NA_KH - 1 - (2 * t + half)
                                src = rel_d[:, heads, row0:row0 + NA_ROWS, :].rearrange("q h i c -> q h (i c)")
                                sp.dma_start(v["rel"][part][64 * half:64 * half + 64, t], src
                                             ).then_inc(*rel_in[part].now(by=16))
                for l in range(2):
                    if c == first("mqk", l) + RING:
                        sp.wait_ge(*(x_ready.after("ffn_out", 1) if l == 0 else x_ready.after("w_pe", 0)))
                        sp.dma_start(G[:, 0:3072] if l else G[:, :],
                                     nrows_d[l:l + 1, 0:3072].partition_broadcast(P) if l else
                                     nrows_d[0:1, :].partition_broadcast(P)).then_inc(*nrows_in.now(l, by=16))
                        sp.dma_start(pT[:, :], pT_d[:, l, :]).then_inc(*pT_in.now(l, by=16))
                sp.dma_start(ring[:, c % RING, :], chunks_d[c]).then_inc(*w_in[c % RING].now(c, by=16))
                if ("bias", c - 2) in plan:
                    b = plan[("bias", c - 2)]
                    if b >= 2:
                        sp.wait_ge(*stored.after("bias", b - 2))
                    sp.dma_start(bias_ring[:, b % 2, :], brows_d[b:b + 1, :].partition_broadcast(P)
                                 ).then_inc(*bias_in[b % 2].now(b, by=16))
            sp.wait_ge(*x_ready.after("out"))
            sp.dma_start(out, xn[:, 0:2, :]).then_inc(*out_done.now(by=16))
            sp.wait_ge(out_done.sem, out_done.count)

        @block.gpsimd
        def _(pool):
            def diagonals(l):
                pool.wait_ge(*(mod_ready.after(0) if l == 0 else x_ready.after("ffn_out", 0)))
                for n, (kind, who, half) in enumerate(gate_list(l)):
                    k = kind * 8 + 4 * half
                    columns = modc[l][:, k:k + 4, who:who + 1].to_broadcast([P, 4, P])
                    pool.tensor_tensor(G[:, n * 512:(n + 1) * 512].rearrange("p (k d) -> p k d", k=4),
                                       ident.unsqueeze(1).to_broadcast([P, 4, P]), columns,
                                       ALU.mult).then_inc(*gate_diag.now(l, n))

            for c in plan["split chunks"]:
                if c == plan.get(("first chunk", "uq", 0)):
                    diagonals(0)
                if c == plan.get(("first chunk", "w_out", 1)):
                    diagonals(1)
                pool.wait_ge(*hi_ready.after(c))
                pool.tensor_tensor(w_lo[:, c % RING, :], ring[:, c % RING, :], w_hi[:, c % HI_RING, :].bitcast(F32),
                                   ALU.subtract).then_inc(*lo_ready.now(c))

        @block.scalar
        def _(act):
            def link(ins, e=act_chain, *key):
                ins.then_inc(*e.now(*key))
                act.wait_ge(e.sem, e.count)

            chunks_left = list(plan["split chunks"])

            def split_to(c):
                while c is not None and chunks_left and chunks_left[0] <= c:
                    n = chunks_left.pop(0)
                    act.wait_ge(*w_in[n % RING].after(n))
                    if n >= HI_RING:
                        act.wait_ge(*projected.after("used", n - HI_RING))
                    act.activation(w_hi[:, n % HI_RING, :], ring[:, n % RING, :], ACT.Copy).then_inc(*hi_ready.now(n))

            def split_for(st, l, j):
                c = plan.get(("last chunk", st, l, j))
                split_to(c if c is None else c + AHEAD)

            def copy_turned(key):
                nb, tiles, width, dst, kind = copies[key]
                for b in range(nb):
                    src = PS[0:width, 4 + b % 4, 0:tiles * P]
                    if kind == "plain":
                        if b % 2:
                            act.wait_ge(*turned.after(key, b))
                            act.activation(dst(b), src, ACT.Copy).then_inc(*copied_s.now(key, b))
                    elif kind == "parts":
                        act.wait_ge(*turned.after(key, b))
                        act.activation(dst(b)[0], src, ACT.Copy).then_inc(*copied_s.now(key, b))
                    elif kind[0] == "gain":
                        act.wait_ge(*turned.after(key, b))
                        act.activation(dst(b)[0], src, ACT.Copy, scale=gain_of(key, b)).then_inc(*copied_s.now(key, b))
                    else:
                        act.wait_ge(*shifted.after(key, b))
                        act.activation(dst(b)[0], SCR[:, 512 * (b % 4):512 * (b % 4) + tiles * P],
                                       ACT.Copy).then_inc(*copied_s.now(key, b))

            def norm(key, tiles, st=None, l=None, j0=0):
                for half in range(2):
                    if st:
                        split_for(st, l, j0 + half)
                    for t in range(tiles):
                        if st:
                            act.wait_ge(*x_ready.after(st, l, j0 + half, t // 2, t % 2))
                        cols = slice(512 * half, 512 * half + 512)
                        at = 12 * half + t
                        junk = xn[:, t, cols] if key == ("mix", 0) else SCR[:, 0:512]
                        link(act.activation(junk, X[:, t, cols], ACT.Square, accum_out=stat[:, at:at + 1]))
                        if half == 1:
                            link(act.activation(stat[:, 4 + t:5 + t], stat[:, 12 + t:13 + t], ACT.Sqrt,
                                                bias=stat[:, 16 + t:17 + t], scale=1.0 / D), root_ready, key, t)
                    if half == 0:
                        link(act.activation(stat[:, 16:16 + tiles], stat[:, 0:tiles], ACT.Identity, bias=eps,
                                            scale=1.0 / D))
                        act.activation(stat[:, 20:21], stat[:, 16:17], ACT.Sqrt)
                if key not in ("out", ("mix", 0)):
                    copy_turned(key)

            def root(key, n, d):
                act.wait_ge(*sums_ready.after(key))
                link(act.activation(stat[:, 64:64 + n], stat[:, 0:n], ACT.Sqrt, bias=eps, scale=1.0 / d),
                     root_ready, key)

            def attend(ph):
                us = units[ph]
                probT = probsT[ph].rearrange("p (b k) -> p b k", b=2)

                def exps(u):
                    d = us[u]
                    s, _, _, slot = attention_banks(ph, u)
                    act.wait_ge(*max_ready.after(ph, u))
                    for i in range(len(d["scores"])):
                        k = 2 * (u % 4) + i
                        ins = act.activation(probs[ph][:, slot, i, 0:d["nk"]], PS[:, s + i, 0:d["nk"]], ACT.Exp,
                                             bias=stat[:, 192 + k:193 + k], scale=d["scale"],
                                             accum_out=stat[:, 200 + k:201 + k])
                    ins.then_inc(*exp_ready.now(ph, u))

                def copy_probs(u):
                    act.wait_ge(*probs_turned.after(ph, u))
                    act.activation(probT[:, u % 2, 0:us[u]["nk"]], PS[:, attention_banks(ph, u)[1], 0:us[u]["nk"]],
                                   ACT.Copy).then_inc(*probsT_ready.now(ph, u))

                exps(0)
                exps(1)
                for u in range(len(us)):
                    copy_probs(u)
                    if u + 2 < len(us):
                        exps(u + 2)

            def gates(l):
                for n in range(len(gate_list(l))):
                    act.wait_ge(*gates_bc.after(l, n))
                    act.activation(G[:, n * 512:(n + 1) * 512], PS[:, 5 + n % 3, :],
                                   ACT.Copy).then_inc(*acted.now("gates", l, n))

            def modulation(l, j0, n):
                for j in range(j0, j0 + n):
                    act.wait_ge(*projected.after("mod", l, j, 1))
                    if j >= 4:
                        act.wait_ge(*mod_turned.after(l, j - 4))
                    act.activation(SCR[0:2, (j % 4) * 512:(j % 4) * 512 + 512], PS[0:2, j % 4, :],
                                   ACT.Copy).then_inc(*mod_rows.now(l, j))

            def swiglu(l, tiles):
                norm(("ffn", l), tiles, "w_out", l)
                for j in range(11):
                    for g in range(tiles // 2):
                        pair = (j * (tiles // 2) + g) % 2
                        split_for("ffn_in", l, j)
                        act.wait_ge(*projected.after("ffn_in", l, j, g))
                        if j * (tiles // 2) + g >= 2:
                            jj, gg = divmod(j * (tiles // 2) + g - 2, tiles // 2)
                            act.wait_ge(*stored.after("hidden", l, jj, gg))
                        act.activation(SCR[:, pair * 512:pair * 512 + 512], PS[:, 2 * pair, :],
                                       ACT.Silu).then_inc(*unit_acted.now("ffn_in", l, j, g))

            act.wait_ge(*cols_in.after())
            act.activation(small[:, 0:16], col("cond"), ACT.Silu).then_inc(*cond_ready.now())
            act.wait_ge(*lam_logit.after())
            act.activation(small[:, 20:22], small[:, 18:20], ACT.Exp).then_inc(*lam_exp.now())
            modulation(0, 0, 9)
            act.wait_ge(*const_ready.after())
            act.wait_ge(*x_in.after())
            norm(("mix", 0), 4)
            modulation(0, 9, 3)
            split_to(plan.get(("first chunk", "ev_in", 0), -AHEAD) + AHEAD - 1)
            copy_turned(("mix", 0))
            split_for("ev_in", 0, 3)
            gates(0)
            root("da", 64, 64)
            modulation(1, 0, 3)
            copy_turned("daq")
            copy_turned("dak")
            attend("da")
            root("cq", 4, 256)
            root("ckv", 4, 128)
            modulation(1, 3, 2)
            root("kr", 4, 64)
            modulation(1, 5, 2)
            split_for("ukv", 0, 3)
            copy_turned("mlac")
            root("mlaq", 16, 192)
            modulation(1, 7, 2)
            root("mlak", 16, 128)
            modulation(1, 9, 1)
            copy_turned("qn")
            copy_turned("qr")
            copy_turned("kn")
            attend("mla")
            split_to(plan.get(("first chunk", "w_out", 0), -AHEAD) + AHEAD - 1)
            root("dao", 16, 128)
            modulation(1, 10, 2)
            copy_turned("y0")
            swiglu(0, 4)
            norm(("mix", 1), 4, "ffn_out", 0, 4)
            split_for("od_q", 1, 1)
            root("naq", 32, 64)
            split_for("od_kv", 1, 1)
            root("nak", 64, 64)
            split_for("od_kv", 1, 3)
            gates(1)
            copy_turned("naq")
            copy_turned("nak")
            attend("na")
            swiglu(1, 2)

            def in_place(st, l, n, buf, func, n0=0):
                for j in range(n0, n0 + n):
                    split_for(st, l, j)
                    act.wait_ge(*stored.after(st, l, j, 0))
                    act.activation(buf[:, :, j * 512:(j + 1) * 512], buf[:, :, j * 512:(j + 1) * 512],
                                   func).then_inc(*tok_acted.now(st, l, j, 0))

            for l in range(2):
                norm(("n1", l), 2, *(("ffn_out", 1) if l == 0 else ("w_pe", 0)))
                act.wait_ge(*gate_abs.after(l))
                link(act.activation(gt[:, 2, :], gt[:, 2, :], ACT.Exp, scale=-1.0))
                link(act.activation(gt[:, 2, :], gt[:, 2, :], ACT.Ln, bias=small[0:4, 60:61], scale=1.0), gate_act, l)
                def silu(j):
                    act.wait_ge(*qk_ready.after("mqk", l, j, 0))
                    act.activation(mqkT[:, 4 * j:4 * j + 4, :], mqkT[:, 4 * j:4 * j + 4, :],
                                   ACT.Silu).then_inc(*qk_ready_act.now("m", l, j))

                for j in range(4):
                    conv_in = conv_ins[j % 2]
                    split_for("mqk", l, j)
                    act.wait_ge(*projected.after("mqk", l, j, 0))
                    act.wait_ge(*(qk_ready.after("mqk", l, j - 2, 0) if j >= 2 else const_ready.after("pad", l)))
                    for s in range(4):
                        ins = act.activation(conv_in[:, s, 3:259],
                                             PS[:, 2 * (j % 2) + s // 2, (s % 2) * 256:(s % 2) * 256 + 256], ACT.Identity,
                                             bias=col("b_mqk")[:, l * 16 + j * 4 + s:l * 16 + j * 4 + s + 1])
                    link(ins, unit_acted, "mqk", l, j, 0)
                    for s in range(4):
                        ch = j * 4 + s
                        ins = act.activation(mqkT[:, ch, :], conv_in[:, s, 0:256], ACT.Identity,
                                             bias=col("conv_b")[:, l * 16 + ch:l * 16 + ch + 1],
                                             scale=col("conv_w")[:, l * 64 + ch:l * 64 + ch + 1])
                    ins.then_inc(*tap_ready.now(l, j))
                    if j:
                        silu(j - 1)
                split_for("mv", l, 0)
                silu(3)
                act.wait_ge(*gate_turned.after(l))
                act.activation(small[:, 32:40], PS[:, 5, 8:16], ACT.Exp, scale=-1.0)
                act.activation(small[:, 24:32], PS[:, 5, 0:8], ACT.Copy).then_inc(*gate_cols.now(l))
                in_place("mo", l, 2, mo, ACT.Sigmoid)
                rope_in = SCR[:, 0:1024].rearrange("p (s t) -> p s t", s=4)
                for j in range(4):
                    split_for("rqk", l, j)
                    act.wait_ge(*projected.after("rqk", l, j, 0))
                    act.wait_ge(*(qk_ready.after("rqk", l, j - 1, 0) if j else qk_ready.after("mqk", l, 3, 0)))
                    for s in range(4):
                        ins = act.activation(rope_in[:, s, :],
                                             PS[:, 2 * (j % 2) + s // 2, (s % 2) * 256:(s % 2) * 256 + 256], ACT.Identity,
                                             bias=col("b_rqk")[:, l * 16 + j * 4 + s:l * 16 + j * 4 + s + 1])
                    ins.then_inc(*unit_acted.now("rqk", l, j, 0))
                def root_of(k):
                    act.wait_ge(*sums_ready.after(k, l))
                    view = stat[:, 128:144].rearrange("p (n s) -> p n s", s=2)
                    link(act.activation(stat[:, 144:152], view[:, :, 1], ACT.Sqrt, bias=eps, scale=1.0), root_ready, k, l)

                for h in range(R_H):
                    if h:
                        split_for("rv", l, h - 1)
                    act.wait_ge(*exp_arg.after(l, h))
                    e = SCR[:, 768 + 384 * (h % 2):1152 + 384 * (h % 2)]
                    act.activation(e, e, ACT.Exp).then_inc(*exp_ready.now("m", l, h))
                in_place("rg", l, 1, rg, ACT.Silu)
                root_of("hm")
                in_place("rg", l, 3, rg, ACT.Silu, 1)
                in_place("gm", l, 2, gm, ACT.Sigmoid)
                in_place("gr", l, 2, gr, ACT.Sigmoid)
                copy_turned(("ym", l))
                root_of("hr")
                split_for("w_bm", l, 1)
                copy_turned(("yr", l))
                split_for("w_br", l, 1)
                copy_turned(("mg", l))
                norm(("n2", l), 2, "w_out2", l)
                for j in range(8):
                    pair = j % 2
                    split_for("ff1", l, j)
                    act.wait_ge(*projected.after("ff1", l, j, 0))
                    if j >= 2:
                        act.wait_ge(*hidden.after("ff1", l, j - 2, 0))
                    for s in range(4):
                        ins = act.activation(SCR[:, 1024 * pair + 256 * s:1024 * pair + 256 * s + 256],
                                             PS[:, 2 * pair + s // 2, (s % 2) * 256:(s % 2) * 256 + 256], ACT.Relu,
                                             bias=col("b_ff1")[:, l * 32 + j * 4 + s:l * 32 + j * 4 + s + 1])
                    ins.then_inc(*ff_acted.now("ff1", l, j, 0))
                norm(("n3", l), 2, "ff2", l)
                for j in range(2):
                    split_for("pe_g", l, j)
                    act.wait_ge(*projected.after("pe_g", l, j, 0))
                    act.activation(gm[:, :, j * 512:(j + 1) * 512], PS[:, 2 * j:2 * j + 2, :],
                                   ACT.Sigmoid).then_inc(*tok_acted.now("pe_g", l, j, 0))
            norm("out", 2, "w_pe", 1)

        @block.vector
        def _(dve):
            def link(ins, e=vec_chain, *key):
                ins.then_inc(*e.now(*key))
                dve.wait_ge(e.sem, e.count)

            def copy_turned(key):
                nb, tiles, width, dst, kind = copies[key]

                def shift(b):
                    dve.wait_ge(*turned.after(key, b))
                    k, m = kind[1], modc[key[1]]
                    for i in range(tiles // 2):
                        at = 512 * (b % 4) + 256 * i
                        ins = dve.tensor_scalar(SCR[:, at:at + 256], PS[:, 4 + b % 4, 256 * i:256 * i + 256],
                                                m[:, (k + 1) * 8 + b, i:i + 1], m[:, k * 8 + b, i:i + 1],
                                                ALU.mult, ALU.add)
                    ins.then_inc(*shifted.now(key, b))

                for b in range(nb):
                    src = PS[0:width, 4 + b % 4, 0:tiles * P]
                    if kind == "plain":
                        if b % 2 == 0:
                            dve.wait_ge(*turned.after(key, b))
                            dve.tensor_copy(dst(b), src).then_inc(*copied_v.now(key, b))
                        continue
                    if kind[0] == "mod":
                        if b == 0:
                            shift(0)
                        if b + 1 < nb:
                            shift(b + 1)
                    dve.wait_ge(*copied_s.after(key, b))
                    hi, lo = dst(b)
                    if kind == "parts":
                        ins = dve.tensor_tensor(lo, src, hi.bitcast(F32), ALU.subtract)
                    elif kind[0] == "gain":
                        ins = dve.scalar_tensor_tensor(lo, src, gain_of(key, b), hi.bitcast(F32), ALU.mult, ALU.subtract)
                    else:
                        ins = dve.tensor_tensor(lo, SCR[:, 512 * (b % 4):512 * (b % 4) + tiles * P], hi.bitcast(F32),
                                                ALU.subtract)
                    ins.then_inc(*copied_v.now(key, b))

            def split(pair, src):
                link(dve.tensor_copy(pair[0], src))
                return dve.tensor_tensor(pair[1], src, pair[0].bitcast(F32), ALU.subtract)

            def norm(key, tiles):
                for t in range(tiles):
                    dve.wait_ge(*root_ready.after(key, t))
                    link(dve.reciprocal(stat[:, 8 + t:9 + t], stat[:, 4 + t:5 + t]))
                    dve.tensor_scalar(xn[:, t, :], X[:, t, :], stat[:, 8 + t:9 + t], None,
                                      ALU.mult).then_inc(*normed.now(key, t))
                if key not in ("out", ("mix", 0)):
                    copy_turned(key)

            def bc(a, shape):
                while len(a.shape) < len(shape):
                    a = a.unsqueeze(1)
                return a.to_broadcast(shape)

            def group_rms(key, x4, sq, gains):
                _, t, g, d = x4.shape
                n = t * g
                sq4 = sq[:, 0:n * d].rearrange("p (t g d) -> p t g d", t=t, g=g)
                link(dve.tensor_tensor(sq4, x4, x4, ALU.mult))
                link(dve.tensor_reduce(stat[:, 0:n], sq[:, 0:n * d].rearrange("p (n d) -> p n d", d=d), AX_X, ALU.add),
                     sums_ready, key)
                dve.wait_ge(*root_ready.after(key))
                link(dve.reciprocal(stat[:, 128:128 + n], stat[:, 64:64 + n]))
                r4 = stat[:, 128:128 + n].rearrange("p (t g) -> p t g", t=t).unsqueeze(3).to_broadcast([P, t, g, d])
                link(dve.tensor_tensor(x4, x4, r4, ALU.mult))
                for lo, hi, gain in gains:
                    part = x4[:, :, lo:hi, :]
                    link(dve.tensor_tensor(part, part, bc(gain, [P, t, hi - lo, d]), ALU.mult))

            def rope(x5, t, tmp):
                g = x5.shape[1]
                cos = bc(tab("cos").rearrange("p (t r j) -> p t r j", t=2, r=2)[:, t], [P, g, 2, 16])
                sin = bc(tab("sin").rearrange("p (t r j) -> p t r j", t=2, r=2)[:, t], [P, g, 2, 16])
                a, b, c, d = (tmp[:, i * g * 32:(i + 1) * g * 32].rearrange("p (g r j) -> p g r j", g=g, r=2)
                              for i in range(4))
                x1, x2 = x5[:, :, :, 0, :], x5[:, :, :, 1, :]
                dve.tensor_tensor(a, x1, cos, ALU.mult)
                dve.tensor_tensor(b, x2, sin, ALU.mult)
                dve.tensor_tensor(c, x1, sin, ALU.mult)
                link(dve.tensor_tensor(d, x2, cos, ALU.mult))
                dve.tensor_tensor(x1, a, b, ALU.subtract)
                link(dve.tensor_tensor(x2, c, d, ALU.add))

            def halves(x3):
                return x3.rearrange("p g (r h j) -> p g r h j", r=2, h=2)

            def attend(ph):
                us = units[ph]

                def maxes(u):
                    d, s = us[u], attention_banks(ph, u)[0]
                    n = len(d["scores"])
                    if ph == "na" and u == len(us) // 2:
                        add_mask(1)
                    dve.wait_ge(*scored.after(ph, u))
                    if d["bias"] is not None:
                        link(dve.scalar_tensor_tensor(PS[:, s, 0:256], d["bias"], 1.0 / d["scale"], PS[:, s, 0:256],
                                                      ALU.mult, ALU.add))
                    m = stat[:, 208:208 + n]
                    link(dve.tensor_reduce(m, PS[:, s:s + n, 0:d["nk"]], AX_X, ALU.max))
                    o = 192 + 2 * (u % 4)
                    link(dve.tensor_scalar(stat[:, o:o + n], m, -d["scale"], None, ALU.mult), max_ready, ph, u)

                def norms(u):
                    if ph == "mla":
                        return
                    o, r, nk = 200 + 2 * (u % 4), stat[:, 212 + u % 4:213 + u % 4], us[u]["nk"]
                    slot = attention_banks(ph, u)[3]
                    dve.wait_ge(*exp_ready.after(ph, u))
                    if ph == "na":
                        link(dve.reciprocal(r, stat[:, o:o + 1]))
                        dve.tensor_scalar(diag[:, u % 2, :], ident, r, None, ALU.mult).then_inc(*probs_ready.now(ph, u))
                        return
                    link(dve.reciprocal(r, stat[:, o + 1:o + 2]))
                    link(dve.scalar_tensor_tensor(r, stat[:, o:o + 1], neg_lam, r, ALU.mult, ALU.mult))
                    dve.scalar_tensor_tensor(mix4[:, u % 2, 0:nk], probs[ph][:, slot, 1, 0:nk], r,
                                             probs[ph][:, slot, 0, 0:nk], ALU.mult, ALU.add
                                             ).then_inc(*probs_ready.now(ph, u))

                def outs(u):
                    d, b = us[u], attention_banks(ph, u)[2]
                    if ph == "na":
                        part, k, q = d["out"]
                        dve.wait_ge(*attended.after(ph, u))
                        split([a[part, k, q] for a in yT_na], PS[part, b, 0:P]).then_inc(*y_out.now(ph, u))
                        return
                    o, r = 200 + 2 * (u % 4), stat[:, 212 + u % 4:213 + u % 4]
                    dve.wait_ge(*exp_ready.after(ph, u))
                    link(dve.reciprocal(r, stat[:, o:o + 1]))
                    dve.wait_ge(*attended.after(ph, u))
                    dve.tensor_scalar(d["out"], PS[:, b, 0:d["dv"]], r, None, ALU.mult).then_inc(*y_out.now(ph, u))

                maxes(0)
                maxes(1)
                for u in range(len(us)):
                    norms(u)
                    if u + 2 < len(us):
                        maxes(u + 2)
                    if u >= 1:
                        outs(u - 1)
                outs(len(us) - 1)

            def pair_view(pair):
                return PS[:, 2 * pair:2 * pair + 2, :]

            def modulation(l, part):
                if l == 0:
                    dve.wait_ge(*modb_in.after())
                j0 = sum(MOD_PARTS[l][:part])
                n = MOD_PARTS[l][part]
                dve.wait_ge(*mod_turned.after(l, j0 + n - 1))
                m = modc[l][:, 4 * j0:4 * (j0 + n), :]
                bias = mod_bias[:, l, 4 * j0:4 * (j0 + n)].unsqueeze(2).to_broadcast([P, 4 * n, 2])
                link(dve.tensor_tensor(m, PS[:, 4, 8 * j0:8 * (j0 + n)].rearrange("p (k c) -> p k c", c=2), bias, ALU.add),
                     mod_stored, l, part)
                if part + 1 < len(MOD_PARTS[l]):
                    return
                for kind, name in ((1, "mix_g"), (4, "ffn_g")):
                    m = modc[l][:, kind * 8:kind * 8 + 8, :]
                    g = col(name)[:, l * 8:l * 8 + 8].unsqueeze(2).to_broadcast([P, 8, 2])
                    link(dve.scalar_tensor_tensor(m, m, 1.0, g, ALU.add, ALU.mult),
                         *((mod_ready, l) if kind == 4 else (vec_chain,)))

            def gated_add(st, l, j, g, pair, gate_of, xs):
                tmp = SCR[:, 1024:2048].rearrange("p (t n) -> p t n", t=2)
                dve.tensor_tensor(tmp[:, 0], PS[:, 2 * pair, :], gate_of[0], ALU.mult).then_inc(*vec_chain.now())
                dve.tensor_tensor(tmp[:, 1], PS[:, 2 * pair + 1, :], gate_of[1],
                                  ALU.mult).then_inc(*stored.now(st, l, j, g))
                dve.wait_ge(vec_chain.sem, vec_chain.count)
                dve.tensor_tensor(xs[:, 0], xs[:, 0], tmp[:, 0], ALU.add).then_inc(*x_ready.now(st, l, j, g, 0))
                dve.wait_ge(stored.sem, stored.count)
                link(dve.tensor_tensor(xs[:, 1], xs[:, 1], tmp[:, 1], ALU.add), x_ready, st, l, j, g, 1)
                x_ready.alias(st, l)

            def residual(st, l, n, groups, gates, n0=0):
                for j in range(n0, n0 + n):
                    for g in range(groups):
                        pair = (j * groups + g) % 2
                        cols = slice((j % 2) * 512, (j % 2) * 512 + 512)
                        dve.wait_ge(*projected.after(st, l, j, g))
                        gated_add(st, l, j, g, pair, [gates[g][:, cols]] * 2, X[:, 2 * g:2 * g + 2, cols])

            def store(st, l, n, groups, dst, n0=0):
                for j in range(n0, n0 + n):
                    for g in range(groups):
                        pair = (j * groups + g) % 2
                        o = dst(j, g)
                        dve.wait_ge(*projected.after(st, l, j, g))
                        dve.tensor_copy(o, pair_view(pair)[:, :, 0:o.shape[2]]).then_inc(*stored.now(st, l, j, g))

            def swiglu(l, tiles):
                g_n = tiles // 2
                norm(("ffn", l), tiles)
                n0 = 0
                for part, n in enumerate(FF_PARTS[l]):
                    for j in range(n0, n0 + n):
                        for g in range(g_n):
                            pair = (j * g_n + g) % 2
                            dve.wait_ge(*unit_acted.after("ffn_in", l, j, g))
                            s = SCR[:, pair * 512:pair * 512 + 512]
                            link(dve.tensor_tensor(s, s, PS[:, 2 * pair + 1, :], ALU.mult), stored, "ffn_in", l, j, g)
                            k = 2 * (j - n0)
                            split([a[:, k:k + 2, g * 256:(g + 1) * 256] for a in ffT[l]],
                                  s.rearrange("p (s t) -> p s t", s=2)).then_inc(*stored.now("hidden", l, j, g))
                    n0 += n
                    residual("ffn_out", l, 2, g_n, [gate(l, 5, g) for g in range(g_n)], 2 * part)

            def add_mask(part):
                dve.wait_ge(*rel_in[part].after())
                rel = v["rel"][part].rearrange("p t h (i c) -> p (t h i) c", i=NA_ROWS)
                link(dve.tensor_tensor(rel, rel, bc(tab("na_mask"), [P, rel.shape[1], GRID_W]), ALU.add))

            dve.memset(small[:, 60:61], 1.0)
            link(dve.memset(eps, EPS), const_ready)
            dve.wait_ge(*cols_in.after())
            dve.wait_ge(*tab_in.after())
            link(dve.tensor_tensor(SCR[:, 0:128], row("lq"), row("lk"), ALU.mult))
            link(dve.tensor_reduce(small[:, 18:20], SCR[:, 0:128].rearrange("p (a d) -> p a d", a=2), AX_X, ALU.add),
                 lam_logit)
            dve.wait_ge(*lam_exp.after())
            link(dve.tensor_tensor(small[:, 22:23], small[:, 21:22], small[:, 20:21], ALU.subtract))
            link(dve.tensor_scalar(neg_lam, small[:, 22:23], -LAM_INIT, None, ALU.add))
            norm(("mix", 0), 4)
            dve.wait_ge(*wgate_in.after())
            split((wgh[:, :], wgl[:, :]), wgate[:, :]).then_inc(*wgate_ready.now())
            modulation(0, 0)
            copy_turned(("mix", 0))
            store("ev_in", 0, 4, 2, lambda j, g: z0[:, 2 * g:2 * g + 2, j * 512:min(j * 512 + 512, EV_IN)])
            dve.wait_ge(stored.sem, stored.count)
            qk = z0[:, :, 0:1024].rearrange("p t (g d) -> p t g d", d=64)
            group_rms("da", qk, squares, [(0, 8, row("da_q_g")), (8, 16, row("da_k_g"))])
            for t in range(TX):
                rope(halves(qk[:, t]), t, squares)
            link(dve.memset(small[:, 16:17], 0.0), pre_turn, "da")
            modulation(1, 0)
            copy_turned("daq")
            copy_turned("dak")
            attend("da")
            group_rms("cq", z0[:, :, 1536:1792].unsqueeze(2), squares, [(0, 1, row("mla_q_a_g"))])
            group_rms("ckv", z0[:, :, 1792:1920].unsqueeze(2), squares, [(0, 1, row("mla_kv_a_g"))])
            kr = z0[:, :, 1920:1984].unsqueeze(2)
            group_rms("kr", kr, squares, [(0, 1, row("mla_kr_g"))])
            for t in range(TX):
                rope(halves(kr[:, t]), t, squares)
            link(dve.memset(small[:, 16:17], 0.0), pre_turn, "mla_c")
            modulation(1, 1)
            copy_turned("mlac")
            copy_turned("mlakr")
            for st, dst, w in (("uq", q_l0, 384), ("ukv", v["kv"], 512)):
                for t in range(4):
                    dve.wait_ge(*projected.after(st, 0, t, 0))
                    dve.tensor_copy(dst[:, t, :].rearrange("p (s n) -> p s n", s=2),
                                    pair_view(t % 2)[:, :, 0:w]).then_inc(*stored.now(st, 0, t, 0))
            dve.wait_ge(stored.sem, stored.count)
            qh = q_l0.rearrange("p t (g d) -> p t g d", g=4)
            group_rms("mlaq", qh, squares, [(0, 4, row("mla_q_g"))])
            for t in range(TX):
                rope(halves(qh[:, t, :, 128:192]), t, squares)
            kh = v["kv"].rearrange("p t (g d) -> p t g d", g=4)[:, :, :, 0:128]
            group_rms("mlak", kh, squares, [(0, 4, row("mla_k_g"))])
            link(dve.memset(small[:, 16:17], 0.0), pre_turn, "mla_q")
            modulation(1, 2)
            for k in ("qn", "qr", "kn"):
                copy_turned(k)
            attend("mla")
            dve.wait_ge(y_out.sem, y_out.count)
            yd = xn[:, :, 0:512].rearrange("p t (g d) -> p t g d", g=4)
            group_rms("dao", yd, squares, [(0, 4, row("da_out_g"))])
            link(dve.tensor_scalar(xn[:, :, 0:512], xn[:, :, 0:512], 1.0 - LAM_INIT, None, ALU.mult), y_ready, "ev", 0)
            modulation(1, 3)
            copy_turned("y0")
            dve.wait_ge(*acted.after("gates", 0, 7))
            residual("w_out", 0, 2, 2, [gate(0, 2, 0), gate(0, 2, 1)])
            swiglu(0, 4)
            norm(("mix", 1), 4)
            store("od_q", 1, 2, 1, lambda j, g: nq[:, :, j * 512:(j + 1) * 512])
            dve.wait_ge(stored.sem, stored.count)
            group_rms("naq", nq.rearrange("p t (g d) -> p t g d", d=64), xn_, [(0, 16, row("na_q_g"))])
            kv_view = lambda j, g: (nk_ if j < 2 else v["nv"])[:, 2 * g:2 * g + 2, (j % 2) * 512:(j % 2) * 512 + 512]
            store("od_kv", 1, 2, 2, kv_view)
            dve.wait_ge(stored.sem, stored.count)
            group_rms("nak", nk_.rearrange("p t (g d) -> p t g d", d=64), xn_, [(0, 16, row("na_k_g"))])
            store("od_kv", 1, 2, 2, kv_view, 2)
            link(dve.memset(small[:, 16:17], 0.0), pre_turn, "na")
            copy_turned("naq")
            copy_turned("nak")
            add_mask(0)
            attend("na")
            dve.wait_ge(*acted.after("gates", 1, 3))
            residual("w_out", 1, 2, 1, [gate(1, 2, 0)])
            swiglu(1, 2)

            state = {"b": 0}

            def biased(st, l, n, dst, n0=0, first_bank=0):
                for j in range(n0, n0 + n):
                    b = state["b"]
                    state["b"] += 1
                    dve.wait_ge(*projected.after(st, l, j, 0))
                    dve.wait_ge(*bias_in[b % 2].after(b))
                    br = bc(bias_ring[:, b % 2, :], [P, 2, 512])
                    bank = first_bank + 2 * (j % 2)
                    ins = dve.tensor_tensor(dst(j), PS[:, bank:bank + 2, :], br, ALU.add)
                    ins.then_inc(*stored.now(st, l, j, 0))
                    stored.alias("bias", b)

            def layer_norms(l, key, h_buf, width, gain, gate_buf):
                link(dve.memset(small[:, 16:17], 0.0), sums_ready, key, l)
                dve.wait_ge(*root_ready.after(key, l))
                link(dve.reciprocal(stat[:, 152:160], stat[:, 144:152]))
                for t in range(2):
                    for h in range(R_H):
                        i = t * R_H + h
                        s = h_buf[t][:, h * width:(h + 1) * width]
                        ins = dve.tensor_scalar(s, s, stat[:, 128 + 2 * i:129 + 2 * i], stat[:, 152 + i:153 + i],
                                                ALU.subtract, ALU.mult)
                link(ins)
                for t in range(2):
                    ins = dve.tensor_tensor(h_buf[t], h_buf[t], gain, ALU.mult)
                link(ins)
                dve.wait_ge(*tok_acted.after("mo" if key == "hm" else "rg", l, R_H * width // 512 - 1, 0))
                for t in range(2):
                    ins = dve.tensor_tensor(h_buf[t], h_buf[t], gate_buf[:, t, :], ALU.mult)
                link(ins, y_ready, "ym" if key == "hm" else "yr", l)

            def wide(buf):
                return lambda j: buf[:, :, j * 512:(j + 1) * 512]

            for l in range(2):
                norm(("n1", l), 2)
                dve.wait_ge(*projected.after("gates", l, 0, 0))
                dve.tensor_scalar(gt[:, 0, :], PS[0:4, 4, 0:256], bgate[:, l, 0:1], None, ALU.add)
                link(dve.tensor_scalar(gt[:, 1, :], PS[0:4, 4, 256:512], bgate[:, l, 1:2], None, ALU.add))
                link(dve.scalar_tensor_tensor(gt[:, 2, :], gt[:, 1, :], -1.0, gt[:, 1, :], ALU.mult, ALU.max), gate_abs, l)
                dve.memset(conv_ins[0][:, :, 0:3], 0.0)
                link(dve.memset(conv_ins[1][:, :, 0:3], 0.0), const_ready, "pad", l)
                dve.wait_ge(*gate_act.after(l))
                link(dve.scalar_tensor_tensor(gt[:, 1, :], gt[:, 1, :], 0.0, gt[:, 2, :], ALU.min, ALU.subtract))
                link(dve.memset(gt[:, 4, :], 0.0))
                link(dve.tensor_tensor_scan(gt[:, 2, :], gt[:, 1, :], gt[:, 4, :], 0.0, ALU.add, ALU.add))
                link(dve.tensor_tensor(gt[:, 0, :], gt[:, 0, :], gt[:, 2, :], ALU.subtract))
                link(dve.tensor_tensor_scan(gt[:, 4, :], gt[:, 0, :], gt[:, 0, :], 0.0, ALU.max, ALU.max))
                link(dve.tensor_scalar(gt[:, 3, :], gt[:, 4, :], -1.0, None, ALU.mult))
                link(dve.tensor_tensor(gt[:, 4, :], gt[:, 4, :], gt[:, 2, :], ALU.add), gate_scan, l)
                cw = col("conv_w")
                for j in range(4):
                    dve.wait_ge(*tap_ready.after(l, j))
                    for k in range(1, 4):
                        for s in range(4):
                            ch = j * 4 + s
                            o = mqkT[:, ch, :]
                            wk = cw[:, (l * 4 + k) * 16 + ch:(l * 4 + k) * 16 + ch + 1]
                            ins = dve.scalar_tensor_tensor(o, conv_ins[j % 2][:, s, k:k + 256], wk, o, ALU.mult, ALU.add)
                        if k < 3:
                            link(ins)
                    ins.then_inc(*qk_ready.now("mqk", l, j, 0))
                biased("mv", l, 2, wide(mv))
                biased("mo", l, 2, wide(mo))
                cosT, sinT = (bc(tab(n), [P, 2, 256]) for n in ("cosT", "sinT"))
                rope_in = SCR[:, 0:1024].rearrange("p (h s t) -> p h s t", h=2, s=2)
                tmp = SCR[:, 1024:2048].rearrange("p (a h t) -> p a h t", a=2, h=2)
                for j in range(4):
                    dve.wait_ge(*unit_acted.after("rqk", l, j, 0))
                    x1, x2 = rope_in[:, :, 0, :], rope_in[:, :, 1, :]
                    o = rqkT[:, 4 * j:4 * j + 4, :].rearrange("p (h s) t -> p h s t", s=2)
                    dve.tensor_tensor(tmp[:, 0], x1, cosT, ALU.mult)
                    link(dve.tensor_tensor(tmp[:, 1], x2, sinT, ALU.mult))
                    link(dve.tensor_tensor(o[:, :, 0, :], tmp[:, 0], tmp[:, 1], ALU.subtract))
                    dve.tensor_tensor(tmp[:, 0], x1, sinT, ALU.mult)
                    link(dve.tensor_tensor(tmp[:, 1], x2, cosT, ALU.mult))
                    ins = dve.tensor_tensor(o[:, :, 1, :], tmp[:, 0], tmp[:, 1], ALU.add)
                    ins.then_inc(*qk_ready.now("rqk", l, j, 0))
                    dve.wait_ge(qk_ready.sem, qk_ready.count)
                dve.wait_ge(*gate_cols.after(l))
                dve.wait_ge(*nrows_in.after(l))
                mask = tab("mask")

                def head_stats(key, h, h_buf, width):
                    for t in range(2):
                        i = t * R_H + h
                        link(dve.bn_stats(stat[:, 160 + 6 * t:166 + 6 * t], h_buf[t][:, h * width:(h + 1) * width]))
                        link(dve.bn_aggr(stat[:, 128 + 2 * i:130 + 2 * i], stat[:, 160 + 6 * t:166 + 6 * t]))

                def m_out(h):
                    dve.wait_ge(*attended.after("m", l, h))
                    for t in range(2):
                        den, floor = small[:, 40 + t:41 + t], small[:, 32 + 4 * t + h:33 + 4 * t + h]
                        link(dve.tensor_scalar(den, PS[:, 6 + t, 256:257], -1.0, floor, ALU.mult, ALU.max))
                        link(dve.tensor_tensor(den, den, PS[:, 6 + t, 256:257], ALU.max))
                    link(dve.reciprocal(small[:, 42:44], small[:, 40:42]))
                    for t in range(2):
                        ins = dve.tensor_scalar(hm[t][:, h * 256:(h + 1) * 256], PS[:, 6 + t, 0:256],
                                                small[:, 42 + t:43 + t], None, ALU.mult)
                    link(ins, y_out, "m", l, h)
                    head_stats("hm", h, hm, 256)

                def r_out(h):
                    dve.wait_ge(*attended.after("r", l, h))
                    for t in range(2):
                        ins = dve.tensor_copy(hr[t][:, h * 512:(h + 1) * 512], PS[:, 6 + t, :])
                    link(ins, y_out, "r", l, h)
                    head_stats("hr", h, hr, 512)

                def arg(h):
                    dve.wait_ge(*u_bc.after(l, h))
                    e = SCR[:, 768 + 384 * (h % 2):1152 + 384 * (h % 2)]
                    ub = PS[:, 5, 0:256]
                    dve.scalar_tensor_tensor(e[:, 0:256], ub, small[:, 24 + h:25 + h], mask[:, 0:256], ALU.add, ALU.add)
                    link(dve.scalar_tensor_tensor(e[:, 256:384], ub[:, 128:256], small[:, 28 + h:29 + h],
                                                  mask[:, 256:384], ALU.add, ALU.add), exp_arg, l, h)

                for h in range(R_H):
                    arg(h)
                    biased("rv", l, 1, wide(rv), h)
                    dve.wait_ge(*exp_ready.after("m", l, h))
                    link(dve.scalar_tensor_tensor(SCR[:, 384 * (h % 2):384 * (h % 2) + 384], PS[:, 4, 0:384],
                                                  QK_SCALE, SCR[:, 768 + 384 * (h % 2):1152 + 384 * (h % 2)],
                                                  ALU.mult, ALU.mult), probs_ready, "m", l, h)
                    if h >= 1:
                        m_out(h - 1)
                biased("rg", l, 1, wide(rg))
                m_out(R_H - 1)
                layer_norms(l, "hm", hm, 256, G[:, 0:1024], mo)
                biased("rg", l, 3, wide(rg), 1)
                decay = tab("decay").rearrange("p (h n) -> p h n", h=R_H)
                for h in range(R_H):
                    dve.wait_ge(*scored.after("r", l, h))
                    link(dve.scalar_tensor_tensor(SCR[:, 384 * (h % 2):384 * (h % 2) + 384], PS[:, 4 + h % 2, 0:384],
                                                  QK_SCALE, decay[:, h, :], ALU.mult, ALU.mult),
                         probs_ready, "r", l, h)
                    if h < 2:
                        biased("gm", l, 1, wide(gm), h)
                    else:
                        biased("gr", l, 1, wide(gr), h - 2)
                    if h >= 1:
                        r_out(h - 1)
                r_out(R_H - 1)
                copy_turned(("ym", l))
                layer_norms(l, "hr", hr, 512, G[:, 1024:3072], rg)
                for j in range(2):
                    dve.wait_ge(*projected.after("w_bm", l, j, 0))
                    if j == 0:
                        dve.wait_ge(*tok_acted.after("gr", l, 1, 0))
                    cols = slice(j * 512, (j + 1) * 512)
                    dve.tensor_tensor(merged[:, :, cols], pair_view(j), gm[:, :, cols],
                                      ALU.mult).then_inc(*stored.now("w_bm", l, j, 0))
                copy_turned(("yr", l))
                for j in range(2):
                    dve.wait_ge(*projected.after("w_br", l, j, 0))
                    cols = slice(j * 512, (j + 1) * 512)
                    link(dve.tensor_tensor(gr[:, :, cols], pair_view(j), gr[:, :, cols], ALU.mult))
                    link(dve.tensor_tensor(merged[:, :, cols], merged[:, :, cols], gr[:, :, cols], ALU.add),
                         stored, "w_br", l, j, 0)
                copy_turned(("mg", l))
                for j in range(2):
                    dve.wait_ge(*projected.after("w_out2", l, j, 0))
                    xs = X[:, 0:2, j * 512:(j + 1) * 512]
                    for t in range(2):
                        ins = dve.tensor_tensor(xs[:, t], xs[:, t], PS[:, 2 * j + t, :], ALU.add)
                        ins.then_inc(*x_ready.now("w_out2", l, j, 0, t))
                    x_ready.alias("w_out2", l, j, 0)
                norm(("n2", l), 2)
                for j in range(8):
                    dve.wait_ge(*ff_acted.after("ff1", l, j, 0))
                    s = SCR[:, 1024 * (j % 2):1024 * (j % 2) + 1024]
                    link(dve.tensor_tensor(s, s, s, ALU.mult))
                    k = 4 * (j % 4)
                    split([a[:, k:k + 4, :] for a in ff2T],
                          s.rearrange("p (s t) -> p s t", s=4)).then_inc(*hidden.now("ff1", l, j, 0))
                t2 = SCR[:, 1024:2048].rearrange("p (t n) -> p t n", t=2)
                for j in range(2):
                    biased("ff2", l, 1, lambda j: t2, j, 4)
                    dve.wait_ge(stored.sem, stored.count)
                    xs = X[:, 0:2, j * 512:(j + 1) * 512]
                    for t in range(2):
                        link(dve.tensor_tensor(xs[:, t], xs[:, t], t2[:, t], ALU.add), x_ready, "ff2", l, j, 0, t)
                norm(("n3", l), 2)
                dve.wait_ge(*pT_in.after(l))
                split(pT2, pT[:, :]).then_inc(*pT_ready.now(l))
                for j in range(2):
                    dve.wait_ge(*projected.after("w_pe", l, j, 0))
                    cols = slice(j * 512, (j + 1) * 512)
                    gated_add("w_pe", l, j, 0, j, [gm[:, t, cols] for t in range(2)], X[:, 0:2, cols])
            norm("out", 2)
            dve.wait_ge(normed.sem, normed.count)
            link(dve.tensor_tensor(xn[:, 0:2, :], xn[:, 0:2, :], bc(G[:, 3072:4096], [P, 2, D]), ALU.mult),
                 x_ready, "out")


def weight_chunks(w):
    k, n = w.shape
    kg, nb = -(-k // (KC * P)), -(-n // NC_)
    full = np.zeros((kg * KC * P, nb * NC_), w.dtype)
    full[:k, :n] = w
    return full.reshape(kg, KC, P, nb, NC_).transpose(3, 0, 2, 1, 4).reshape(nb * kg, P, CHUNK)


def flat_chunk(w):
    k, n = w.shape
    out = np.zeros((1, P, CHUNK), w.dtype)
    out[0, :, :k // P * n] = w.reshape(k // P, P, n).transpose(1, 0, 2).reshape(P, -1)
    return out


def paired(w):
    g, u = w[:, :D_FF], w[:, D_FF:]
    return np.stack([g.reshape(-1, D_FF // 256, 256), u.reshape(-1, D_FF // 256, 256)], 2).reshape(w.shape)


def feature_cols(a):
    return a.reshape(-1, a.shape[-1] // P, P).transpose(2, 0, 1).reshape(P, -1)


def lay_out(i):
    chunks = []
    mod = [weight_chunks(i["mod_w"][1])[2 * sum(MOD_PARTS[1][:n]):2 * sum(MOD_PARTS[1][:n + 1])] for n in range(4)]
    for l in range(2):
        if l == 0:
            chunks += [weight_chunks(i["mod_w"][0]), weight_chunks(i["ev_w_in"][0]), mod[0], mod[1],
                       flat_chunk(i["mla_w_uq"][0]), flat_chunk(i["mla_w_ukv"][0]), mod[2], mod[3]]
        else:
            chunks.append(weight_chunks(i["od_w_in"][0]))
        chunks.append(weight_chunks(i["w_out"][l]))
        n0 = 0
        for n in FF_PARTS[l]:
            chunks += [weight_chunks(paired(i["ffn_w_in"][l])[:, 512 * n0:512 * (n0 + n)]),
                       weight_chunks(i["ffn_w_out"][l][256 * n0:256 * (n0 + n)])]
            n0 += n
    cuts = [0, 2048, 3072, 4096, 4104, 6152, 8200, 10248, 11272, 12296]
    brows = []
    for l in range(2):
        w, b = i["w_in_2"][l], i["b_in_2"][l]
        for n in (0, 1, 2, 4, 5, 6, 7, 8):
            chunks.append(weight_chunks(w[:, cuts[n]:cuts[n + 1]]))
            if n not in (0, 4):
                brows.append(b[cuts[n]:cuts[n + 1]])
        brows.append(i["b_ff2_2"][l])
        chunks += [weight_chunks(i[k][l]) for k in ("w_bm_2", "w_br_2", "w_out_2")]
        for half in (slice(0, 2048), slice(2048, 4096)):
            chunks += [weight_chunks(i["w_ff1_2"][l][:, half]), weight_chunks(i["w_ff2_2"][l][half])]
        chunks.append(weight_chunks(i["w_pe_gate_2"][l]))
        chunks.append(flat_chunk(i["w_pe_2"][l]))
    cols = [np.stack([i["c"][0], i["c_ctx"]]).reshape(2, KD, P).transpose(2, 1, 0).reshape(P, -1)]
    cols += [feature_cols(i[k]) for k in ("norm_mix_g", "norm_ffn_g", "norm1_g_2", "norm2_g_2", "norm3_g_2")]
    b_in = i["b_in_2"]
    cols += [feature_cols(b_in[:, 0:2048]), feature_cols(b_in[:, 4104:6152]), feature_cols(i["conv_w_2"]),
             feature_cols(i["conv_b_2"]), feature_cols(i["b_ff1_2"])]
    rows = [i["da_q_g"], i["da_k_g"], i["da_lq1"], i["da_lq2"], i["da_lk1"], i["da_lk2"], i["da_out_g"],
            i["mla_q_a_g"], i["mla_kv_a_g"], i["mla_q_g"], i["mla_k_g"], i["mla_kr_g"], i["na_q_g"], i["na_k_g"]]
    padded = np.zeros((NA_H, 2 * NA_KH - 1, REL_W), np.float32)
    padded[:, :, GRID_W - NA_KW:GRID_W + NA_KW - 1] = i["na_rpb"][0]
    rel = np.stack([padded[:, :, GRID_W - 1 - q:REL_W - q] for q in range(GRID_W)])
    wg = i["w_in_2"][:, :, 4096:4104].reshape(2, KD, P, 8).transpose(2, 0, 1, 3).reshape(P, -1)
    nrows = np.zeros((2, 4096), np.float32)
    nrows[:, 0:1024], nrows[:, 1024:3072], nrows[:, 3072:] = i["m_norm_g_2"], i["r_norm_g_2"], i["final_g_2"]
    tiles = lambda a: a.reshape(TX, P, D).transpose(1, 0, 2)
    arrays = [tiles(i["x"]), tiles(i["ctx"]), np.concatenate(chunks), np.concatenate(cols, 1),
              np.concatenate([r.reshape(-1) for r in rows]), tables(), feature_cols(i["mod_b"]).reshape(P, 2, -1), rel,
              np.concatenate(brows).reshape(-1, NC_), b_in[:, 4096:4104].reshape(2, 2, 4).transpose(2, 0, 1), wg, nrows,
              i["p_2"][:, 0].reshape(2, SEQ, 2, P).transpose(3, 0, 2, 1).reshape(P, 2, 512)]
    return [np.ascontiguousarray(a) for a in arrays]


NAMES = ["x", "ctx", "chunks", "cols", "rows", "tabs", "modb", "rel", "brows", "bgate", "wgate", "nrows", "pT"]


def kernel(**inputs):
    import concourse.bacc as bacc
    from concourse.bass_utils import run_bass_kernel_spmd

    arrays = lay_out({k: np.asarray(a) for k, a in inputs.items()})
    plan = {}
    for _ in range(2):
        nc = bacc.Bacc("TRN2", target_bir_lowering=False, num_devices=1, dynamic_dma_scratch_size=2048)
        ins = [nc.dram_tensor(n + "_in", a.shape, F32, kind="ExternalInput").ap() for n, a in zip(NAMES, arrays)]
        out = nc.dram_tensor("out", (1, SEQ, D), F32, kind="ExternalOutput").ap()
        build_program(nc, plan, ins, out.rearrange("b (t p) d -> p (b t) d", p=P))
    r = run_bass_kernel_spmd(nc, [{n + "_in": a for n, a in zip(NAMES, arrays)}], core_ids=[0])
    return r.results[0]["out"]
```
